# Optimizing a Trainium2 kernel written in Bass

```python
import math
import jax, jax.numpy as jnp
from jax import lax
import numpy as np

D_MODEL = 1024
BATCH = 1
SEQ = 256
DEPTH = 2

N_MIXERS = 2
N_CONV = (DEPTH + 1) // 2
N_ATTN = DEPTH // 2
CONV_WIDTH = 31
N_HEADS = 8
HEAD_DIM = D_MODEL // (2 * N_HEADS)
V_DIM = 2 * HEAD_DIM
Q_BLOCK = 128
NUM_BUCKETS = 32
MAX_EXACT = NUM_BUCKETS // 2
MAX_DISTANCE = 128
D_FF = int(math.ceil(8 * D_MODEL / 3 / 256) * 256)
PLE_DIM = 256
EPS = 1e-6


def rms_norm(x, g):
    xf = x.astype(jnp.float32)
    y = xf * lax.rsqrt(jnp.mean(xf * xf, axis=-1, keepdims=True) + EPS)
    return (y * g.astype(jnp.float32)).astype(x.dtype)

def layer_norm(x, g, b):
    xf = x.astype(jnp.float32)
    mu = jnp.mean(xf, axis=-1, keepdims=True)
    xc = xf - mu
    var = jnp.mean(xc * xc, axis=-1, keepdims=True)
    y = xc * lax.rsqrt(var + EPS) * g.astype(jnp.float32) + b.astype(jnp.float32)
    return y.astype(x.dtype)

def conformer_conv(x, w_pw1, b_pw1, dw_w, dw_b, ln_g, ln_b, w_pw2, b_pw2):
    a = x @ w_pw1 + b_pw1
    u = a[..., :D_MODEL] * jax.nn.sigmoid(a[..., D_MODEL:])
    u = lax.conv_general_dilated(
        u, dw_w[:, None, :].astype(u.dtype), window_strides=(1,),
        padding=[(CONV_WIDTH - 1, 0)],
        dimension_numbers=("NWC", "WIO", "NWC"),
        feature_group_count=D_MODEL) + dw_b
    u = jax.nn.silu(layer_norm(u, ln_g, ln_b))
    return u @ w_pw2 + b_pw2

def t5_bucket(dist):
    n = jnp.maximum(dist, 0)
    is_small = n < MAX_EXACT
    nf = jnp.maximum(n, 1).astype(jnp.float32)
    large = MAX_EXACT + (jnp.log(nf / MAX_EXACT) / math.log(MAX_DISTANCE / MAX_EXACT)
                         * (NUM_BUCKETS - MAX_EXACT)).astype(jnp.int32)
    large = jnp.minimum(large, NUM_BUCKETS - 1)
    return jnp.where(is_small, n, large)

def diff_attention(x, w_qkv, q_g, k_g, lq1, lk1, lq2, lk2, sub_g, w_o, rel_bias, lambda_init):
    B, S, _ = x.shape
    qkv = x @ w_qkv
    q, k, v = jnp.split(qkv, 3, axis=-1)
    q = rms_norm(q.reshape(B, S, N_HEADS, 2, HEAD_DIM), q_g) * (HEAD_DIM ** -0.5)
    k = rms_norm(k.reshape(B, S, N_HEADS, 2, HEAD_DIM), k_g)
    v = v.reshape(B, S, N_HEADS, V_DIM)
    q = jnp.transpose(q, (0, 2, 3, 1, 4))
    k = jnp.transpose(k, (0, 2, 3, 1, 4))
    v = jnp.transpose(v, (0, 2, 1, 3))
    lam = (jnp.exp(jnp.sum(lq1.astype(jnp.float32) * lk1.astype(jnp.float32)))
           - jnp.exp(jnp.sum(lq2.astype(jnp.float32) * lk2.astype(jnp.float32)))
           + lambda_init)
    n_blk = S // Q_BLOCK
    qb = jnp.moveaxis(q.reshape(B, N_HEADS, 2, n_blk, Q_BLOCK, HEAD_DIM), 3, 0)
    k_pos = jnp.arange(S, dtype=jnp.int32)

    def block(args):
        q_blk, bi = args
        q_pos = bi * Q_BLOCK + jnp.arange(Q_BLOCK, dtype=jnp.int32)
        dist = q_pos[:, None] - k_pos[None, :]
        bias = jnp.transpose(rel_bias[t5_bucket(dist)], (2, 0, 1)).astype(jnp.float32)
        logits = jnp.einsum('bhcqd,bhckd->bhcqk', q_blk, k).astype(jnp.float32)
        logits = logits + bias[None, :, None]
        logits = jnp.where(dist >= 0, logits, -jnp.inf)
        probs = jax.nn.softmax(logits, axis=-1)
        w = probs[:, :, 0] - lam * probs[:, :, 1]
        return jnp.einsum('bhqk,bhkd->bhqd', w.astype(v.dtype), v)

    outs = lax.map(block, (qb, jnp.arange(n_blk, dtype=jnp.int32)))
    o = jnp.transpose(outs, (1, 0, 3, 2, 4)).reshape(B, S, N_HEADS, V_DIM)
    o = rms_norm(o, sub_g) * (1.0 - lambda_init)
    return o.reshape(B, S, N_HEADS * V_DIM) @ w_o

def swiglu(x, w_gate, w_up, w_down):
    return (jax.nn.silu(x @ w_gate) * (x @ w_up)) @ w_down

def first_inputs(seed: int = 0) -> dict:
    key = jax.random.key(seed)
    ks = iter(jax.random.split(key, 64))
    f32 = jnp.float32

    def nrm(shape, scale):
        return jax.random.normal(next(ks), shape, f32) * scale

    def gain(shape):
        return 1.0 + nrm(shape, 0.05)

    D = D_MODEL
    return {
        "x": nrm((BATCH, SEQ, D), 1.0),
        "p": nrm((DEPTH, BATCH, SEQ, PLE_DIM), 1.0),
        "conv_norm_g": gain((N_CONV, D)),
        "conv_w_pw1": nrm((N_CONV, D, 2 * D), D ** -0.5),
        "conv_b_pw1": nrm((N_CONV, 2 * D), 0.02),
        "conv_dw_w": nrm((N_CONV, CONV_WIDTH, D), CONV_WIDTH ** -0.5),
        "conv_dw_b": nrm((N_CONV, D), 0.02),
        "conv_ln_g": gain((N_CONV, D)),
        "conv_ln_b": nrm((N_CONV, D), 0.02),
        "conv_w_pw2": nrm((N_CONV, D, D), D ** -0.5),
        "conv_b_pw2": nrm((N_CONV, D), 0.02),
        "attn_norm_g": gain((N_ATTN, D)),
        "attn_w_qkv": nrm((N_ATTN, D, 3 * D), D ** -0.5),
        "attn_q_norm_g": gain((N_ATTN, HEAD_DIM)),
        "attn_k_norm_g": gain((N_ATTN, HEAD_DIM)),
        "attn_lambda_q1": nrm((N_ATTN, HEAD_DIM), 0.1),
        "attn_lambda_k1": nrm((N_ATTN, HEAD_DIM), 0.1),
        "attn_lambda_q2": nrm((N_ATTN, HEAD_DIM), 0.1),
        "attn_lambda_k2": nrm((N_ATTN, HEAD_DIM), 0.1),
        "attn_sub_norm_g": gain((N_ATTN, V_DIM)),
        "attn_w_o": nrm((N_ATTN, D, D), D ** -0.5),
        "rel_bias": nrm((NUM_BUCKETS, N_HEADS), 0.5),
        "ffn_norm_g": gain((DEPTH, D)),
        "ffn_w_gate": nrm((DEPTH, D, D_FF), D ** -0.5),
        "ffn_w_up": nrm((DEPTH, D, D_FF), D ** -0.5),
        "ffn_w_down": nrm((DEPTH, D_FF, D), D_FF ** -0.5),
        "ple_norm_g": gain((DEPTH, D)),
        "ple_w_gate": nrm((DEPTH, D, D), D ** -0.5),
        "ple_w_proj": nrm((DEPTH, PLE_DIM, D), PLE_DIM ** -0.5),
    }

def first_block(x, p, conv_norm_g, conv_w_pw1, conv_b_pw1, conv_dw_w, conv_dw_b, conv_ln_g,
              conv_ln_b, conv_w_pw2, conv_b_pw2, attn_norm_g, attn_w_qkv, attn_q_norm_g,
              attn_k_norm_g, attn_lambda_q1, attn_lambda_k1, attn_lambda_q2, attn_lambda_k2,
              attn_sub_norm_g, attn_w_o, rel_bias, ffn_norm_g, ffn_w_gate, ffn_w_up, ffn_w_down,
              ple_norm_g, ple_w_gate, ple_w_proj):
    h = x
    for i in range(DEPTH):
        j = i // N_MIXERS
        if i % N_MIXERS == 0:
            u = rms_norm(h, conv_norm_g[j])
            h = h + conformer_conv(u, conv_w_pw1[j], conv_b_pw1[j], conv_dw_w[j], conv_dw_b[j],
                                   conv_ln_g[j], conv_ln_b[j], conv_w_pw2[j], conv_b_pw2[j])
        else:
            lambda_init = 0.8 - 0.6 * math.exp(-0.3 * i)
            u = rms_norm(h, attn_norm_g[j])
            h = h + diff_attention(u, attn_w_qkv[j], attn_q_norm_g[j], attn_k_norm_g[j],
                                   attn_lambda_q1[j], attn_lambda_k1[j], attn_lambda_q2[j],
                                   attn_lambda_k2[j], attn_sub_norm_g[j], attn_w_o[j],
                                   rel_bias, lambda_init)
        u = rms_norm(h, ffn_norm_g[i])
        h = h + swiglu(u, ffn_w_gate[i], ffn_w_up[i], ffn_w_down[i])
        gate = jax.nn.sigmoid(rms_norm(h, ple_norm_g[i]) @ ple_w_gate[i])
        h = h + gate * (p[i] @ ple_w_proj[i])
    return h


DEPTH_2 = 1

CHUNK = 64
SGU_BLOCK = 128
D_A = 1024
A_GROUPS = 8
A_GROUP_DIM = D_A // A_GROUPS
D_B = 1024
POOL_WINDOWS = (2, 4, 8, 16)
B_GROUPS = len(POOL_WINDOWS)
B_GROUP_DIM = D_B // B_GROUPS
D_C = 1024
CONV_WIDTH_2 = 3
N_BRANCH = 3
SPLIT_SIZES = (D_A, D_A, D_A, D_B, D_B, D_C, D_C, D_C, D_C, N_BRANCH * D_MODEL)
N_IN = sum(SPLIT_SIZES)
SPLIT_OFFSETS = tuple(int(o) for o in np.cumsum(SPLIT_SIZES)[:-1])
RMS_EPS = 1e-6
LN_EPS = 1e-5


def rmsnorm(x, g):
    xf = x.astype(jnp.float32)
    y = xf * lax.rsqrt(jnp.mean(xf * xf, axis=-1, keepdims=True) + RMS_EPS)
    return (y * g.astype(jnp.float32)).astype(x.dtype)

def layernorm(x, g, b):
    xf = x.astype(jnp.float32)
    mu = jnp.mean(xf, axis=-1, keepdims=True)
    var = jnp.mean(jnp.square(xf - mu), axis=-1, keepdims=True)
    y = (xf - mu) * lax.rsqrt(var + LN_EPS)
    return (y * g.astype(jnp.float32) + b.astype(jnp.float32)).astype(x.dtype)

def chunk_causal_mask():
    c = jnp.arange(SGU_BLOCK) // CHUNK
    return c[None, :] <= c[:, None]

def spatial_gating(u, v, w_s, b_s, ln_g, ln_b):
    bsz, s, _ = v.shape
    v = layernorm(v, ln_g, ln_b)
    vb = v.reshape(bsz, s // SGU_BLOCK, SGU_BLOCK, A_GROUPS, A_GROUP_DIM)
    w = jnp.where(chunk_causal_mask()[None], w_s, jnp.zeros_like(w_s))
    mixed = jnp.einsum('gij,bnjgc->bnigc', w, vb) + b_s.T[:, :, None]
    return u * mixed.reshape(bsz, s, D_A)

def multiscale_pool(p, w_g, b_g, scale):
    bsz, s, _ = p.shape
    pf = p.astype(jnp.float32)
    csum = jnp.cumsum(pf, axis=1)
    pos1 = jnp.arange(1, s + 1, dtype=jnp.int32)
    outs = []
    for k, win in enumerate(POOL_WINDOWS):
        sl = slice(k * B_GROUP_DIM, (k + 1) * B_GROUP_DIM)
        cg = csum[..., sl]
        shifted = jnp.pad(cg, ((0, 0), (win, 0), (0, 0)))[:, :s]
        count = jnp.minimum(pos1, win).astype(jnp.float32)[:, None]
        outs.append((cg - shifted) / count - pf[..., sl])
    d = jnp.concatenate(outs, axis=-1).astype(p.dtype)
    d = d.reshape(bsz, s, B_GROUPS, B_GROUP_DIM)
    y = jnp.einsum('bsgc,gcd->bsgd', d, w_g).reshape(bsz, s, D_B) + b_g
    return y * scale

def causal_depthwise_conv(h, w, b):
    s = h.shape[1]
    hp = jnp.pad(h, ((0, 0), (CONV_WIDTH_2 - 1, 0), (0, 0)))
    y = sum(w[k] * hp[:, k:k + s] for k in range(CONV_WIDTH_2))
    return y + b

def second_inputs(seed: int = 0) -> dict:
    key = jax.random.key(seed)
    ks = jax.random.split(key, 20)

    def nrm(k, shape, scale):
        return jax.random.normal(k, shape, jnp.float32) * scale

    L = DEPTH_2
    return {
        "x": nrm(ks[0], (BATCH, SEQ, D_MODEL), 1.0),
        "norm_g": 1.0 + nrm(ks[1], (L, D_MODEL), 0.05),
        "w_in": nrm(ks[2], (L, D_MODEL, N_IN), D_MODEL ** -0.5),
        "sgu_ln_g": 1.0 + nrm(ks[3], (L, D_A), 0.05),
        "sgu_ln_b": nrm(ks[4], (L, D_A), 0.02),
        "sgu_w": nrm(ks[5], (L, A_GROUPS, SGU_BLOCK, SGU_BLOCK), SGU_BLOCK ** -0.5),
        "sgu_b": 1.0 + nrm(ks[6], (L, A_GROUPS, SGU_BLOCK), 0.05),
        "pool_w": nrm(ks[7], (L, B_GROUPS, B_GROUP_DIM, B_GROUP_DIM), B_GROUP_DIM ** -0.5),
        "pool_b": nrm(ks[8], (L, D_B), 0.01),
        "pool_scale": 1.0 + nrm(ks[9], (L, D_B), 0.1),
        "conv_w": nrm(ks[10], (L, CONV_WIDTH_2, D_C), CONV_WIDTH_2 ** -0.5),
        "conv_b": nrm(ks[11], (L, D_C), 0.01),
        "w_branch_a": nrm(ks[12], (L, D_A, D_MODEL), D_A ** -0.5),
        "w_branch_b": nrm(ks[13], (L, D_B, D_MODEL), D_B ** -0.5),
        "w_branch_c": nrm(ks[14], (L, D_C, D_MODEL), D_C ** -0.5),
        "w_out": nrm(ks[15], (L, D_MODEL, D_MODEL), D_MODEL ** -0.5),
        "final_g": 1.0 + nrm(ks[16], (D_MODEL,), 0.05),
    }

def second_block(x, norm_g, w_in, sgu_ln_g, sgu_ln_b, sgu_w, sgu_b, pool_w, pool_b,
              pool_scale, conv_w, conv_b, w_branch_a, w_branch_b, w_branch_c,
              w_out, final_g):
    bsz, s, _ = x.shape
    for l in range(DEPTH_2):
        h = rmsnorm(x, norm_g[l])
        proj = jnp.einsum('bsd,dn->bsn', h, w_in[l])
        a_u, a_v, a_z, b_p, b_z, c_h, c_b, c_c, c_z, gate_logits = jnp.split(
            proj, SPLIT_OFFSETS, axis=-1)

        ya = spatial_gating(jax.nn.gelu(a_u), jax.nn.gelu(a_v), sgu_w[l], sgu_b[l],
                            sgu_ln_g[l], sgu_ln_b[l]) * jax.nn.silu(a_z)
        yb = multiscale_pool(b_p, pool_w[l], pool_b[l], pool_scale[l]) * jax.nn.silu(b_z)
        yc = c_b * causal_depthwise_conv(c_c * c_h, conv_w[l], conv_b[l]) * jax.nn.silu(c_z)

        gates = jax.nn.sigmoid(gate_logits.reshape(bsz, s, N_BRANCH, D_MODEL))
        merged = (gates[:, :, 0] * jnp.einsum('bsc,cd->bsd', ya, w_branch_a[l])
                  + gates[:, :, 1] * jnp.einsum('bsc,cd->bsd', yb, w_branch_b[l])
                  + gates[:, :, 2] * jnp.einsum('bsc,cd->bsd', yc, w_branch_c[l]))
        x = x + jnp.einsum('bsd,de->bse', merged, w_out[l])
    return rmsnorm(x, final_g)


def setup_inputs(seed=0):
    out = dict(first_inputs(seed))
    for name, value in second_inputs(seed + 1).items():
        if name != "x":
            out[name + "_2"] = value
    return out


def reference(
    x, p, conv_norm_g, conv_w_pw1, conv_b_pw1, conv_dw_w, conv_dw_b, conv_ln_g, conv_ln_b,
    conv_w_pw2, conv_b_pw2, attn_norm_g, attn_w_qkv, attn_q_norm_g, attn_k_norm_g,
    attn_lambda_q1, attn_lambda_k1, attn_lambda_q2, attn_lambda_k2, attn_sub_norm_g, attn_w_o,
    rel_bias, ffn_norm_g, ffn_w_gate, ffn_w_up, ffn_w_down, ple_norm_g, ple_w_gate, ple_w_proj,
    norm_g_2, w_in_2, sgu_ln_g_2, sgu_ln_b_2, sgu_w_2, sgu_b_2, pool_w_2, pool_b_2,
    pool_scale_2, conv_w_2, conv_b_2, w_branch_a_2, w_branch_b_2, w_branch_c_2, w_out_2,
    final_g_2,
):
    x = first_block(
        x, p, conv_norm_g, conv_w_pw1, conv_b_pw1, conv_dw_w, conv_dw_b, conv_ln_g, conv_ln_b,
        conv_w_pw2, conv_b_pw2, attn_norm_g, attn_w_qkv, attn_q_norm_g, attn_k_norm_g,
        attn_lambda_q1, attn_lambda_k1, attn_lambda_q2, attn_lambda_k2, attn_sub_norm_g,
        attn_w_o, rel_bias, ffn_norm_g, ffn_w_gate, ffn_w_up, ffn_w_down, ple_norm_g,
        ple_w_gate, ple_w_proj,
    )
    return second_block(
        x, norm_g_2, w_in_2, sgu_ln_g_2, sgu_ln_b_2, sgu_w_2, sgu_b_2, pool_w_2, pool_b_2,
        pool_scale_2, conv_w_2, conv_b_2, w_branch_a_2, w_branch_b_2, w_branch_c_2, w_out_2,
        final_g_2,
    )


_drawn_inputs = setup_inputs


def setup_inputs(seed=0):
    import zlib

    import numpy as np

    out = dict(_drawn_inputs(seed))
    spreads = {}
    factors = {'conv_b_pw1': 3.064,
     'conv_ln_b': 3.394,
     'attn_q_norm_g': 2.681,
     'attn_k_norm_g': 2.743,
     'attn_lambda_k2': 4.135,
     'ple_norm_g': 5.14,
     'sgu_ln_g_2': 8.0,
     'sgu_ln_b_2': 48.807,
     'sgu_b_2': 8.0,
     'pool_b_2': 8.0,
     'pool_scale_2': 3.62,
     'conv_b_2': 50.073,
     'attn_lambda_k1': 2.856}
    for name, (base, spread) in spreads.items():
        noise = np.random.default_rng([zlib.crc32(name.encode()), seed]).standard_normal(out[name].shape)
        drawn = base * np.exp(spread * noise) if base else spread * noise
        out[name] = __import__('jax').numpy.asarray(drawn.astype(out[name].dtype))
    for name, factor in factors.items():
        out[name] = (out[name] * factor).astype(out[name].dtype)
    return out
```

```python
import math
from contextlib import ExitStack

import numpy as np

import concourse.bass as bass
from concourse import mybir

F32 = mybir.dt.float32
F32R = mybir.dt.float32r
I32 = mybir.dt.int32
ALU = mybir.AluOpType
ACT = mybir.ActivationFunctionType
AX = mybir.AxisListType.X

P = 128
SEQ, D = 256, 1024
TT = SEQ // P
KB = D // P
DFF = 2816
PLE = 256
TAPS = 31
HEADS = 8
HD = 64
NBUCKET = 32
EPS = 1e-6
LN_EPS_2 = 1e-5
LAMBDA_INIT = 0.8 - 0.6 * math.exp(-0.3)
NEG = -1e30
WINDOWS = (2, 4, 8, 16)
HALF = 2048
RAW, SPLIT = 4, 3
GU = DFF // 256

STREAM = [("pw1", 8), ("proj0", 1), ("pw2", 4), ("ffn0", 33), ("ple0", 4), ("qkv", 12), ("proj1", 1),
          ("wo", 4), ("ffn1", 33), ("ple1", 4), ("av", 4), ("au", 4), ("az", 4), ("ga", 4), ("wa", 4),
          ("bp", 4), ("bz", 4), ("poolw", 1), ("gb", 4), ("wb", 4), ("cc", 16), ("gc", 4), ("wc", 4),
          ("wout", 4)]
G, NPIECE = {}, 0
for _name, _n in STREAM:
    G[_name] = NPIECE
    NPIECE += _n


def gu_at(i):
    return 0 if i == 0 else 2 + 6 * ((i - 1) // 2) + 2 * ((i - 1) % 2)


def down_at(q):
    return 2 + 6 * q + 4


PCOL, PCOLS = {}, 0
for _name, _n in [("conv_g", 8), ("b_a", 8), ("b_g", 8), ("dw_b", 8), ("ln_g", 8), ("ln_b", 8), ("ffn_g0", 8),
                  ("ffn_g1", 8), ("ple_g0", 8), ("ple_g1", 8), ("attn_g", 8), ("norm_g2", 8), ("c3_w", 24),
                  ("c3_b", 8), ("q_g", 1), ("k_g", 1), ("sub_g", 1), ("sgu_b", 8), ("dw_w", 8 * TAPS)]:
    PCOL[_name] = PCOLS
    PCOLS += _n


def build(nc, ws, x_tok, x_feat, p_feat, par, rows, lam_rows, rel, onehot, sgu_w, pool_m, toep, out):
    ctx = ExitStack()
    with ctx:
        def sb(name, shape, dt=F32):
            return ctx.enter_context(nc.sbuf_tensor(name, shape, dt))

        def sem(name):
            return ctx.enter_context(nc.semaphore(name))

        raw = sb("raw", [P, RAW, HALF])
        w_hi = sb("w_hi", [P, SPLIT, HALF], F32R)
        w_lo = sb("w_lo", [P, SPLIT, HALF], F32R)
        h = sb("h", [P, TT, D])
        x_hi = sb("x_hi", [P, KB, SEQ], F32R)
        x_lo = sb("x_lo", [P, KB, SEQ], F32R)
        z_hi = sb("z_hi", [P, KB, SEQ], F32R)
        z_lo = sb("z_lo", [P, KB, SEQ], F32R)
        prm = sb("prm", [P, PCOLS])
        ident = sb("ident", [P, P])
        ones = sb("ones", [P, P])
        st = sb("st", [P, 96])
        st2 = sb("st2", [P, 64])
        NA = 17664
        arena = sb("arena", [P, NA])
        banks = [ctx.enter_context(nc.psum_tensor(f"bank{b}", [P, 512], F32)) for b in range(8)]

        def view(off, *dims):
            n = int(np.prod(dims))
            assert off + n <= NA
            v = arena[:, off:off + n]
            if len(dims) == 1:
                return v
            names = "abc"[:len(dims)]
            return v.rearrange(f"p ({' '.join(names)}) -> p {' '.join(names)}",
                               **{c: d for c, d in zip(names, dims)})

        xf = view(0, KB, SEQ)
        u_pad = view(2048, KB, TAPS - 1 + SEQ)
        y = view(4336, KB, SEQ)
        sq = view(6384, KB, SEQ)
        row_b2 = view(8432, D)
        p_t0 = view(9456, 2, SEQ)
        sig = view(10480, 2, SEQ)
        wide = view(10992, 4, SEQ)
        pp = view(15616, TT, D)
        p_t1 = view(15616, 2, SEQ)
        stage = view(0, 2, 512)
        silu_t = view(1024, 2, 256)
        hid = view(1536, 2, 256)
        gate_t = view(2048, 2, 512)
        prod_t = view(3072, 2, 512)
        junk = view(4096, D)
        wt = view(1024, 384)
        w_f = view(1408, 384)
        oo = view(2048, TT, D)
        lg = view(4096, 2, 384)
        qk_t = arena[:, 5120:7168].rearrange("p (i t c) -> p i t c", i=2, t=TT)
        sq_t = view(7168, 512)
        vv = view(7680, TT, D)
        q_f = view(9728, 4, SEQ)
        k_f = view(10752, 4, SEQ)
        toep_t = view(11776, HEADS, 384)
        pr = view(14848, 2, 384)
        lam_t = view(14848, 4, HD)
        rel_t = arena[0:NBUCKET, 15104:15104 + HEADS]
        onehot_t = arena[0:NBUCKET, 15112:15112 + 384]
        bias_row = arena[0:HEADS, 9728:9728 + 384]
        av = view(2048, TT, D)
        au = view(4096, TT, D)
        az = view(6144, TT, D)
        gate = view(8192, TT, D)
        merged = view(10240, TT, D)
        ln_row = view(12288, 2, D)
        pool_row = view(12288, 2, D)
        sgu_t = view(14336, HEADS, P)
        final_row = view(14336, D)
        pm = view(15360, 4, 384)
        junk_v = view(10240, TT, D)
        junk_f = view(8192, D)
        tmp = view(2048, TT, 512)
        c_h = view(2048, 2, SEQ)
        c_pad = view(2560, 2, SEQ + 2)
        c_y = view(3076, 2, SEQ)
        c_b = view(3588, 2, SEQ)
        c_z = view(4100, 2, SEQ)
        c_s = view(4612, 2, SEQ)
        c_f = view(5124, 2, SEQ)
        rb = view(16896, SEQ)
        rb2 = view(17152, SEQ)
        diag = view(17408, TT, P)

        raw_loaded = [sem(f"raw_loaded{s}") for s in range(RAW)]
        hi_done, lo_done, w_used = sem("hi_done"), sem("lo_done"), sem("w_used")
        pe_filled = sem("pe_filled")
        bank_free = [sem(f"bank_free{b}") for b in range(8)]
        dve_step, act_step, pool_step = sem("dve_step"), sem("act_step"), sem("pool_step")
        ev = {}

        def S(name):
            if name not in ev:
                ev[name] = sem(name)
            return ev[name]

        def col(name, i=0, n=1):
            return prm[:, PCOL[name] + i:PCOL[name] + i + n]

        filled = {}
        jobs = {}
        job_no = {}

        block = ctx.enter_context(nc.Block())

        @block.sync
        def _(sp):
            sp.dma_start(xf, x_feat).then_inc(S("ld_x"), 16)
            for g in range(NPIECE):
                if g >= RAW:
                    sp.wait_ge(lo_done, g - RAW + 1)
                sp.dma_start(raw[:, g % RAW, :], ws[g]).then_inc(raw_loaded[g % RAW], 16)
            for t in range(TT):
                sp.wait_ge(S("out_ready"), t + 1)
                sp.dma_start(out[t * P:(t + 1) * P, :], av[:, t, :]).then_inc(S("stored"), 16)
            sp.wait_ge(S("stored"), 16 * TT)

        def bcast(src, i, n=1):
            return bass.AP(src.tensor, i * D, [[0, P], [D, n], [1, D]]) if n > 1 else \
                bass.AP(src.tensor, i * D, [[0, P], [1, D]])

        @block.tensor
        def _(pe):
            released = [None] * 8
            frees = [0] * 8
            count = {"filled": 0, "gain": 0}

            def begin(b):
                if released[b]:
                    pe.wait_ge(*released[b])

            def end(key, b, ins, piece=None, release=None):
                if release is None:
                    frees[b] += 1
                    release = (bank_free[b], frees[b])
                if piece is None:
                    ins.then_inc(pe_filled, 1)
                    count["filled"] += 1
                    filled[key] = (pe_filled, count["filled"], b, release)
                else:
                    ins.then_inc(w_used, 1)
                    filled[key] = (w_used, piece + 1, b, release)
                released[b] = release

            def mm3(dst, s_hi, s_lo, m_hi, m_lo, first, last):
                pe.matmul(dst, s_hi, m_hi, start=first, stop=False)
                pe.matmul(dst, s_hi, m_lo, start=False, stop=False)
                return pe.matmul(dst, s_lo, m_hi, start=False, stop=last)

            def tok(ap, k, t):
                return ap[:, k, t * P:(t + 1) * P]

            def wait_job(*keys):
                for key in keys:
                    pe.wait_ge(*jobs[key])

            def token_chunk(key, g0, a_hi, a_lo, ready=None, between=None, release=None):
                for a in range(2):
                    if ready:
                        ready(a)
                    pe.wait_ge(lo_done, g0 + a + 1)
                    s = (g0 + a) % SPLIT
                    for t in range(TT):
                        b = t
                        if a == 0:
                            begin(b)
                        for k in range(4):
                            c = slice(k * 512, (k + 1) * 512)
                            ins = mm3(banks[b][:, :], tok(a_hi, 4 * a + k, t), tok(a_lo, 4 * a + k, t),
                                      w_hi[:, s, c], w_lo[:, s, c], a == 0 and k == 0, a == 1 and k == 3)
                        if a == 1:
                            end((key, t), b, ins, g0 + 1 if t == 1 else None, release(t) if release else None)
                        elif t == 1:
                            ins.then_inc(w_used, 1)
                    if a == 0 and between:
                        between()

            def transpose_job(key, src, wait, gain):
                pe.wait_ge(*wait)
                n = job_no[key] = len(job_no)
                b = 2 + n % 2
                begin(b)
                for k in range(4):
                    ins = pe.transpose(banks[b][:, k * P:(k + 1) * P], src[:, k * P:(k + 1) * P], ident[:, :])
                end(("tr",) + key, b, ins)
                if gain:
                    count["gain"] += 1
                    jobs[key] = (S("x_split"), count["gain"])
                else:
                    jobs[key] = released[b]

            def h_release(m, n):
                return lambda t: (S("h_done"), 4 * m + 2 * n + t + 1)

            def h_jobs(m, n):
                for t in range(TT):
                    transpose_job((m, n, t), h[:, t, n * 512:(n + 1) * 512], (S("h_done"), 4 * m + 2 * n + t + 1), True)

            def ready_from(m):
                def ready(a):
                    wait_job((m, a, 0), (m, a, 1))
                return ready

            def projection(layer, g, bank):
                pe.wait_ge(S("p_split"), layer + 1)
                pe.wait_ge(lo_done, g + 1)
                for t in range(TT):
                    for n in range(2):
                        b = bank[2 * t + n]
                        begin(b)
                        for k in range(2):
                            c = slice(k * D + n * 512, k * D + (n + 1) * 512)
                            ins = mm3(banks[b][:, :], tok(z_hi, k, t), tok(z_lo, k, t),
                                      w_hi[:, g % SPLIT, c], w_lo[:, g % SPLIT, c], k == 0, k == 1)
                        end(("proj", layer, t, n), b, ins, g if t == 1 and n == 1 else None)

            def feature_piece(key, g, b, release=None):
                pe.wait_ge(lo_done, g + 1)
                begin(b)
                for c in range(2):
                    for k in range(KB):
                        w = slice(k * 256 + c * P, k * 256 + (c + 1) * P)
                        ins = mm3(banks[b][:, c * SEQ:(c + 1) * SEQ], w_hi[:, g % SPLIT, w], w_lo[:, g % SPLIT, w],
                                  x_hi[:, k, :], x_lo[:, k, :], k == 0, k == KB - 1)
                end(key, b, ins, g, release)

            def ffn(layer, m):
                g0 = G[f"ffn{layer}"]

                def hidden_job(i):
                    n = job_no[("hid", layer, i)] = len(job_no)
                    b = 2 + n % 2
                    begin(b)
                    for t in range(TT):
                        pe.wait_ge(S("hidden"), 2 * (GU * layer + i) + t + 1)
                        for k in range(2):
                            ins = pe.transpose(banks[b][:, k * SEQ + t * P:k * SEQ + (t + 1) * P],
                                               hid[:, t, k * P:(k + 1) * P], ident[:, :])
                    end(("tr", "hid", layer, i), b, ins)
                    jobs[("hid", layer, i)] = released[b]

                def down(q):
                    for a in range(2 if q < 5 else 1):
                        i = 2 * q + a
                        g = g0 + (down_at(q) + a if q < 5 else 32)
                        wait_job(("hid", layer, i))
                        pe.wait_ge(lo_done, g + 1)
                        for n in range(2):
                            for t in range(TT):
                                b = 4 + 2 * n + t
                                if i == 0:
                                    begin(b)
                                for k in range(2):
                                    c = slice(k * D + n * 512, k * D + (n + 1) * 512)
                                    zk = (2 * i + k) % KB
                                    ins = mm3(banks[b][:, :], tok(z_hi, zk, t), tok(z_lo, zk, t),
                                              w_hi[:, g % SPLIT, c], w_lo[:, g % SPLIT, c],
                                              i == 0 and k == 0, i == GU - 1 and k == 1)
                                if i == GU - 1:
                                    end(("ffn", layer, n, t), b, ins, g if n == 1 and t == 1 else None,
                                        (S("h_done"), 4 * (m + 1) + 2 * n + t + 1))
                                elif n == 1 and t == 1:
                                    ins.then_inc(w_used, 1)
                        if q == 4 and a == 0:
                            hidden_job(GU - 1)

                for i in range(GU):
                    token_chunk(("gu", layer, i), g0 + gu_at(i), x_hi, x_lo, ready=ready_from(m) if i == 0 else None,
                                release=lambda t: (S("hidden"), 2 * (GU * layer + i) + t + 1),
                                between=(lambda: hidden_job(i - 1)) if i else None)
                    if i >= 2 and i % 2 == 0:
                        down(i // 2 - 1)
                down(5)
                h_jobs(m + 1, 0)
                h_jobs(m + 1, 1)

            def ple(layer, m):
                g0 = G[f"ple{layer}"]
                token_chunk(("ple", layer, 0), g0, x_hi, x_lo, ready=ready_from(m))
                token_chunk(("ple", layer, 1), g0 + 2, x_hi, x_lo, between=lambda: h_jobs(m + 1, 0))
                h_jobs(m + 1, 1)

            pe.wait_ge(S("consts"), 3)
            begin(4)
            for k in range(KB):
                pe.wait_ge(S("x_sq"), k // 4 + 1)
                ins = pe.matmul(banks[4][:, 0:SEQ], ones[:, :], sq[:, k, :], start=k == 0, stop=k == KB - 1)
            end("x_ss", 4, ins, release=(S("x_r"), 1))
            pe.wait_ge(S("xn_split"), 2)
            for f in range(KB):
                feature_piece(("pw1", f), G["pw1"] + f, f % 2, (S("u"), f + 1))
            projection(0, G["proj0"], (2, 3, 5, 6))
            begin(4)
            for f in range(KB):
                pe.wait_ge(S("conv"), f + 1)
                ins = pe.matmul(banks[4][:, 0:SEQ], ones[:, :], y[:, f, :], start=f == 0, stop=f == KB - 1)
            end("mean", 4, ins, release=(S("centred"), 1))
            begin(7)
            for f in range(KB):
                pe.wait_ge(S("y_sq"), f // 2 + 1)
                ins = pe.matmul(banks[7][:, 0:SEQ], ones[:, :], sq[:, f, :], start=f == 0, stop=f == KB - 1)
            end("var", 7, ins, release=(S("x_r"), 2))

            def z_ready(a):
                pe.wait_ge(S("v_split"), a + 1)
            token_chunk(("pw2", 0), G["pw2"], z_hi, z_lo, ready=z_ready, release=h_release(0, 0))
            token_chunk(("pw2", 1), G["pw2"] + 2, z_hi, z_lo, between=lambda: h_jobs(0, 0), release=h_release(0, 1))
            h_jobs(0, 1)
            ffn(0, 0)
            pe.wait_ge(S("ld_attn"), 16 * 3)
            begin(4)
            end("bias", 4, pe.matmul(banks[4][0:HEADS, 0:384], rel_t, onehot_t, start=True, stop=True))
            ple(0, 1)

            def head(hd):
                j = hd % 4
                for c in range(2):
                    begin(4 + c)
                    r = slice(c * HD, (c + 1) * HD)
                    pe.matmul(banks[4 + c][:, 0:SEQ], q_f[r, j, P:SEQ], k_f[r, j, :], start=True, stop=True)
                    ins = pe.matmul(banks[4 + c][:, SEQ:384], q_f[r, j, 0:P], k_f[r, j, 0:P], start=True, stop=True)
                    end(("lg", hd, c), 4 + c, ins)

            def head_values(hd):
                j = hd % 4
                pe.wait_ge(S("w_mix"), hd + 1)
                n = job_no[("w", hd)] = len(job_no)
                b = 2 + n % 2
                begin(b)
                for k in range(3):
                    ins = pe.transpose(banks[b][:, k * P:(k + 1) * P], wt[:, k * P:(k + 1) * P], ident[:, :])
                end(("tr", "w", hd), b, ins, release=(S("w_copied"), hd + 1))
                if j == 0:
                    begin(6)
                    begin(7)
                pe.wait_ge(S("w_copied"), hd + 1)
                c, d = slice(j * P, (j + 1) * P), slice(hd * P, (hd + 1) * P)
                pe.matmul(banks[7][:, c], w_f[:, 0:P], vv[:, 0, d], start=True, stop=False)
                ins = pe.matmul(banks[7][:, c], w_f[:, P:2 * P], vv[:, 1, d], start=False, stop=True)
                end(("pv", hd, 1), 7, ins, release=(S("o_copied"), 2 * (hd // 4) + 2))
                ins = pe.matmul(banks[6][:, c], w_f[:, 2 * P:3 * P], vv[:, 0, d], start=True, stop=True)
                end(("pv", hd, 0), 6, ins, release=(S("o_copied"), 2 * (hd // 4) + 1))

            for hg in range(2):
                g = G["qkv"] + 6 * hg
                token_chunk(("q", hg), g, x_hi, x_lo, ready=ready_from(2) if hg == 0 else None)
                token_chunk(("k", hg), g + 2, x_hi, x_lo)
                token_chunk(("v", hg), g + 4, x_hi, x_lo, release=lambda t: (S("v_copied"), 2 * hg + t + 1))
                for i in range(2):
                    for t in range(TT):
                        transpose_job(("qk", hg, i, t), qk_t[:, i, t, :], (S("qk_normed"), 4 * hg + 2 * i + t + 1), False)
                wait_job(("qk", hg, 0, 0), ("qk", hg, 0, 1), ("qk", hg, 1, 0), ("qk", hg, 1, 1))
                pe.wait_ge(S("v_copied"), 2 * hg + 2)
                head(4 * hg)
                for j in range(4):
                    hd = 4 * hg + j
                    if j < 3:
                        head(hd + 1)
                    head_values(hd)
            projection(1, G["proj1"], (0, 1, 4, 5))
            for n in range(2):
                for t in range(TT):
                    transpose_job(("o", n, t), oo[:, t, n * 512:(n + 1) * 512], (S("o_normed"), t + 1), True)

            def o_ready(a):
                wait_job(("o", a, 0), ("o", a, 1))
            token_chunk(("wo", 0), G["wo"], z_hi, z_lo, ready=o_ready, release=h_release(3, 0))
            token_chunk(("wo", 1), G["wo"] + 2, z_hi, z_lo, between=lambda: h_jobs(3, 0), release=h_release(3, 1))
            h_jobs(3, 1)
            ffn(1, 3)
            ple(1, 4)

            for name in ("av", "au"):
                for n in range(2):
                    token_chunk((name, n), G[name] + 2 * n, x_hi, x_lo,
                                ready=ready_from(5) if name == "av" and n == 0 else None)
            begin(4)
            pe.wait_ge(S("diag"), 2)
            for t in range(TT):
                ins = pe.matmul(banks[4][:, t * P:(t + 1) * P], ones[:, :], diag[:, t, :], start=True, stop=True)
            end("r_row", 4, ins)
            token_chunk(("az", 0), G["az"], x_hi, x_lo)
            pe.wait_ge(S("sgu_masked"), 1)
            pe.wait_ge(S("sgu_ready"), 2)
            for t in range(TT):
                for q in range(2):
                    b = 4 + 2 * t + q
                    begin(b)
                    for j in range(4):
                        gi = 4 * q + j
                        ins = pe.matmul(banks[b][:, j * P:(j + 1) * P], sgu_t[:, gi, :],
                                        av[:, t, gi * P:(gi + 1) * P], start=True, stop=True)
                    end(("mixed", t, q), b, ins)
            token_chunk(("az", 1), G["az"] + 2, x_hi, x_lo)

            def y_jobs(name, src, n):
                def go():
                    for t in range(TT):
                        transpose_job((name, n, t), src[:, t, n * 512:(n + 1) * 512], (S(name), 2 * n + t + 1), False)
                return go

            def job_ready(name):
                def ready(a):
                    wait_job((name, a, 0), (name, a, 1))
                return ready

            token_chunk(("ga", 0), G["ga"], x_hi, x_lo)
            token_chunk(("ga", 1), G["ga"] + 2, x_hi, x_lo, between=y_jobs("ya", au, 0))
            y_jobs("ya", au, 1)()
            for n in range(2):
                token_chunk(("wa", n), G["wa"] + 2 * n, z_hi, z_lo, ready=job_ready("ya") if n == 0 else None)

            for n in range(2):
                token_chunk(("bp", n), G["bp"] + 2 * n, x_hi, x_lo)
            token_chunk(("bz", 0), G["bz"], x_hi, x_lo)
            for n in range(2):
                for t in range(TT):
                    pe.wait_ge(*filled[(("bp", n), t)][3])
            pe.wait_ge(S("ld_pm"), 16)
            for f in range(KB):
                b = 4 + f // 2
                if f % 2 == 0:
                    begin(b)
                w = f // 2
                dst = banks[b][:, (f % 2) * SEQ:(f % 2 + 1) * SEQ]
                fs = slice(f * P, (f + 1) * P)
                pe.matmul(dst, av[:, 0, fs], pm[:, w, 0:SEQ], start=True, stop=False)
                ins = pe.matmul(dst[:, P:SEQ], av[:, 1, fs], pm[:, w, SEQ:384], start=False, stop=True)
                if f % 2:
                    end(("pool", w), b, ins)
            token_chunk(("bz", 1), G["bz"] + 2, x_hi, x_lo)
            g = G["poolw"]
            pe.wait_ge(lo_done, g + 1)
            for w in range(4):
                pe.wait_ge(*filled[("pool", w)][3])
            for n in range(2):
                for t in range(TT):
                    b = (0, 1)[t]
                    begin(b)
                    for w in (2 * n, 2 * n + 1):
                        for k in range(2):
                            c = slice((2 * w + k) * 256, (2 * w + k + 1) * 256)
                            ins = mm3(banks[b][:, (w % 2) * 256:(w % 2 + 1) * 256], tok(z_hi, 2 * w + k, t),
                                      tok(z_lo, 2 * w + k, t), w_hi[:, g % SPLIT, c], w_lo[:, g % SPLIT, c],
                                      k == 0, k == 1)
                    end(("pooled", n, t), b, ins, g if n == 1 and t == 1 else None)
            token_chunk(("gb", 0), G["gb"], x_hi, x_lo)
            token_chunk(("gb", 1), G["gb"] + 2, x_hi, x_lo, between=y_jobs("yb", au, 0))
            y_jobs("yb", au, 1)()
            for n in range(2):
                token_chunk(("wb", n), G["wb"] + 2 * n, z_hi, z_lo, ready=job_ready("yb") if n == 0 else None)

            for j in range(KB):
                for a in range(2):
                    feature_piece(("cc", j, a), G["cc"] + 2 * j + a, 4 + (2 * j + a) % 4,
                                  (S("c_zr"), j + 1) if a else None)
            for n in range(2):
                token_chunk(("gc", n), G["gc"] + 2 * n, x_hi, x_lo)

            def c_ready(a):
                pe.wait_ge(S("yc_split"), 4 * a + 4)
            token_chunk(("wc", 0), G["wc"], z_hi, z_lo, ready=c_ready)
            token_chunk(("wc", 1), G["wc"] + 2, z_hi, z_lo, between=y_jobs("merged", merged, 0))
            y_jobs("merged", merged, 1)()
            for n in range(2):
                token_chunk(("wout", n), G["wout"] + 2 * n, x_hi, x_lo, ready=job_ready("merged") if n == 0 else None,
                            release=h_release(6, n))

        def take(eng, key):
            s, v, b, _ = filled[key]
            eng.wait_ge(s, v)
            return banks[b], bank_free[b]

        def freed(eng, key):
            eng.wait_ge(*filled[key][3])

        @block.gpsimd
        def _(pool):
            n = [0]

            def link(ins):
                n[0] += 1
                ins.then_inc(pool_step, 1)
                pool.wait_ge(pool_step, n[0])

            pool.dma_start(prm[:, :], par).then_inc(S("ld_par"), 16)
            pool.dma_start(p_t0, p_feat[0]).then_inc(S("ld_p"), 16)
            pool.dma_start(h[:, :, :], x_tok.rearrange("(t p) d -> p t d", p=P)).then_inc(S("ld_h"), 16)
            pool.dma_start(row_b2, bcast(rows, 0)).then_inc(S("ld_h"), 16)
            link(pool.memset(ident[:, :], 0.0))
            pool.affine_select(out=ident[:, :], in_=ident[:, :], compare_op=ALU.not_equal, fill=1.0, base=0,
                               pattern=[[-1, P]], channel_multiplier=1).then_inc(S("consts"), 1)
            pool.memset(ones[:, :], 1.0).then_inc(S("consts"), 1)
            pool.memset(u_pad[:, :, 0:TAPS - 1], 0.0).then_inc(S("consts"), 1)
            pool.wait_ge(S("ld_h"), 32)
            for t in range(TT):
                pool.tensor_tensor(h[:, t, :], h[:, t, :], row_b2, ALU.add).then_inc(S("h_biased"), 1)

            pool.wait_ge(S("h_done"), 4)
            pool.dma_start(rel_t, rel).then_inc(S("ld_attn"), 16)
            pool.dma_start(onehot_t, onehot).then_inc(S("ld_attn"), 16)
            pool.dma_start(lam_t, bass.AP(lam_rows.tensor, 0, [[0, P], [HD, 4], [1, HD]])).then_inc(S("ld_attn"), 16)
            pool.wait_ge(S("bias_row"), 2)
            pool.dma_start(toep, bias_row.unsqueeze(1).to_broadcast([HEADS, P, 384])).then_inc(S("toep_out"), 16)
            pool.wait_ge(S("toep_out"), 16)
            pool.dma_start(toep_t[:, :, 0:SEQ], bass.AP(toep.tensor, P - 1, [[383, P], [P * 384, HEADS], [1, SEQ]])) \
                .then_inc(S("ld_toep"), 16)
            pool.dma_start(toep_t[:, :, SEQ:384], bass.AP(toep.tensor, 2 * P - 1, [[383, P], [P * 384, HEADS], [1, P]])) \
                .then_inc(S("ld_toep"), 16)
            pool.wait_ge(S("h_done"), 12)
            pool.dma_start(p_t1, p_feat[1]).then_inc(S("ld_p"), 16)
            pool.wait_ge(S("h_done"), 16)
            pool.dma_start(ln_row, bcast(rows, 1, 2)).then_inc(S("ld_sgu"), 16)
            pool.dma_start(sgu_t, sgu_w).then_inc(S("ld_sgu"), 16)
            pool.wait_ge(S("ld_sgu"), 32)
            pool.memset(sgu_t[HD:P, :, 0:HD], 0.0).then_inc(S("sgu_masked"), 1)
            pool.wait_ge(S("h_done"), 24)
            pool.dma_start(pm, pool_m).then_inc(S("ld_pm"), 16)
            pool.wait_ge(S("sgu_ready"), 2)
            pool.dma_start(pool_row, bcast(rows, 3, 2)).then_inc(S("ld_pool"), 16)
            for t in range(TT):
                for q in range(2):
                    freed(pool, ("mixed", t, q))
            pool.dma_start(final_row, bcast(rows, 5)).then_inc(S("ld_final"), 16)

        @block.scalar
        def _(act):
            fed = [0]
            n = [0]

            def link(ins):
                n[0] += 1
                ins.then_inc(act_step, 1)
                act.wait_ge(act_step, n[0])

            def feed(to):
                while fed[0] <= min(to, NPIECE - 1):
                    g = fed[0]
                    act.wait_ge(raw_loaded[g % RAW], 16 * (g // RAW + 1))
                    if g >= SPLIT:
                        act.wait_ge(w_used, g - SPLIT + 1)
                    act.activation(w_hi[:, g % SPLIT, :], raw[:, g % RAW, :], ACT.Copy).then_inc(hi_done, 1)
                    fed[0] += 1

            def ahead(g):
                feed(g + SPLIT - 1)

            jn = [0]

            def split_hi(key, dst, k0, w):
                freed(act, ("tr",) + key)
                src = stage[:, job_no[key] % 2, :].rearrange("p (k c) -> p k c", k=4)
                act.activation(dst[:, k0:k0 + 4, w], src, ACT.Copy).then_inc(S("t_hi"), 1)

            def h_split(m, n):
                for t in range(TT):
                    split_hi((m, n, t), x_hi, 4 * n, slice(t * P, (t + 1) * P))

            def h_stats(m):
                for t in range(TT):
                    act.wait_ge(S("h_done"), 4 * m + 3 + t)
                    if t:
                        act.wait_ge(S("h_ss"), 2 * m + 1)
                    act.activation(junk if m < 6 else junk_f, h[:, t, :], ACT.Square,
                                   accum_out=st[:, 2 * m + t:2 * m + t + 1]).then_inc(S("h_ss"), 1)

            def plain_hi(key, dst, k0, w):
                bank, _ = take(act, ("tr",) + key)
                src = bank[:, :].rearrange("p (k c) -> p k c", k=4)
                act.activation(dst[:, k0:k0 + 4, w], src, ACT.Copy).then_inc(S("t_hi"), 1)

            def ffn(layer, m):
                g0 = G[f"ffn{layer}"]

                def hidden_hi(i):
                    bank, _ = take(act, ("tr", "hid", layer, i))
                    k0 = (2 * i) % KB
                    act.activation(z_hi[:, k0:k0 + 2, :], bank[:, :].rearrange("p (k s) -> p k s", k=2),
                                   ACT.Copy).then_inc(S("t_hi"), 1)

                for i in range(GU):
                    g = g0 + gu_at(i)
                    ahead(g)
                    if i:
                        hidden_hi(i - 1)
                    ahead(g + 1)
                    if i == 0:
                        act.wait_ge(S("r_done"), m + 1)
                    for t in range(TT):
                        bank, _ = take(act, (("gu", layer, i), t))
                        if i:
                            act.wait_ge(S("hidden"), 2 * (GU * layer + i - 1) + t + 1)
                        act.activation(silu_t[:, t, :], bank[:, 0:256], ACT.Silu,
                                       scale=st2[:, 2 * m + t:2 * m + t + 1]).then_inc(S("silu"), 1)
                    if i >= 2 and i % 2 == 0:
                        ahead(g0 + down_at(i // 2 - 1))
                        ahead(g0 + down_at(i // 2 - 1) + 1)
                hidden_hi(GU - 1)
                ahead(g0 + 32)
                h_split(m + 1, 0)
                h_split(m + 1, 1)
                h_stats(m + 1)

            gates = [0]

            def ple(layer, m):
                g0 = G[f"ple{layer}"]
                act.wait_ge(S("r_done"), m + 1)
                for n in range(2):
                    ahead(g0 + 2 * n)
                    if n:
                        h_split(m + 1, 0)
                    ahead(g0 + 2 * n + 1)
                    for t in range(TT):
                        bank, free = take(act, (("ple", layer, n), t))
                        if n:
                            act.wait_ge(S("gate_used"), 4 * layer + t + 1)
                        act.activation(gate_t[:, t, :], bank[:, :], ACT.Sigmoid,
                                       scale=st2[:, 2 * m + t:2 * m + t + 1]).then_inc(free, 1)
                h_split(m + 1, 1)
                h_stats(m + 1)

            def p_split(layer):
                act.wait_ge(S("ld_p"), 16 * (layer + 1))
                act.activation(z_hi[:, 0:2, :], p_t1 if layer else p_t0, ACT.Copy).then_inc(S("p_hi"), 1)

            def proj_copy(layer):
                for t in range(TT):
                    for n in range(2):
                        bank, free = take(act, ("proj", layer, t, n))
                        act.activation(pp[:, t, n * 512:(n + 1) * 512], bank[:, :], ACT.Copy).then_inc(free, 1)

            act.wait_ge(S("ld_x"), 16)
            for k in range(2):
                act.activation(sq[:, 4 * k:4 * k + 4, :], xf[:, 4 * k:4 * k + 4, :], ACT.Square).then_inc(S("x_sq"), 1)
            feed(SPLIT - 1)
            for k in range(2):
                act.wait_ge(S("xn"), 4 * k + 4)
                act.activation(x_hi[:, 4 * k:4 * k + 4, :], xf[:, 4 * k:4 * k + 4, :], ACT.Copy).then_inc(S("xn_hi"), 1)
            p_split(0)
            act.wait_ge(S("ld_par"), 16)
            for f in range(KB):
                ahead(G["pw1"] + f)
                bank, _ = take(act, ("pw1", f))
                if f >= 2:
                    act.wait_ge(S("u"), f - 1)
                act.activation(sig[:, f % 2, :], bank[:, SEQ:2 * SEQ], ACT.Sigmoid, bias=col("b_g", f)).then_inc(S("sig"), 1)
            ahead(G["proj0"])
            proj_copy(0)
            for f in range(4):
                act.wait_ge(S("centred"), 1)
                act.activation(sq[:, 2 * f:2 * f + 2, :], y[:, 2 * f:2 * f + 2, :], ACT.Square).then_inc(S("y_sq"), 1)
            for a in range(2):
                for f in range(4 * a, 4 * a + 4):
                    act.wait_ge(S("scaled"), a + 1)
                    act.activation(xf[:, f, :], y[:, f, :], ACT.Silu, scale=col("ln_g", f), bias=col("ln_b", f)) \
                       .then_inc(S("v_act"), 1)
            ahead(G["pw2"] + 2)
            h_split(0, 0)
            ahead(G["pw2"] + 3)
            h_split(0, 1)
            h_stats(0)
            ffn(0, 0)
            ple(0, 1)

            ahead(G["qkv"])
            act.wait_ge(S("lam_sum"), 1)
            act.activation(st[:, 90:92], st[:, 88:90], ACT.Exp).then_inc(S("lam_exp"), 1)
            p_split(1)
            act.wait_ge(S("r_done"), 3)
            act.wait_ge(S("attn_small"), 3)
            for hg in range(2):
                g = G["qkv"] + 6 * hg
                for i in range(2):
                    ahead(g + 2 * i + 1)
                    for t in range(TT):
                        bank, free = take(act, (("qk"[i], hg), t))
                        r = st2[:, 4 + t:5 + t]
                        if hg:
                            freed(act, ("tr", "qk", 0, i, t))
                        act.activation(qk_t[:, i, t, :], bank[:, :], ACT.Copy, scale=r).then_inc(free, 1)
                ahead(g + 5)
                for t in range(TT):
                    bank, free = take(act, (("v", hg), t))
                    act.activation(vv[:, t, hg * 512:(hg + 1) * 512], bank[:, :], ACT.Copy, scale=st2[:, 4 + t:5 + t]) \
                       .then_inc(S("v_copied"), 1)
                for i in range(2):
                    for t in range(TT):
                        key = ("qk", hg, i, t)
                        bank, free = take(act, ("tr",) + key)
                        act.activation((q_f, k_f)[i][:, :, t * P:(t + 1) * P],
                                       bank[:, :].rearrange("p (j s) -> p j s", j=4), ACT.Copy,
                                       scale=st[:, 92 + i:93 + i]).then_inc(free, 1)
                for j in range(4):
                    hd = 4 * hg + j
                    act.wait_ge(S("row_max"), hd + 1)
                    for c in range(2):
                        act.activation(pr[:, c, 0:SEQ], lg[:, c, 0:SEQ], ACT.Exp, bias=st[:, 64 + c:65 + c],
                                       accum_out=st[:, 68 + c:69 + c])
                        act.activation(pr[:, c, SEQ:384], lg[:, c, SEQ:384], ACT.Exp, bias=st[:, 66 + c:67 + c],
                                       accum_out=st[:, 70 + c:71 + c]).then_inc(S("exps"), 1)
                    bank, free = take(act, ("tr", "w", hd))
                    if hd:
                        take(act, ("pv", hd - 1, 0))
                    act.activation(w_f, bank[:, 0:384], ACT.Copy).then_inc(S("w_copied"), 1)
                for t in range(TT):
                    bank, _ = take(act, ("pv", 4 * hg + 3, t))
                    act.activation(oo[:, t, hg * 512:(hg + 1) * 512], bank[:, :], ACT.Copy).then_inc(S("o_copied"), 1)
            ahead(G["proj1"])
            proj_copy(1)
            for k in range(2):
                for t in range(TT):
                    split_hi(("o", k, t), z_hi, 4 * k, slice(t * P, (t + 1) * P))
            ahead(G["wo"] + 2)
            h_split(3, 0)
            ahead(G["wo"] + 3)
            h_split(3, 1)
            h_stats(3)
            ffn(1, 3)
            ple(1, 4)

            act.wait_ge(S("r_done"), 6)

            def evac(name, func, dst, extra=None, accum=None, sig=None):
                for n in range(2):
                    ahead(G[name] + 2 * n + 1)
                    for t in range(TT):
                        bank, free = take(act, ((name, n), t))
                        if extra:
                            extra(n, t)
                        act.activation(dst[:, t, n * 512:(n + 1) * 512], bank[:, :], func, scale=st2[:, 10 + t:11 + t],
                                       **({"accum_out": accum[:, 2 * t + n:2 * t + n + 1]} if accum is not None else {})) \
                           .then_inc(free, 1)

            evac("av", ACT.Gelu_apprx_tanh, av, accum=st[:, 16:20])
            act.wait_ge(S("v_mean"), 1)
            for t in range(TT):
                act.activation(junk_v[:, t, :], av[:, t, :], ACT.Square, bias=st[:, 20 + t:21 + t],
                               accum_out=st[:, 22 + t:23 + t]).then_inc(S("v_var"), 1)
            evac("au", ACT.Gelu_apprx_tanh, au)
            evac("az", ACT.Silu, az)
            for n in range(2):
                ahead(G["ga"] + 2 * n)
                if n:
                    for t in range(TT):
                        plain_hi(("ya", 0, t), z_hi, 0, slice(t * P, (t + 1) * P))
                ahead(G["ga"] + 2 * n + 1)
                for t in range(TT):
                    bank, free = take(act, (("ga", n), t))
                    act.activation(gate[:, t, n * 512:(n + 1) * 512], bank[:, :], ACT.Sigmoid,
                                   scale=st2[:, 10 + t:11 + t]).then_inc(free, 1)
            for t in range(TT):
                plain_hi(("ya", 1, t), z_hi, 4, slice(t * P, (t + 1) * P))
            ahead(G["wa"] + 3)
            evac("bp", ACT.Copy, av, extra=lambda n, t: freed(act, ("mixed", 1, 1)))
            for n in range(2):
                ahead(G["bz"] + 2 * n + 1)
                if n:
                    for w in range(4):
                        bank, _ = take(act, ("pool", w))
                        act.activation(z_hi[:, 2 * w:2 * w + 2, :], bank[:, :].rearrange("p (k s) -> p k s", k=2),
                                       ACT.Copy).then_inc(S("t_hi"), 1)
                for t in range(TT):
                    bank, free = take(act, (("bz", n), t))
                    if n == 0 and t == 0:
                        act.wait_ge(S("ya"), 4)
                    act.activation(az[:, t, n * 512:(n + 1) * 512], bank[:, :], ACT.Silu,
                                   scale=st2[:, 10 + t:11 + t]).then_inc(free, 1)
            ahead(G["poolw"])
            for n in range(2):
                ahead(G["gb"] + 2 * n)
                if n:
                    for t in range(TT):
                        plain_hi(("yb", 0, t), z_hi, 0, slice(t * P, (t + 1) * P))
                ahead(G["gb"] + 2 * n + 1)
                for t in range(TT):
                    bank, free = take(act, (("gb", n), t))
                    freed(act, (("wa", n), t))
                    act.activation(gate[:, t, n * 512:(n + 1) * 512], bank[:, :], ACT.Sigmoid,
                                   scale=st2[:, 10 + t:11 + t]).then_inc(free, 1)
            for t in range(TT):
                plain_hi(("yb", 1, t), z_hi, 4, slice(t * P, (t + 1) * P))
            ahead(G["wb"] + 3)
            act.wait_ge(S("c_zero"), 1)
            for j in range(KB):
                g = G["cc"] + 2 * j
                ahead(g)
                s = j % 2
                bank, free = take(act, ("cc", j, 0))
                if j >= 2:
                    act.wait_ge(S("yc_split"), j - 1)
                act.activation(c_h[:, s, :], bank[:, 0:SEQ], ACT.Copy).then_inc(S("c_hc"), 1)
                ahead(g + 1)
                act.wait_ge(S("c_zr"), j + 1)
                act.activation(c_s[:, s, :], c_z[:, s, :], ACT.Silu).then_inc(S("c_silu"), 1)
                act.wait_ge(S("yc"), j + 1)
                act.activation(z_hi[:, j, :], c_f[:, s, :], ACT.Copy).then_inc(S("yc_hi"), 1)
            for n in range(2):
                ahead(G["gc"] + 2 * n + 1)
                for t in range(TT):
                    bank, free = take(act, (("gc", n), t))
                    freed(act, (("wb", n), t))
                    act.activation(gate[:, t, n * 512:(n + 1) * 512], bank[:, :], ACT.Sigmoid,
                                   scale=st2[:, 10 + t:11 + t]).then_inc(free, 1)
            ahead(G["wc"] + 2)
            for t in range(TT):
                plain_hi(("merged", 0, t), x_hi, 0, slice(t * P, (t + 1) * P))
            ahead(G["wc"] + 3)
            for t in range(TT):
                plain_hi(("merged", 1, t), x_hi, 4, slice(t * P, (t + 1) * P))
            ahead(NPIECE)
            h_stats(6)

        @block.vector
        def _(dve):
            fed = [0]
            n = [0]

            def link(ins):
                n[0] += 1
                ins.then_inc(dve_step, 1)
                dve.wait_ge(dve_step, n[0])

            def feed(to):
                while fed[0] <= min(to, NPIECE - 1):
                    g = fed[0]
                    dve.wait_ge(hi_done, g + 1)
                    dve.tensor_tensor(w_lo[:, g % SPLIT, :], raw[:, g % RAW, :], w_hi[:, g % SPLIT, :].bitcast(F32),
                                      ALU.subtract).then_inc(lo_done, 1)
                    fed[0] += 1

            def ahead(g):
                feed(g + SPLIT - 1)

            def rsqrt(src, v, yy, tmp, scale, eps, done):
                link(dve.tensor_scalar(v, src, scale, eps, ALU.mult, ALU.add))
                link(dve.tensor_scalar(yy.bitcast(I32), v.bitcast(I32), 1, None, ALU.logical_shift_right))
                link(dve.tensor_scalar(yy.bitcast(I32), yy.bitcast(I32), -1.0, float(0x5F3759DF), ALU.mult, ALU.add))
                for it in range(3):
                    link(dve.tensor_tensor(tmp, yy, yy, ALU.mult))
                    link(dve.scalar_tensor_tensor(out=tmp, in0=v, scalar=-0.5, in1=tmp, op0=ALU.mult, op1=ALU.mult))
                    ins = dve.scalar_tensor_tensor(out=yy, in0=tmp, scalar=1.5, in1=yy, op0=ALU.add, op1=ALU.mult)
                    if it < 2:
                        link(ins)
                ins.then_inc(done, 1)

            hi_count = [0]
            stage_read = [0, 0]
            split_count = [0]

            def gain_block(key, gain, gcols):
                bank, free = take(dve, ("tr",) + key)
                s = job_no[key] % 2
                if stage_read[s]:
                    dve.wait_ge(S("x_split"), stage_read[s])
                dve.tensor_tensor(stage[:, s, :].rearrange("p (k c) -> p k c", k=4),
                                  bank[:, :].rearrange("p (k c) -> p k c", k=4),
                                  gain.unsqueeze(2).to_broadcast([P, 4, P]), ALU.mult).then_inc(free, 1)

            def split_lo(key, hi, lo, k0, w):
                s = job_no[key] % 2
                hi_count[0] += 1
                split_count[0] += 1
                stage_read[s] = split_count[0]
                dve.wait_ge(S("t_hi"), hi_count[0])
                dve.tensor_tensor(lo[:, k0:k0 + 4, w], stage[:, s, :].rearrange("p (k c) -> p k c", k=4),
                                  hi[:, k0:k0 + 4, w].bitcast(F32), ALU.subtract).then_inc(S("x_split"), 1)

            def h_split(m, n, gname):
                for t in range(TT):
                    gain_block((m, n, t), col(gname, 4 * n, 4), 4)
                for t in range(TT):
                    split_lo((m, n, t), x_hi, x_lo, 4 * n, slice(t * P, (t + 1) * P))

            def h_factor(m):
                dve.wait_ge(S("h_ss"), 2 * m + 2)
                c = slice(2 * m, 2 * m + 2)
                rsqrt(st[:, c], st2[:, 60:62], st2[:, c], st2[:, 62:64], 1.0 / D, EPS, S("r_done"))

            def plain_lo(key, hi, lo, k0, w):
                bank, free = take(dve, ("tr",) + key)
                hi_count[0] += 1
                dve.wait_ge(S("t_hi"), hi_count[0])
                dve.tensor_tensor(lo[:, k0:k0 + 4, w], bank[:, :].rearrange("p (k c) -> p k c", k=4),
                                  hi[:, k0:k0 + 4, w].bitcast(F32), ALU.subtract).then_inc(free, 1)

            def ffn(layer, m, gname):
                g0 = G[f"ffn{layer}"]

                def hidden_lo(i):
                    bank, free = take(dve, ("tr", "hid", layer, i))
                    k0 = (2 * i) % KB
                    hi_count[0] += 1
                    dve.wait_ge(S("t_hi"), hi_count[0])
                    dve.tensor_tensor(z_lo[:, k0:k0 + 2, :], bank[:, :].rearrange("p (k s) -> p k s", k=2),
                                      z_hi[:, k0:k0 + 2, :].bitcast(F32), ALU.subtract).then_inc(free, 1)

                dve.wait_ge(S("r_done"), m + 1)
                for i in range(GU):
                    g = g0 + gu_at(i)
                    ahead(g)
                    if i:
                        hidden_lo(i - 1)
                    ahead(g + 1)
                    for t in range(TT):
                        bank, free = take(dve, (("gu", layer, i), t))
                        dve.wait_ge(S("silu"), 2 * (GU * layer + i) + t + 1)
                        dve.scalar_tensor_tensor(out=hid[:, t, :], in0=bank[:, 256:512],
                                                 scalar=st2[:, 2 * m + t:2 * m + t + 1], in1=silu_t[:, t, :],
                                                 op0=ALU.mult, op1=ALU.mult).then_inc(S("hidden"), 1)
                    if i >= 2 and i % 2 == 0:
                        ahead(g0 + down_at(i // 2 - 1))
                        ahead(g0 + down_at(i // 2 - 1) + 1)
                hidden_lo(GU - 1)
                ahead(g0 + 32)
                for n in range(2):
                    for t in range(TT):
                        add_h(("ffn", layer, n, t), n, t)
                    h_split(m + 1, n, gname)
                h_factor(m + 1)

            def add_h(key, n, t):
                bank, free = take(dve, key)
                hs = h[:, t, n * 512:(n + 1) * 512]
                dve.tensor_tensor(hs, hs, bank[:, :], ALU.add).then_inc(S("h_done"), 1)

            def ple(layer, m, gname):
                g0 = G[f"ple{layer}"]
                for n in range(2):
                    ahead(g0 + 2 * n)
                    if n:
                        h_split(m + 1, 0, gname)
                    ahead(g0 + 2 * n + 1)
                    for t in range(TT):
                        freed(dve, (("ple", layer, n), t))
                        c = slice(n * 512, (n + 1) * 512)
                        dve.tensor_tensor(prod_t[:, t, :], gate_t[:, t, :], pp[:, t, c], ALU.mult).then_inc(S("gate_used"), 1)
                        dve.wait_ge(S("gate_used"), 4 * layer + 2 * n + t + 1)
                        dve.tensor_tensor(h[:, t, c], h[:, t, c], prod_t[:, t, :], ALU.add).then_inc(S("h_done"), 1)
                h_split(m + 1, 1, gname)
                h_factor(m + 1)

            feed(0)
            bank, free = take(dve, "x_ss")
            rsqrt(bank[:, 0:SEQ], wide[:, 0, :], wide[:, 1, :], wide[:, 2, :], 1.0 / D, EPS, S("x_r"))
            dve.wait_ge(S("x_r"), 1)
            dve.wait_ge(S("ld_par"), 16)
            for k in range(KB):
                dve.scalar_tensor_tensor(out=xf[:, k, :], in0=xf[:, k, :], scalar=col("conv_g", k), in1=wide[:, 1, :],
                                         op0=ALU.mult, op1=ALU.mult).then_inc(S("xn"), 1)
            for a in range(2):
                dve.wait_ge(S("xn_hi"), a + 1)
                k = slice(4 * a, 4 * a + 4)
                dve.tensor_tensor(x_lo[:, k, :], xf[:, k, :], x_hi[:, k, :].bitcast(F32), ALU.subtract) \
                   .then_inc(S("xn_split"), 1)
            feed(SPLIT - 1)

            def p_split(layer):
                dve.wait_ge(S("p_hi"), layer + 1)
                dve.tensor_tensor(z_lo[:, 0:2, :], p_t1 if layer else p_t0, z_hi[:, 0:2, :].bitcast(F32),
                                  ALU.subtract).then_inc(S("p_split"), 1)

            p_split(0)
            dve.wait_ge(S("consts"), 3)

            def gated(f):
                ahead(G["pw1"] + f)
                bank, free = take(dve, ("pw1", f))
                dve.wait_ge(S("sig"), f + 1)
                dve.scalar_tensor_tensor(out=u_pad[:, f, TAPS - 1:], in0=bank[:, 0:SEQ], scalar=col("b_a", f),
                                         in1=sig[:, f % 2, :], op0=ALU.add, op1=ALU.mult).then_inc(S("u"), 1)

            gated(0)
            for f in range(KB):
                if f + 1 < KB:
                    gated(f + 1)
                dve.wait_ge(S("u"), f + 1)
                link(dve.tensor_scalar(y[:, f, :], u_pad[:, f, 0:SEQ], col("dw_w", f * TAPS), col("dw_b", f),
                                       ALU.mult, ALU.add))
                for tap in range(1, TAPS):
                    ins = dve.scalar_tensor_tensor(out=y[:, f, :], in0=u_pad[:, f, tap:tap + SEQ],
                                                   scalar=col("dw_w", f * TAPS + tap), in1=y[:, f, :],
                                                   op0=ALU.mult, op1=ALU.add)
                    if tap < TAPS - 1:
                        link(ins)
                    else:
                        ins.then_inc(S("conv"), 1)
            ahead(G["proj0"])
            bank, free = take(dve, "mean")
            link(dve.tensor_scalar(wide[:, 3, :], bank[:, 0:SEQ], 1.0 / D, None, ALU.mult))
            dve.wait_ge(S("conv"), KB)
            dve.tensor_tensor(y, y, wide[:, 3:4, :].to_broadcast([P, KB, SEQ]), ALU.subtract).then_inc(S("centred"), 1)
            dve.wait_ge(S("centred"), 1)
            bank, free = take(dve, "var")
            rsqrt(bank[:, 0:SEQ], wide[:, 0, :], wide[:, 1, :], wide[:, 2, :], 1.0 / D, EPS, S("x_r"))
            dve.wait_ge(S("x_r"), 2)
            for a in range(2):
                k = slice(4 * a, 4 * a + 4)
                dve.tensor_tensor(y[:, k, :], y[:, k, :], wide[:, 1:2, :].to_broadcast([P, 4, SEQ]), ALU.mult) \
                   .then_inc(S("scaled"), 1)
            for a in range(2):
                k = slice(4 * a, 4 * a + 4)
                dve.wait_ge(S("v_act"), 4 * a + 4)
                take(dve, ("proj", 0, 1, 1))
                link(dve.tensor_copy(z_hi[:, k, :], xf[:, k, :]))
                dve.tensor_tensor(z_lo[:, k, :], xf[:, k, :], z_hi[:, k, :].bitcast(F32), ALU.subtract) \
                   .then_inc(S("v_split"), 1)
            dve.wait_ge(S("h_biased"), 2)
            ahead(G["pw2"] + 1)
            for t in range(TT):
                add_h((("pw2", 0), t), 0, t)
            ahead(G["pw2"] + 2)
            h_split(0, 0, "ffn_g0")
            ahead(G["pw2"] + 3)
            for t in range(TT):
                add_h((("pw2", 1), t), 1, t)
            h_split(0, 1, "ffn_g0")
            h_factor(0)
            ffn(0, 0, "ple_g0")
            bank, free = take(dve, "bias")
            dve.tensor_copy(bias_row[:, 0:SEQ], bank[0:HEADS, 0:SEQ]).then_inc(free, 1)
            freed(dve, "bias")
            dve.tensor_scalar(bias_row[:, 0:1], bias_row[:, 0:1], 1.0, None, ALU.mult).then_inc(S("bias_row"), 1)
            dve.memset(bias_row[:, SEQ:384], NEG).then_inc(S("bias_row"), 1)
            link(dve.tensor_tensor(lam_t[:, 0:4:2, :], lam_t[:, 0:4:2, :], lam_t[:, 1:4:2, :], ALU.mult))
            dve.tensor_reduce(st[:, 88:90], lam_t[:, 0:4:2, :], AX, ALU.add).then_inc(S("lam_sum"), 1)
            dve.tensor_scalar(st[:, 92:93], col("q_g"), HD ** -0.5, None, ALU.mult).then_inc(S("attn_small"), 1)
            dve.tensor_scalar(st[:, 93:94], col("k_g"), 1.0, None, ALU.mult).then_inc(S("attn_small"), 1)
            dve.tensor_scalar(st[:, 95:96], col("sub_g"), 1.0 - LAMBDA_INIT, None, ALU.mult).then_inc(S("attn_small"), 1)
            ple(0, 1, "attn_g")

            ahead(G["qkv"])
            dve.wait_ge(S("lam_exp"), 1)
            link(dve.tensor_tensor(st[:, 94:95], st[:, 91:92], st[:, 90:91], ALU.subtract))
            link(dve.tensor_scalar(st[:, 94:95], st[:, 94:95], -LAMBDA_INIT, None, ALU.add))
            p_split(1)
            for hg in range(2):
                g = G["qkv"] + 6 * hg
                for i in range(2):
                    ahead(g + 2 * i + 1)
                    for t in range(TT):
                        freed(dve, (("qk"[i], hg), t))
                        link(dve.tensor_tensor(sq_t, qk_t[:, i, t, :], qk_t[:, i, t, :], ALU.mult))
                        c = 16 + 16 * i + 8 * t
                        dve.tensor_reduce(st[:, c:c + 8], sq_t.rearrange("p (g d) -> p g d", d=HD), AX, ALU.add) \
                           .then_inc(S("qk_ss"), 1)
                        dve.wait_ge(S("qk_ss"), 4 * hg + 2 * i + t + 1)
                rsqrt(st[:, 16:48], sq_t[:, 0:32], st2[:, 16:48], sq_t[:, 32:64], 1.0 / HD, EPS, S("qk_r"))
                dve.wait_ge(S("qk_r"), hg + 1)
                for i in range(2):
                    for t in range(TT):
                        v = qk_t[:, i, t, :].rearrange("p (g d) -> p g d", d=HD)
                        c = 16 + 16 * i + 8 * t
                        dve.tensor_tensor(v, v, st2[:, c:c + 8].unsqueeze(2).to_broadcast([P, 8, HD]), ALU.mult) \
                           .then_inc(S("qk_normed"), 1)
                ahead(g + 5)
                dve.wait_ge(S("ld_toep"), 32)
                for j in range(4):
                    hd = 4 * hg + j
                    for c in range(2):
                        bank, free = take(dve, ("lg", hd, c))
                        dve.tensor_tensor(lg[:, c, :], bank[:, 0:384], toep_t[:, hd, :], ALU.add).then_inc(free, 1)
                    for c in range(2):
                        freed(dve, ("lg", hd, c))
                    link(dve.tensor_reduce(st[:, 64:66], lg[:, :, 0:SEQ], AX, ALU.max, negate=True))
                    dve.tensor_reduce(st[:, 66:68], lg[:, :, SEQ:384], AX, ALU.max, negate=True) \
                       .then_inc(S("row_max"), 1)
                    dve.wait_ge(S("exps"), 2 * hd + 2)
                    link(dve.reciprocal(st[:, 72:76], st[:, 68:72]))
                    link(dve.tensor_scalar(st[:, 73:76:2], st[:, 73:76:2], st[:, 94:95], None, ALU.mult))
                    if hd:
                        take(dve, ("tr", "w", hd - 1))
                    link(dve.tensor_scalar(wt[:, 0:SEQ], pr[:, 0, 0:SEQ], st[:, 72:73], None, ALU.mult))
                    link(dve.tensor_scalar(wt[:, SEQ:384], pr[:, 0, SEQ:384], st[:, 74:75], None, ALU.mult))
                    link(dve.scalar_tensor_tensor(out=wt[:, 0:SEQ], in0=pr[:, 1, 0:SEQ], scalar=st[:, 73:74],
                                                  in1=wt[:, 0:SEQ], op0=ALU.mult, op1=ALU.add))
                    dve.scalar_tensor_tensor(out=wt[:, SEQ:384], in0=pr[:, 1, SEQ:384], scalar=st[:, 75:76],
                                             in1=wt[:, SEQ:384], op0=ALU.mult, op1=ALU.add).then_inc(S("w_mix"), 1)
                for t in range(TT):
                    dve.wait_ge(S("o_copied"), 2 * hg + t + 1)
                    o = oo[:, t, hg * 512:(hg + 1) * 512]
                    link(dve.tensor_tensor(sq_t, o, o, ALU.mult))
                    c = 48 + 8 * t + 4 * hg
                    dve.tensor_reduce(st[:, c:c + 4], sq_t.rearrange("p (g d) -> p g d", d=P), AX, ALU.add) \
                       .then_inc(S("o_ss"), 1)
                    dve.wait_ge(S("o_ss"), 2 * hg + t + 1)
            rsqrt(st[:, 48:64], sq_t[:, 0:16], st2[:, 16:32], sq_t[:, 16:32], 1.0 / P, EPS, S("o_r"))
            dve.wait_ge(S("o_r"), 1)
            for t in range(TT):
                v = oo[:, t, :].rearrange("p (g d) -> p g d", d=P)
                dve.tensor_tensor(v, v, st2[:, 16 + 8 * t:24 + 8 * t].unsqueeze(2).to_broadcast([P, 8, P]), ALU.mult) \
                   .then_inc(S("o_normed"), 1)
            ahead(G["proj1"])
            for n_ in range(2):
                for t in range(TT):
                    gain_block(("o", n_, t), st[:, 95:96], 1)
                for t in range(TT):
                    split_lo(("o", n_, t), z_hi, z_lo, 4 * n_, slice(t * P, (t + 1) * P))
            ahead(G["wo"] + 1)
            for t in range(TT):
                add_h((("wo", 0), t), 0, t)
            ahead(G["wo"] + 2)
            h_split(3, 0, "ffn_g1")
            ahead(G["wo"] + 3)
            for t in range(TT):
                add_h((("wo", 1), t), 1, t)
            h_split(3, 1, "ffn_g1")
            h_factor(3)
            ffn(1, 3, "ple_g1")
            ple(1, 4, "norm_g2")

            ahead(G["av"] + 3)
            for n_ in range(2):
                for t in range(TT):
                    freed(dve, (("av", n_), t))
            link(dve.tensor_tensor(st[:, 20:22], st[:, 16:20:2], st[:, 17:20:2], ALU.add))
            dve.tensor_scalar(st[:, 20:22], st[:, 20:22], -1.0 / D, None, ALU.mult).then_inc(S("v_mean"), 1)
            dve.wait_ge(S("v_mean"), 1)
            dve.wait_ge(S("v_var"), 2)
            rsqrt(st[:, 22:24], st2[:, 60:62], st2[:, 22:24], st2[:, 62:64], 1.0 / D, LN_EPS_2, S("v_r"))
            dve.wait_ge(S("v_r"), 1)
            dve.wait_ge(S("ld_sgu"), 32)
            for t in range(TT):
                link(dve.tensor_scalar(av[:, t, :], av[:, t, :], st[:, 20 + t:21 + t], st2[:, 22 + t:23 + t],
                                       ALU.add, ALU.mult))
                link(dve.tensor_tensor(av[:, t, :], av[:, t, :], ln_row[:, 0, :], ALU.mult))
                dve.tensor_tensor(av[:, t, :], av[:, t, :], ln_row[:, 1, :], ALU.add).then_inc(S("sgu_ready"), 1)
                ahead(G["au"] + t)
            for t in range(TT):
                dve.tensor_scalar(diag[:, t, :], ident[:, :], st2[:, 10 + t:11 + t], None, ALU.mult).then_inc(S("diag"), 1)
            ahead(G["au"] + 3)
            bank, free = take(dve, "r_row")
            dve.tensor_copy(rb, bank[:, 0:SEQ]).then_inc(free, 1)
            freed(dve, "r_row")
            link(dve.tensor_tensor(rb2, rb, rb, ALU.mult))
            ahead(G["az"] + 1)
            for n_ in range(2):
                for t in range(TT):
                    bank, free = take(dve, ("mixed", t, n_))
                    freed(dve, (("au", n_), t))
                    for j in range(4):
                        gi = 4 * n_ + j
                        c = slice(gi * P, (gi + 1) * P)
                        ins = dve.scalar_tensor_tensor(out=au[:, t, c], in0=bank[:, j * P:(j + 1) * P],
                                                       scalar=col("sgu_b", gi), in1=au[:, t, c], op0=ALU.add, op1=ALU.mult)
                    ins.then_inc(free, 1)
                if n_:
                    ahead(G["az"] + 3)
                for t in range(TT):
                    freed(dve, ("mixed", t, n_))
                    freed(dve, (("az", n_), t))
                    c = slice(n_ * 512, (n_ + 1) * 512)
                    dve.tensor_tensor(au[:, t, c], au[:, t, c], az[:, t, c], ALU.mult).then_inc(S("ya"), 1)
            for n_ in range(2):
                ahead(G["ga"] + 2 + n_)
                for t in range(TT):
                    plain_lo(("ya", n_, t), z_hi, z_lo, 4 * n_, slice(t * P, (t + 1) * P))
            for n_ in range(2):
                ahead(G["wa"] + 2 * n_ + 1)
                for t in range(TT):
                    c = slice(n_ * 512, (n_ + 1) * 512)
                    bank, free = take(dve, (("wa", n_), t))
                    freed(dve, (("ga", n_), t))
                    dve.tensor_tensor(merged[:, t, c], bank[:, :], gate[:, t, c], ALU.mult).then_inc(free, 1)

            ahead(G["bp"] + 3)
            ahead(G["bz"] + 1)
            for w in range(4):
                bank, free = take(dve, ("pool", w))
                hi_count[0] += 1
                dve.wait_ge(S("t_hi"), hi_count[0])
                dve.tensor_tensor(z_lo[:, 2 * w:2 * w + 2, :], bank[:, :].rearrange("p (k s) -> p k s", k=2),
                                  z_hi[:, 2 * w:2 * w + 2, :].bitcast(F32), ALU.subtract).then_inc(free, 1)
            ahead(G["bz"] + 3)
            ahead(G["poolw"])
            dve.wait_ge(S("ld_pool"), 16)
            for n_ in range(2):
                c = slice(n_ * 512, (n_ + 1) * 512)
                for t in range(TT):
                    bank, free = take(dve, ("pooled", n_, t))
                    dve.tensor_tensor(au[:, t, c], bank[:, :], pool_row[:, 0, c], ALU.add).then_inc(free, 1)
                    freed(dve, ("pooled", n_, t))
                    link(dve.tensor_tensor(au[:, t, c], au[:, t, c], pool_row[:, 1, c], ALU.mult))
                    freed(dve, (("bz", n_), t))
                    dve.tensor_tensor(au[:, t, c], au[:, t, c], az[:, t, c], ALU.mult).then_inc(S("yb"), 1)
            for n_ in range(2):
                ahead(G["gb"] + 2 + n_)
                for t in range(TT):
                    plain_lo(("yb", n_, t), z_hi, z_lo, 4 * n_, slice(t * P, (t + 1) * P))

            def merge(name, gate_name, done):
                for n_ in range(2):
                    ahead(G[name] + 2 * n_ + 1)
                    if name == "wc" and n_:
                        pass
                    c = slice(n_ * 512, (n_ + 1) * 512)
                    for t in range(TT):
                        bank, free = take(dve, ((name, n_), t))
                        freed(dve, ((gate_name, n_), t))
                        dve.tensor_tensor(tmp[:, t, :], bank[:, :], gate[:, t, c], ALU.mult).then_inc(free, 1)
                        freed(dve, ((name, n_), t))
                        dve.tensor_tensor(merged[:, t, c], merged[:, t, c], tmp[:, t, :], ALU.add).then_inc(S(done), 1)
                    if name == "wc":
                        if n_ == 0:
                            ahead(G[name] + 2)
                        for t in range(TT):
                            plain_lo(("merged", n_, t), x_hi, x_lo, 4 * n_, slice(t * P, (t + 1) * P))

            merge("wb", "gb", "merged_b")

            dve.wait_ge(S("merged_b"), 4)
            dve.memset(c_pad[:, :, 0:2], 0.0).then_inc(S("c_zero"), 1)
            for j in range(KB):
                g = G["cc"] + 2 * j
                s = j % 2
                ahead(g)
                bank, free = take(dve, ("cc", j, 0))
                dve.wait_ge(S("c_hc"), j + 1)
                dve.tensor_tensor(c_y[:, s, :], bank[:, SEQ:2 * SEQ], c_h[:, s, :], ALU.mult).then_inc(free, 1)
                freed(dve, ("cc", j, 0))
                link(dve.tensor_tensor(c_pad[:, s, 2:], c_y[:, s, :], rb2, ALU.mult))
                link(dve.tensor_scalar(c_y[:, s, :], c_pad[:, s, 0:SEQ], col("c3_w", 3 * j), col("c3_b", j),
                                       ALU.mult, ALU.add))
                for k in (1, 2):
                    link(dve.scalar_tensor_tensor(out=c_y[:, s, :], in0=c_pad[:, s, k:k + SEQ],
                                                  scalar=col("c3_w", 3 * j + k), in1=c_y[:, s, :],
                                                  op0=ALU.mult, op1=ALU.add))
                ahead(g + 1)
                bank, _ = take(dve, ("cc", j, 1))
                dve.tensor_tensor(c_b[:, s, :], bank[:, 0:SEQ], rb, ALU.mult)
                dve.tensor_tensor(c_z[:, s, :], bank[:, SEQ:2 * SEQ], rb, ALU.mult).then_inc(S("c_zr"), 1)
                dve.wait_ge(S("c_zr"), j + 1)
                link(dve.tensor_tensor(c_y[:, s, :], c_y[:, s, :], c_b[:, s, :], ALU.mult))
                dve.wait_ge(S("c_silu"), j + 1)
                dve.tensor_tensor(c_f[:, s, :], c_y[:, s, :], c_s[:, s, :], ALU.mult).then_inc(S("yc"), 1)
                dve.wait_ge(S("yc_hi"), j + 1)
                dve.tensor_tensor(z_lo[:, j, :], c_f[:, s, :], z_hi[:, j, :].bitcast(F32), ALU.subtract) \
                   .then_inc(S("yc_split"), 1)
            ahead(G["gc"] + 3)
            merge("wc", "gc", "merged")

            for n_ in range(2):
                ahead(G["wout"] + 2 * n_ + 1)
                for t in range(TT):
                    add_h((("wout", n_), t), n_, t)
            h_factor(6)
            dve.wait_ge(S("r_done"), 7)
            dve.wait_ge(S("ld_final"), 16)
            for t in range(TT):
                dve.scalar_tensor_tensor(out=av[:, t, :], in0=h[:, t, :], scalar=st2[:, 12 + t:13 + t], in1=final_row,
                                         op0=ALU.mult, op1=ALU.mult).then_inc(S("out_ready"), 1)


def bucket(dist):
    n = np.maximum(dist, 0)
    f = np.maximum(n, 1).astype(np.float32)
    large = 16 + (np.log(f / np.float32(16)) / np.float32(math.log(128 / 16)) * np.float32(16)).astype(np.int32)
    return np.where(n < 16, n, np.minimum(large, NBUCKET - 1))


def constants():
    onehot = np.zeros((NBUCKET, 384), np.float32)
    dist = np.arange(SEQ - 1, -1, -1)
    onehot[bucket(dist), np.arange(SEQ)] = 1.0
    pool = np.zeros((4, SEQ, SEQ), np.float32)
    for w, win in enumerate(WINDOWS):
        for s in range(SEQ):
            lo = max(0, s - win + 1)
            pool[w, lo:s + 1, s] = np.float32(1.0) / np.float32(s + 1 - lo)
            pool[w, s, s] -= 1.0
    pm = np.zeros((P, 4, 384), np.float32)
    for w in range(4):
        pm[:, w, 0:SEQ] = pool[w, 0:P, :]
        pm[:, w, SEQ:384] = pool[w, P:, P:]
    return onehot, pm


def kernel(**inputs):
    import concourse.bacc as bacc
    from concourse.bass_utils import run_bass_kernel_spmd

    a = {k: np.asarray(v) for k, v in inputs.items()}
    ws = np.empty((NPIECE, P, HALF), np.float32)

    def rows_cols(w, k0, nk, *cols):
        b = w[k0 * P:(k0 + nk) * P].reshape(nk, P, -1)
        parts = [b[:, :, c] for c in cols]
        return np.concatenate(parts, axis=2).transpose(1, 0, 2).reshape(P, -1)

    def chunks(name, w):
        for i in range(w.shape[1] // 512):
            for k in range(2):
                ws[G[name] + 2 * i + k] = rows_cols(w, 4 * k, 4, slice(i * 512, (i + 1) * 512))

    pw1 = a["conv_w_pw1"][0]
    for f in range(KB):
        ws[G["pw1"] + f] = rows_cols(pw1, 0, KB, slice(f * P, (f + 1) * P), slice(D + f * P, D + (f + 1) * P))
    chunks("pw2", a["conv_w_pw2"][0])
    for l in range(2):
        ws[G[f"proj{l}"]] = rows_cols(a["ple_w_proj"][l], 0, 2, slice(0, D))
        chunks(f"ple{l}", a["ple_w_gate"][l])
        g0 = G[f"ffn{l}"]
        both = np.stack([a["ffn_w_gate"][l].reshape(D, GU, 256), a["ffn_w_up"][l].reshape(D, GU, 256)], 2)             .reshape(D, GU * 512)
        for i in range(GU):
            for k in range(2):
                ws[g0 + gu_at(i) + k] = rows_cols(both, 4 * k, 4, slice(i * 512, (i + 1) * 512))
            at = down_at(i // 2) + i % 2 if i < 10 else 32
            ws[g0 + at] = rows_cols(a["ffn_w_down"][l], 2 * i, 2, slice(0, D))
    qkv = a["attn_w_qkv"][0]
    order = [m * D + hg * 512 for hg in range(2) for m in range(3)]
    for i, c in enumerate(order):
        for k in range(2):
            ws[G["qkv"] + 2 * i + k] = rows_cols(qkv, 4 * k, 4, slice(c, c + 512))
    chunks("wo", a["attn_w_o"][0])
    w_in = a["w_in_2"][0]
    for name, i in [("au", 0), ("av", 1), ("az", 2), ("bp", 3), ("bz", 4), ("ga", 9), ("gb", 10), ("gc", 11)]:
        chunks(name, w_in[:, i * D:(i + 1) * D])
    for j in range(KB):
        for k, (one, two) in enumerate([(5, 7), (6, 8)]):
            ws[G["cc"] + 2 * j + k] = rows_cols(w_in, 0, KB, slice(one * D + j * P, one * D + (j + 1) * P),
                                                slice(two * D + j * P, two * D + (j + 1) * P))
    ws[G["poolw"]] = a["pool_w_2"][0].reshape(4, 2, P, 256).transpose(2, 0, 1, 3).reshape(P, HALF)
    chunks("wa", a["w_branch_a_2"][0])
    chunks("wb", a["w_branch_b_2"][0])
    chunks("wc", a["w_branch_c_2"][0])
    chunks("wout", a["w_out_2"][0])

    par = np.zeros((P, PCOLS), np.float32)

    def features(name, v):
        v = v.reshape(-1, P).T
        par[:, PCOL[name]:PCOL[name] + v.shape[1]] = v

    features("conv_g", a["conv_norm_g"][0])
    features("b_a", a["conv_b_pw1"][0, :D])
    features("b_g", a["conv_b_pw1"][0, D:])
    features("dw_b", a["conv_dw_b"][0])
    features("ln_g", a["conv_ln_g"][0])
    features("ln_b", a["conv_ln_b"][0])
    for l in range(2):
        features(f"ffn_g{l}", a["ffn_norm_g"][l])
        features(f"ple_g{l}", a["ple_norm_g"][l])
    features("attn_g", a["attn_norm_g"][0])
    features("norm_g2", a["norm_g_2"][0])
    features("c3_b", a["conv_b_2"][0])
    features("q_g", np.tile(a["attn_q_norm_g"][0], 2))
    features("k_g", np.tile(a["attn_k_norm_g"][0], 2))
    features("sub_g", a["attn_sub_norm_g"][0])
    features("sgu_b", a["sgu_b_2"][0])
    par[:, PCOL["dw_w"]:PCOL["dw_w"] + KB * TAPS] =         a["conv_dw_w"][0].reshape(TAPS, KB, P).transpose(2, 1, 0).reshape(P, KB * TAPS)
    par[:, PCOL["c3_w"]:PCOL["c3_w"] + 24] = a["conv_w_2"][0].reshape(3, KB, P).transpose(2, 1, 0).reshape(P, 24)

    onehot, pool_m = constants()
    x = a["x"][0]
    arrays = {
        "ws": ws, "x_tok": x, "x_feat": x.T.reshape(KB, P, SEQ).transpose(1, 0, 2),
        "p_feat": a["p"][:, 0].transpose(0, 2, 1).reshape(2, 2, P, SEQ).transpose(0, 2, 1, 3),
        "par": par,
        "rows": np.concatenate([a["conv_b_pw2"], a["sgu_ln_g_2"], a["sgu_ln_b_2"], a["pool_b_2"], a["pool_scale_2"],
                                a["final_g_2"][None]]),
        "lam_rows": np.concatenate([a["attn_lambda_q1"], a["attn_lambda_k1"], a["attn_lambda_q2"],
                                    a["attn_lambda_k2"]]),
        "rel": a["rel_bias"], "onehot": onehot, "sgu_w": a["sgu_w_2"][0].transpose(2, 0, 1), "pool_m": pool_m,
    }
    arrays = {f"in_{k}": np.ascontiguousarray(v) for k, v in arrays.items()}
    nc = bacc.Bacc("TRN2", target_bir_lowering=False, num_devices=1)
    args = [nc.dram_tensor(k, v.shape, F32, kind="ExternalInput").ap() for k, v in arrays.items()]
    toep = nc.dram_tensor("toep", (HEADS, P, 384), F32).ap()
    out = nc.dram_tensor("out_0", (SEQ, D), F32, kind="ExternalOutput").ap()
    build(nc, *args, toep, out)
    r = run_bass_kernel_spmd(nc, [arrays], core_ids=[0])
    return r.results[0]["out_0"].reshape(1, SEQ, D)
```

```python
import math
from contextlib import ExitStack

import numpy as np

import concourse.bass as bass
from concourse import mybir

F32 = mybir.dt.float32
F32R = mybir.dt.float32r
I32 = mybir.dt.int32
ALU = mybir.AluOpType
ACT = mybir.ActivationFunctionType
AX = mybir.AxisListType.X

P = 128
SEQ, D = 256, 1024
TT = SEQ // P
KB = D // P
DFF = 2816
PLE = 256
TAPS = 31
HEADS = 8
HD = 64
NBUCKET = 32
EPS = 1e-6
LN_EPS_2 = 1e-5
LAMBDA_INIT = 0.8 - 0.6 * math.exp(-0.3)
NEG = -1e30
WINDOWS = (2, 4, 8, 16)
HALF = 2048
RAW, SPLIT = 4, 3
GU = DFF // 256

STREAM = [("proj0", 1), ("pw1", 8), ("pw2", 4), ("ffn0", 33), ("ple0", 4), ("qkv", 12), ("proj1", 1),
          ("wo", 4), ("ffn1", 33), ("ple1", 4), ("av", 4), ("au", 4), ("az", 4), ("ga", 4), ("wa", 4),
          ("bp", 4), ("bz", 4), ("poolw", 1), ("gb", 4), ("wb", 4), ("cc", 16), ("gc", 4), ("wc", 4),
          ("wout", 4)]
G, NPIECE = {}, 0
for _name, _n in STREAM:
    G[_name] = NPIECE
    NPIECE += _n


def gu_at(i):
    return 0 if i == 0 else 2 + 6 * ((i - 1) // 2) + 2 * ((i - 1) % 2)


def down_at(q):
    return 2 + 6 * q + 4


PCOL, PCOLS = {}, 0
for _name, _n in [("conv_g", 8), ("b_a", 8), ("b_g", 8), ("dw_b", 8), ("ln_g", 8), ("ln_b", 8), ("ffn_g0", 8),
                  ("ffn_g1", 8), ("ple_g0", 8), ("ple_g1", 8), ("attn_g", 8), ("norm_g2", 8), ("c3_w", 24),
                  ("c3_b", 8), ("q_g", 1), ("k_g", 1), ("sub_g", 1), ("sgu_b", 8), ("dw_w", 8 * TAPS)]:
    PCOL[_name] = PCOLS
    PCOLS += _n


CONV_PE = 4
PADDED = TAPS - 1 + SEQ
TAP_GROUPS = [(0, 7), (7, 6), (13, 6), (19, 6), (25, 6)]


def build(nc, ws, x_tok, p_feat, par, rows, lam_rows, rel, onehot, sgu_w, pool_m, toep, out):
    ctx = ExitStack()
    with ctx:
        def sb(name, shape, dt=F32):
            return ctx.enter_context(nc.sbuf_tensor(name, shape, dt))

        def sem(name):
            return ctx.enter_context(nc.semaphore(name))

        raw = sb("raw", [P, RAW, HALF])
        w_hi = sb("w_hi", [P, SPLIT, HALF], F32R)
        w_lo = sb("w_lo", [P, SPLIT, HALF], F32R)
        h = sb("h", [P, TT, D])
        x_hi = sb("x_hi", [P, KB, SEQ], F32R)
        x_lo = sb("x_lo", [P, KB, SEQ], F32R)
        z_hi = sb("z_hi", [P, KB, SEQ], F32R)
        z_lo = sb("z_lo", [P, KB, SEQ], F32R)
        prm = sb("prm", [P, PCOLS])
        ident = sb("ident", [P, P])
        ones = sb("ones", [P, P])
        st = sb("st", [P, 96])
        st2 = sb("st2", [P, 64])
        NA = 17664
        arena = sb("arena", [P, NA])
        arena_at = nc.sbuf_base - 4 * NA
        banks = [ctx.enter_context(nc.psum_tensor(f"bank{b}", [P, 512], F32)) for b in range(8)]

        def view(off, *dims):
            n = int(np.prod(dims))
            assert off + n <= NA
            v = arena[:, off:off + n]
            if len(dims) == 1:
                return v
            names = "abc"[:len(dims)]
            return v.rearrange(f"p ({' '.join(names)}) -> p {' '.join(names)}",
                               **{c: d for c, d in zip(names, dims)})

        v_f = view(0, KB, SEQ)
        x_s = view(4336, TT, D)
        inv_d = view(11760, P)
        diag_hi = nc.alloc_sbuf_tensor_at("diag_hi", [P, 2, 7, P], F32R, offset=arena_at + 4 * 12032)
        diag_lo = nc.alloc_sbuf_tensor_at("diag_lo", [P, 2, 7, P], F32R, offset=arena_at + 4 * (12032 + 1792))
        taps_hi = view(9968, KB - CONV_PE, TAPS)
        taps_lo = view(10104, KB - CONV_PE, TAPS)
        u_pad = view(2048, KB, PADDED)
        y = view(4336, KB, SEQ)
        sq = view(6384, KB, SEQ)
        sq_x = view(6384, TT, D)
        row_b2 = view(8432, D)
        p_t0 = view(9456, 2, SEQ)
        sig = view(10480, 2, SEQ)
        wide = view(10992, 4, SEQ)
        pp = view(15616, TT, D)
        p_t1 = view(15616, 2, SEQ)
        stage = view(0, 2, 512)
        silu_t = view(1024, 2, 256)
        hid = view(1536, 2, 256)
        gate_t = view(2048, 2, 512)
        prod_t = view(3072, 2, 512)
        junk = view(4096, D)
        wt = view(1024, 2, 384)
        sq_o = view(1792, 2, P)
        oo = view(2048, TT, D)
        rec = view(4864, HEADS, 4)
        qk_t = arena[:, 5120:7168].rearrange("p (i t c) -> p i t c", i=2, t=TT)
        sq_t = view(0, TT, 512)
        qk_v, qk_tmp = view(7168, 16), view(7184, 16)
        vv = view(7680, TT, D)
        q_f = view(9728, 4, SEQ)
        k_f = view(10752, 4, SEQ)
        toep_t = view(11776, HEADS, 384)
        lg = [view(4096, 768), view(14848, 768)]
        w_f = [view(16128 + 384 * i, 384) for i in range(4)] + [view(5120 + 384 * i, 384) for i in range(4)]
        lam_t = view(14848, 4, HD)
        rel_t = arena[0:NBUCKET, 15104:15104 + HEADS]
        onehot_t = arena[0:NBUCKET, 15112:15112 + 384]
        bias_row = arena[0:HEADS, 9728:9728 + 384]
        av = view(2048, TT, D)
        au = view(4096, TT, D)
        az = view(6144, TT, D)
        gate = view(8192, TT, D)
        merged = view(10240, TT, D)
        ln_row = view(12288, 2, D)
        pool_row = view(12288, 2, D)
        sgu_t = view(14336, HEADS, P)
        final_row = view(14336, D)
        pm = view(15360, 4, 384)
        junk_v = view(10240, TT, D)
        junk_f = view(8192, D)
        tmp = view(2048, TT, 512)
        c_h = view(2048, 2, SEQ)
        c_pad = view(2560, 2, SEQ + 2)
        c_y = view(3076, 2, SEQ)
        c_b = view(3588, 2, SEQ)
        c_z = view(4100, 2, SEQ)
        c_s = view(4612, 2, SEQ)
        c_f = view(5124, 2, SEQ)
        rb = view(16896, SEQ)
        rb2 = view(17152, SEQ)
        diag = view(17408, TT, P)

        def flat(z):
            return z[:, :, :].rearrange("p k s -> p (k s)")

        raw_loaded = [sem(f"raw_loaded{s}") for s in range(RAW)]
        hi_done, lo_done, w_used = sem("hi_done"), sem("lo_done"), sem("w_used")
        pe_filled = sem("pe_filled")
        bank_free = [sem(f"bank_free{b}") for b in range(8)]
        dve_step, act_step, pool_step = sem("dve_step"), sem("act_step"), sem("pool_step")
        ev = {}

        def S(name):
            if name not in ev:
                ev[name] = sem(name)
            return ev[name]

        def col(name, i=0, n=1):
            return prm[:, PCOL[name] + i:PCOL[name] + i + n]

        filled = {}
        jobs = {}
        job_no = {}

        block = ctx.enter_context(nc.Block())

        @block.sync
        def _(sp):
            for t in range(TT):
                sp.dma_start(h[:, t, :], x_tok[t * P:(t + 1) * P, :]).then_inc(S(f"ld_h{t}"), 16)
            for g in range(NPIECE):
                if g >= RAW:
                    sp.wait_ge(lo_done, g - RAW + 1)
                sp.dma_start(raw[:, g % RAW, :], ws[g]).then_inc(raw_loaded[g % RAW], 16)
            for t in range(TT):
                sp.wait_ge(S("out_ready"), t + 1)
                sp.dma_start(out[t * P:(t + 1) * P, :], av[:, t, :]).then_inc(S("stored"), 16)
            sp.wait_ge(S("stored"), 16 * TT)

        def bcast(src, i, n=1):
            return bass.AP(src.tensor, i * D, [[0, P], [D, n], [1, D]]) if n > 1 else \
                bass.AP(src.tensor, i * D, [[0, P], [1, D]])

        @block.tensor
        def _(pe):
            released = [None] * 8
            frees = [0] * 8
            count = {"filled": 0, "gain": 0}

            def begin(b):
                if released[b]:
                    pe.wait_ge(*released[b])

            def end(key, b, ins, piece=None, release=None):
                if release is None:
                    frees[b] += 1
                    release = (bank_free[b], frees[b])
                if piece is None:
                    ins.then_inc(pe_filled, 1)
                    count["filled"] += 1
                    filled[key] = (pe_filled, count["filled"], b, release)
                else:
                    ins.then_inc(w_used, 1)
                    filled[key] = (w_used, piece + 1, b, release)
                released[b] = release

            def mm3(dst, s_hi, s_lo, m_hi, m_lo, first, last):
                pe.matmul(dst, s_hi, m_hi, start=first, stop=False)
                pe.matmul(dst, s_hi, m_lo, start=False, stop=False)
                return pe.matmul(dst, s_lo, m_hi, start=False, stop=last)

            def tok(ap, k, t):
                return ap[:, k, t * P:(t + 1) * P]

            def wait_job(*keys):
                for key in keys:
                    pe.wait_ge(*jobs[key])

            def token_chunk(key, g0, a_hi, a_lo, ready=None, between=None, release=None, hooks={}):
                for a in range(2):
                    if ready:
                        ready(a)
                    pe.wait_ge(lo_done, g0 + a + 1)
                    s = (g0 + a) % SPLIT
                    for t in range(TT):
                        b = t
                        if a == 0:
                            begin(b)
                        for k in range(4):
                            c = slice(k * 512, (k + 1) * 512)
                            ins = mm3(banks[b][:, :], tok(a_hi, 4 * a + k, t), tok(a_lo, 4 * a + k, t),
                                      w_hi[:, s, c], w_lo[:, s, c], a == 0 and k == 0, a == 1 and k == 3)
                        if a == 1:
                            end((key, t), b, ins, g0 + 1 if t == 1 else None, release(t) if release else None)
                        elif t == 1:
                            ins.then_inc(w_used, 1)
                        for step in hooks.get((a, t), ()):
                            step()
                    if a == 0 and between:
                        between()

            def transpose_job(key, src, wait, gain):
                pe.wait_ge(*wait)
                n = job_no[key] = len(job_no)
                b = 2 + n % 2
                begin(b)
                for k in range(4):
                    ins = pe.transpose(banks[b][:, k * P:(k + 1) * P], src[:, k * P:(k + 1) * P], ident[:, :])
                end(("tr",) + key, b, ins)
                if gain:
                    count["gain"] += 1
                    jobs[key] = (S("x_split"), count["gain"])
                else:
                    jobs[key] = released[b]

            def h_release(m, n):
                return lambda t: (S("h_done"), 4 * m + 2 * n + t + 1)

            def h_jobs(m, n):
                for t in range(TT):
                    transpose_job((m, n, t), h[:, t, n * 512:(n + 1) * 512], (S("h_done"), 4 * m + 2 * n + t + 1), True)

            def ready_from(m):
                def ready(a):
                    wait_job((m, a, 0), (m, a, 1))
                return ready

            def projection(layer, g, bank):
                pe.wait_ge(S("p_split"), layer + 1)
                pe.wait_ge(lo_done, g + 1)
                for t in range(TT):
                    for n in range(2):
                        b = bank[2 * t + n]
                        begin(b)
                        for k in range(2):
                            c = slice(k * D + n * 512, k * D + (n + 1) * 512)
                            ins = mm3(banks[b][:, :], tok(z_hi, k, t), tok(z_lo, k, t),
                                      w_hi[:, g % SPLIT, c], w_lo[:, g % SPLIT, c], k == 0, k == 1)
                        end(("proj", layer, t, n), b, ins, g if t == 1 and n == 1 else None)

            def feature_piece(key, g, b, release=None):
                pe.wait_ge(lo_done, g + 1)
                begin(b)
                for c in range(2):
                    for k in range(KB):
                        w = slice(k * 256 + c * P, k * 256 + (c + 1) * P)
                        ins = mm3(banks[b][:, c * SEQ:(c + 1) * SEQ], w_hi[:, g % SPLIT, w], w_lo[:, g % SPLIT, w],
                                  x_hi[:, k, :], x_lo[:, k, :], k == 0, k == KB - 1)
                end(key, b, ins, g, release)

            def ffn(layer, m):
                g0 = G[f"ffn{layer}"]

                def hidden_job(i):
                    n = job_no[("hid", layer, i)] = len(job_no)
                    b = 2 + n % 2
                    begin(b)
                    for t in range(TT):
                        pe.wait_ge(S("hidden"), 2 * (GU * layer + i) + t + 1)
                        for k in range(2):
                            ins = pe.transpose(banks[b][:, k * SEQ + t * P:k * SEQ + (t + 1) * P],
                                               hid[:, t, k * P:(k + 1) * P], ident[:, :])
                    end(("tr", "hid", layer, i), b, ins)
                    jobs[("hid", layer, i)] = released[b]

                def down(q):
                    for a in range(2 if q < 5 else 1):
                        i = 2 * q + a
                        g = g0 + (down_at(q) + a if q < 5 else 32)
                        wait_job(("hid", layer, i))
                        pe.wait_ge(lo_done, g + 1)
                        for n in range(2):
                            for t in range(TT):
                                b = 4 + 2 * n + t
                                if i == 0:
                                    begin(b)
                                for k in range(2):
                                    c = slice(k * D + n * 512, k * D + (n + 1) * 512)
                                    zk = (2 * i + k) % KB
                                    ins = mm3(banks[b][:, :], tok(z_hi, zk, t), tok(z_lo, zk, t),
                                              w_hi[:, g % SPLIT, c], w_lo[:, g % SPLIT, c],
                                              i == 0 and k == 0, i == GU - 1 and k == 1)
                                if i == GU - 1:
                                    end(("ffn", layer, n, t), b, ins, g if n == 1 and t == 1 else None,
                                        (S("h_done"), 4 * (m + 1) + 2 * n + t + 1))
                                elif n == 1 and t == 1:
                                    ins.then_inc(w_used, 1)
                        if q == 4 and a == 0:
                            hidden_job(GU - 1)

                for i in range(GU):
                    token_chunk(("gu", layer, i), g0 + gu_at(i), x_hi, x_lo, ready=ready_from(m) if i == 0 else None,
                                release=lambda t: (S("hidden"), 2 * (GU * layer + i) + t + 1),
                                between=(lambda: hidden_job(i - 1)) if i else None)
                    if i >= 2 and i % 2 == 0:
                        down(i // 2 - 1)
                down(5)
                h_jobs(m + 1, 0)
                h_jobs(m + 1, 1)

            def ple(layer, m):
                g0 = G[f"ple{layer}"]
                token_chunk(("ple", layer, 0), g0, x_hi, x_lo, ready=ready_from(m))
                token_chunk(("ple", layer, 1), g0 + 2, x_hi, x_lo, between=lambda: h_jobs(m + 1, 0))
                h_jobs(m + 1, 1)

            pe.wait_ge(S("consts"), 4)
            for n in range(2):
                for t in range(TT):
                    transpose_job(("x", n, t), x_s[:, t, n * 512:(n + 1) * 512], (S("x_scaled"), t + 1), True)
            projection(0, G["proj0"], (4, 5, 6, 7))

            def pw1(f):
                if f == 0:
                    wait_job(("x", 0, 0), ("x", 0, 1), ("x", 1, 0), ("x", 1, 1))
                feature_piece(("pw1", f), G["pw1"] + f, (0, 1, 4, 7)[f % 4], (S("u"), f + 1))

            def conv_taps(f):
                i, b = f - CONV_PE, (2, 3, 5, 6)[f - CONV_PE]
                pe.wait_ge(S("u_split"), i + 1)
                begin(b)
                for q, (t0, nt) in enumerate(TAP_GROUPS):
                    gr = len(TAP_GROUPS) * i + q
                    pe.wait_ge(S("diag_built"), 2 * gr + 2)
                    for j in range(nt):
                        w = slice(i * PADDED + t0 + j, i * PADDED + t0 + j + SEQ)
                        ins = mm3(banks[b][:, 0:SEQ], diag_hi[:, gr % 2, j, :], diag_lo[:, gr % 2, j, :],
                                  flat(z_hi)[:, w], flat(z_lo)[:, w], q == 0 and j == 0, t0 + j == TAPS - 1)
                    if t0 + nt < TAPS:
                        ins.then_inc(S("diag_used"), 1)
                end(("conv", f), b, ins, release=(S("conv_pe"), i + 1))

            def mean_of(f, first=False, last=False):
                if first:
                    begin(0)
                pe.wait_ge(S("conv_pe" if f >= CONV_PE else "conv"), f % CONV_PE + 1)
                ins = pe.matmul(banks[0][:, 0:SEQ], inv_d, y[:, f, :], start=first, stop=last)
                if last:
                    end("mean", 0, ins, release=(S("centred"), 2))

            for f in range(6):
                pw1(f)
            conv_taps(4)
            pw1(6)
            conv_taps(5)
            pw1(7)
            conv_taps(6)
            for f in (0, 1, 4, 5):
                mean_of(f, first=f == 0)
            conv_taps(7)
            for f in (6, 2, 3, 7):
                mean_of(f, last=f == 7)
            begin(7)
            for f in range(KB):
                pe.wait_ge(S("y_sq"), f // 2 + 1)
                ins = pe.matmul(banks[7][:, 0:SEQ], inv_d, sq[:, f, :], start=f == 0, stop=f == KB - 1)
            end("var", 7, ins, release=(S("y_r"), 1))

            def z_ready(a):
                pe.wait_ge(S("v_split"), a + 1)
            token_chunk(("pw2", 0), G["pw2"], z_hi, z_lo, ready=z_ready, release=h_release(0, 0))
            token_chunk(("pw2", 1), G["pw2"] + 2, z_hi, z_lo, between=lambda: h_jobs(0, 0), release=h_release(0, 1))
            h_jobs(0, 1)
            ffn(0, 0)
            pe.wait_ge(S("ld_attn"), 16 * 3)
            begin(4)
            end("bias", 4, pe.matmul(banks[4][0:HEADS, 0:384], rel_t, onehot_t, start=True, stop=True))
            ple(0, 1)

            def logits(hd):
                def go():
                    j, b0 = hd % 4, 4 + 2 * (hd % 2)
                    for c in range(2):
                        begin(b0 + c)
                        r = slice(c * HD, (c + 1) * HD)
                        pe.matmul(banks[b0 + c][:, 0:SEQ], q_f[r, j, P:SEQ], k_f[r, j, :], start=True, stop=True)
                        ins = pe.matmul(banks[b0 + c][:, SEQ:384], q_f[r, j, 0:P], k_f[r, j, 0:P], start=True, stop=True)
                        end(("lg", hd, c), b0 + c, ins, release=(S("lg_read"), 2 * hd + c + 1))
                return go

            def group_logits(hd):
                def go():
                    hg = hd // 4
                    wait_job(("qk", hg, 0, 0), ("qk", hg, 0, 1), ("qk", hg, 1, 0), ("qk", hg, 1, 1))
                    logits(hd)()
                return go

            def weights(hd):
                def go():
                    pe.wait_ge(S("w_mix"), hd + 1)
                    n = job_no[("w", hd)] = len(job_no)
                    b = 2 + n % 2
                    begin(b)
                    for k in range(3):
                        ins = pe.transpose(banks[b][:, k * P:(k + 1) * P], wt[:, hd % 2, k * P:(k + 1) * P], ident[:, :])
                    end(("tr", "w", hd), b, ins, release=(S("w_copied"), hd + 1))
                return go

            def values(pair):
                def go():
                    b = pair % 2
                    begin(b)
                    pe.wait_ge(S("v_copied"), 2 * (pair // 2) + 2)
                    pe.wait_ge(S("w_copied"), 2 * pair + 2)
                    for i in range(2):
                        hd = 2 * pair + i
                        w, d = w_f[hd], slice(hd * P, (hd + 1) * P)
                        t0, t1 = banks[b][:, i * P:(i + 1) * P], banks[b][:, (2 + i) * P:(3 + i) * P]
                        pe.matmul(t1, w[:, 0:P], vv[:, 0, d], start=True, stop=False)
                        pe.matmul(t1, w[:, P:2 * P], vv[:, 1, d], start=False, stop=True)
                        ins = pe.matmul(t0, w[:, 2 * P:3 * P], vv[:, 0, d], start=True, stop=True)
                    end(("pv", pair), b, ins)
                return go

            def qk_jobs(hg, i):
                def go():
                    for t in range(TT):
                        transpose_job(("qk", hg, i, t), qk_t[:, i, t, :], (S("qk_normed"), 4 * hg + 2 * i + t + 1), False)
                return go

            g = G["qkv"]
            token_chunk(("q", 0), g, x_hi, x_lo, ready=ready_from(2))
            token_chunk(("k", 0), g + 2, x_hi, x_lo)
            token_chunk(("q", 1), g + 4, x_hi, x_lo,
                        hooks={(0, 1): [qk_jobs(0, 0)], (1, 0): [qk_jobs(0, 1)], (1, 1): [group_logits(0), logits(1)]})
            token_chunk(("k", 1), g + 6, x_hi, x_lo,
                        hooks={(0, 0): [logits(2)], (0, 1): [weights(0)], (1, 0): [logits(3)]})
            token_chunk(("v", 0), g + 8, x_hi, x_lo, release=lambda t: (S("v_copied"), t + 1),
                        hooks={(0, 0): [weights(1)], (0, 1): [qk_jobs(1, 0)], (1, 0): [weights(2)]})
            token_chunk(("v", 1), g + 10, x_hi, x_lo, release=lambda t: (S("v_copied"), t + 3),
                        hooks={(0, 0): [qk_jobs(1, 1)], (0, 1): [group_logits(4), logits(5)],
                               (1, 0): [weights(3), logits(6)], (1, 1): [weights(4), logits(7)]})
            for step in (values(0), weights(5), values(1), weights(6), values(2), weights(7), values(3)):
                step()
            projection(1, G["proj1"], (4, 5, 6, 7))
            for n in range(2):
                for t in range(TT):
                    transpose_job(("o", n, t), oo[:, t, n * 512:(n + 1) * 512], (S("o_normed"), t + 1), True)

            def o_ready(a):
                wait_job(("o", a, 0), ("o", a, 1))
            token_chunk(("wo", 0), G["wo"], z_hi, z_lo, ready=o_ready, release=h_release(3, 0))
            token_chunk(("wo", 1), G["wo"] + 2, z_hi, z_lo, between=lambda: h_jobs(3, 0), release=h_release(3, 1))
            h_jobs(3, 1)
            ffn(1, 3)
            ple(1, 4)

            for name in ("av", "au"):
                for n in range(2):
                    token_chunk((name, n), G[name] + 2 * n, x_hi, x_lo,
                                ready=ready_from(5) if name == "av" and n == 0 else None)
            begin(4)
            pe.wait_ge(S("diag"), 2)
            for t in range(TT):
                ins = pe.matmul(banks[4][:, t * P:(t + 1) * P], ones[:, :], diag[:, t, :], start=True, stop=True)
            end("r_row", 4, ins)
            token_chunk(("az", 0), G["az"], x_hi, x_lo)
            pe.wait_ge(S("sgu_masked"), 1)
            pe.wait_ge(S("sgu_ready"), 2)
            for t in range(TT):
                for q in range(2):
                    b = 4 + 2 * t + q
                    begin(b)
                    for j in range(4):
                        gi = 4 * q + j
                        ins = pe.matmul(banks[b][:, j * P:(j + 1) * P], sgu_t[:, gi, :],
                                        av[:, t, gi * P:(gi + 1) * P], start=True, stop=True)
                    end(("mixed", t, q), b, ins)
            token_chunk(("az", 1), G["az"] + 2, x_hi, x_lo)

            def y_jobs(name, src, n):
                def go():
                    for t in range(TT):
                        transpose_job((name, n, t), src[:, t, n * 512:(n + 1) * 512], (S(name), 2 * n + t + 1), False)
                return go

            def job_ready(name):
                def ready(a):
                    wait_job((name, a, 0), (name, a, 1))
                return ready

            token_chunk(("ga", 0), G["ga"], x_hi, x_lo)
            token_chunk(("ga", 1), G["ga"] + 2, x_hi, x_lo, between=y_jobs("ya", au, 0))
            y_jobs("ya", au, 1)()
            for n in range(2):
                token_chunk(("wa", n), G["wa"] + 2 * n, z_hi, z_lo, ready=job_ready("ya") if n == 0 else None)

            for n in range(2):
                token_chunk(("bp", n), G["bp"] + 2 * n, x_hi, x_lo)
            token_chunk(("bz", 0), G["bz"], x_hi, x_lo)
            for n in range(2):
                for t in range(TT):
                    pe.wait_ge(*filled[(("bp", n), t)][3])
            pe.wait_ge(S("ld_pm"), 16)
            for f in range(KB):
                b = 4 + f // 2
                if f % 2 == 0:
                    begin(b)
                w = f // 2
                dst = banks[b][:, (f % 2) * SEQ:(f % 2 + 1) * SEQ]
                fs = slice(f * P, (f + 1) * P)
                pe.matmul(dst, av[:, 0, fs], pm[:, w, 0:SEQ], start=True, stop=False)
                ins = pe.matmul(dst[:, P:SEQ], av[:, 1, fs], pm[:, w, SEQ:384], start=False, stop=True)
                if f % 2:
                    end(("pool", w), b, ins)
            token_chunk(("bz", 1), G["bz"] + 2, x_hi, x_lo)
            g = G["poolw"]
            pe.wait_ge(lo_done, g + 1)
            for w in range(4):
                pe.wait_ge(*filled[("pool", w)][3])
            for n in range(2):
                for t in range(TT):
                    b = (0, 1)[t]
                    begin(b)
                    for w in (2 * n, 2 * n + 1):
                        for k in range(2):
                            c = slice((2 * w + k) * 256, (2 * w + k + 1) * 256)
                            ins = mm3(banks[b][:, (w % 2) * 256:(w % 2 + 1) * 256], tok(z_hi, 2 * w + k, t),
                                      tok(z_lo, 2 * w + k, t), w_hi[:, g % SPLIT, c], w_lo[:, g % SPLIT, c],
                                      k == 0, k == 1)
                    end(("pooled", n, t), b, ins, g if n == 1 and t == 1 else None)
            token_chunk(("gb", 0), G["gb"], x_hi, x_lo)
            token_chunk(("gb", 1), G["gb"] + 2, x_hi, x_lo, between=y_jobs("yb", au, 0))
            y_jobs("yb", au, 1)()
            for n in range(2):
                token_chunk(("wb", n), G["wb"] + 2 * n, z_hi, z_lo, ready=job_ready("yb") if n == 0 else None)

            for j in range(KB):
                for a in range(2):
                    feature_piece(("cc", j, a), G["cc"] + 2 * j + a, 4 + (2 * j + a) % 4,
                                  (S("c_zr"), j + 1) if a else None)
            for n in range(2):
                token_chunk(("gc", n), G["gc"] + 2 * n, x_hi, x_lo)

            def c_ready(a):
                pe.wait_ge(S("yc_split"), 4 * a + 4)
            token_chunk(("wc", 0), G["wc"], z_hi, z_lo, ready=c_ready)
            token_chunk(("wc", 1), G["wc"] + 2, z_hi, z_lo, between=y_jobs("merged", merged, 0))
            y_jobs("merged", merged, 1)()
            for n in range(2):
                token_chunk(("wout", n), G["wout"] + 2 * n, x_hi, x_lo, ready=job_ready("merged") if n == 0 else None,
                            release=h_release(6, n))

        def take(eng, key):
            s, v, b, _ = filled[key]
            eng.wait_ge(s, v)
            return banks[b], bank_free[b]

        def freed(eng, key):
            eng.wait_ge(*filled[key][3])

        @block.gpsimd
        def _(pool):
            n = [0]

            def link(ins):
                n[0] += 1
                ins.then_inc(pool_step, 1)
                pool.wait_ge(pool_step, n[0])

            pool.dma_start(row_b2, bcast(rows, 0)).then_inc(S("ld_b2"), 16)
            link(pool.memset(ident[:, :], 0.0))
            pool.affine_select(out=ident[:, :], in_=ident[:, :], compare_op=ALU.not_equal, fill=1.0, base=0,
                               pattern=[[-1, P]], channel_multiplier=1).then_inc(S("consts"), 1)
            pool.memset(ones[:, :], 1.0).then_inc(S("consts"), 1)
            pool.memset(inv_d, 1.0 / D).then_inc(S("consts"), 1)
            pool.memset(u_pad[:, :, 0:TAPS - 1], 0.0).then_inc(S("consts"), 1)
            pool.wait_ge(S("taps_split"), 1)
            for gr in range((KB - CONV_PE) * len(TAP_GROUPS)):
                i, (t0, nt) = gr // len(TAP_GROUPS), TAP_GROUPS[gr % len(TAP_GROUPS)]
                if gr >= 2:
                    f, q = divmod(gr - 2, len(TAP_GROUPS))
                    if q < len(TAP_GROUPS) - 1:
                        pool.wait_ge(S("diag_used"), (len(TAP_GROUPS) - 1) * f + q + 1)
                    else:
                        take(pool, ("conv", CONV_PE + f))
                for taps, dst in ((taps_hi, diag_hi), (taps_lo, diag_lo)):
                    pool.affine_select(out=dst[:, gr % 2, 0:nt, :],
                                       in_=taps[:, i, t0:t0 + nt].unsqueeze(2).to_broadcast([P, nt, P]),
                                       compare_op=ALU.is_equal, fill=0.0, base=0, pattern=[[0, nt], [1, P]],
                                       channel_multiplier=-1).then_inc(S("diag_built"), 1)
            pool.wait_ge(S("ld_b2"), 16)
            pool.wait_ge(S("x_scaled"), 2)
            for t in range(TT):
                pool.tensor_tensor(h[:, t, :], h[:, t, :], row_b2, ALU.add).then_inc(S("h_biased"), 1)

            pool.wait_ge(S("h_done"), 4)
            pool.dma_start(rel_t, rel).then_inc(S("ld_attn"), 16)
            pool.dma_start(onehot_t, onehot).then_inc(S("ld_attn"), 16)
            pool.dma_start(lam_t, bass.AP(lam_rows.tensor, 0, [[0, P], [HD, 4], [1, HD]])).then_inc(S("ld_attn"), 16)
            pool.wait_ge(S("bias_row"), 2)
            pool.dma_start(toep, bias_row.unsqueeze(1).to_broadcast([HEADS, P, 384])).then_inc(S("toep_out"), 16)
            pool.wait_ge(S("toep_out"), 16)
            pool.dma_start(toep_t[:, :, 0:SEQ], bass.AP(toep.tensor, P - 1, [[383, P], [P * 384, HEADS], [1, SEQ]])) \
                .then_inc(S("ld_toep"), 16)
            pool.dma_start(toep_t[:, :, SEQ:384], bass.AP(toep.tensor, 2 * P - 1, [[383, P], [P * 384, HEADS], [1, P]])) \
                .then_inc(S("ld_toep"), 16)
            pool.wait_ge(S("h_done"), 12)
            pool.dma_start(p_t1, p_feat[1]).then_inc(S("ld_p1"), 16)
            pool.wait_ge(S("h_done"), 16)
            pool.dma_start(ln_row, bcast(rows, 1, 2)).then_inc(S("ld_sgu"), 16)
            pool.dma_start(sgu_t, sgu_w).then_inc(S("ld_sgu"), 16)
            pool.wait_ge(S("ld_sgu"), 32)
            pool.memset(sgu_t[HD:P, :, 0:HD], 0.0).then_inc(S("sgu_masked"), 1)
            pool.wait_ge(S("h_done"), 24)
            pool.dma_start(pm, pool_m).then_inc(S("ld_pm"), 16)
            pool.wait_ge(S("sgu_ready"), 2)
            pool.dma_start(pool_row, bcast(rows, 3, 2)).then_inc(S("ld_pool"), 16)
            for t in range(TT):
                for q in range(2):
                    freed(pool, ("mixed", t, q))
            pool.dma_start(final_row, bcast(rows, 5)).then_inc(S("ld_final"), 16)

        @block.scalar
        def _(act):
            fed = [0]
            n = [0]

            def link(ins):
                n[0] += 1
                ins.then_inc(act_step, 1)
                act.wait_ge(act_step, n[0])

            def feed(to):
                while fed[0] <= min(to, NPIECE - 1):
                    g = fed[0]
                    act.wait_ge(raw_loaded[g % RAW], 16 * (g // RAW + 1))
                    if g >= SPLIT:
                        act.wait_ge(w_used, g - SPLIT + 1)
                    act.activation(w_hi[:, g % SPLIT, :], raw[:, g % RAW, :], ACT.Copy).then_inc(hi_done, 1)
                    fed[0] += 1

            def ahead(g):
                feed(g + SPLIT - 1)

            jn = [0]

            def split_hi(key, dst, k0, w):
                freed(act, ("tr",) + key)
                src = stage[:, job_no[key] % 2, :].rearrange("p (k c) -> p k c", k=4)
                act.activation(dst[:, k0:k0 + 4, w], src, ACT.Copy).then_inc(S("t_hi"), 1)

            def h_split(m, n):
                for t in range(TT):
                    split_hi((m, n, t), x_hi, 4 * n, slice(t * P, (t + 1) * P))

            def h_stats(m):
                for t in range(TT):
                    act.wait_ge(S("h_done"), 4 * m + 3 + t)
                    if t:
                        act.wait_ge(S("h_ss"), 2 * m + 1)
                    act.activation(junk if m < 6 else junk_f, h[:, t, :], ACT.Square,
                                   accum_out=st[:, 2 * m + t:2 * m + t + 1]).then_inc(S("h_ss"), 1)

            def plain_hi(key, dst, k0, w):
                bank, _ = take(act, ("tr",) + key)
                src = bank[:, :].rearrange("p (k c) -> p k c", k=4)
                act.activation(dst[:, k0:k0 + 4, w], src, ACT.Copy).then_inc(S("t_hi"), 1)

            def ffn(layer, m):
                g0 = G[f"ffn{layer}"]

                def hidden_hi(i):
                    bank, _ = take(act, ("tr", "hid", layer, i))
                    k0 = (2 * i) % KB
                    act.activation(z_hi[:, k0:k0 + 2, :], bank[:, :].rearrange("p (k s) -> p k s", k=2),
                                   ACT.Copy).then_inc(S("t_hi"), 1)

                for i in range(GU):
                    g = g0 + gu_at(i)
                    ahead(g)
                    if i:
                        hidden_hi(i - 1)
                    ahead(g + 1)
                    if i == 0:
                        act.wait_ge(S("r_done"), m + 1)
                    for t in range(TT):
                        bank, _ = take(act, (("gu", layer, i), t))
                        if i:
                            act.wait_ge(S("hidden"), 2 * (GU * layer + i - 1) + t + 1)
                        act.activation(silu_t[:, t, :], bank[:, 0:256], ACT.Silu,
                                       scale=st2[:, 2 * m + t:2 * m + t + 1]).then_inc(S("silu"), 1)
                    if i >= 2 and i % 2 == 0:
                        ahead(g0 + down_at(i // 2 - 1))
                        ahead(g0 + down_at(i // 2 - 1) + 1)
                hidden_hi(GU - 1)
                ahead(g0 + 32)
                h_split(m + 1, 0)
                h_split(m + 1, 1)
                h_stats(m + 1)

            gates = [0]

            def ple(layer, m):
                g0 = G[f"ple{layer}"]
                act.wait_ge(S("r_done"), m + 1)
                for n in range(2):
                    ahead(g0 + 2 * n)
                    if n:
                        h_split(m + 1, 0)
                    ahead(g0 + 2 * n + 1)
                    for t in range(TT):
                        bank, free = take(act, (("ple", layer, n), t))
                        if n:
                            act.wait_ge(S("gate_used"), 4 * layer + t + 1)
                        act.activation(gate_t[:, t, :], bank[:, :], ACT.Sigmoid,
                                       scale=st2[:, 2 * m + t:2 * m + t + 1]).then_inc(free, 1)
                h_split(m + 1, 1)
                h_stats(m + 1)

            def p_split(layer):
                act.wait_ge(S(f"ld_p{layer}"), 16)
                act.activation(z_hi[:, 0:2, :], p_t1 if layer else p_t0, ACT.Copy).then_inc(S("p_hi"), 1)

            def proj_copy(layer):
                for t in range(TT):
                    for n in range(2):
                        bank, free = take(act, ("proj", layer, t, n))
                        act.activation(pp[:, t, n * 512:(n + 1) * 512], bank[:, :], ACT.Copy).then_inc(free, 1)

            act.dma_start(prm[:, :], par).then_inc(S("ld_par"), 16)
            act.dma_start(p_t0, p_feat[0]).then_inc(S("ld_p0"), 16)
            for t in range(TT):
                act.wait_ge(S(f"ld_h{t}"), 16)
                act.activation(sq_x[:, t, :], h[:, t, :], ACT.Square, accum_out=st[:, 80 + t:81 + t]) \
                   .then_inc(S("x_ss"), 1)
            act.wait_ge(S("ld_par"), 16)
            taps = prm[:, PCOL["dw_w"] + CONV_PE * TAPS:PCOL["dw_w"] + KB * TAPS]
            act.activation(taps_hi.rearrange("p a b -> p (a b)").bitcast(F32R), taps, ACT.Copy).then_inc(S("taps_hi"), 1)
            act.wait_ge(S("x_r"), 1)
            for t in range(TT):
                act.activation(x_s[:, t, :], h[:, t, :], ACT.Copy, scale=st2[:, 48 + t:49 + t]).then_inc(S("x_scaled"), 1)
            p_split(0)
            feed(0)
            h_split("x", 0)
            feed(1)
            h_split("x", 1)
            feed(2)
            proj_copy(0)

            def u_high(f):
                act.wait_ge(S("u"), f + 1)
                w = slice((f - CONV_PE) * PADDED, (f - CONV_PE + 1) * PADDED)
                act.activation(flat(z_hi)[:, w], u_pad[:, f, :], ACT.Copy).then_inc(S("u_hi"), 1)

            def conv_out(f):
                bank, _ = take(act, ("conv", f))
                act.activation(y[:, f, :], bank[:, 0:SEQ], ACT.Identity, bias=col("dw_b", f)).then_inc(S("conv_pe"), 1)

            for f in range(KB):
                ahead(G["pw1"] + f)
                bank, _ = take(act, ("pw1", f))
                if f >= 2:
                    act.wait_ge(S("u"), f - 1)
                act.activation(sig[:, f % 2, :], bank[:, SEQ:2 * SEQ], ACT.Sigmoid, bias=col("b_g", f)).then_inc(S("sig"), 1)
                if f >= CONV_PE:
                    u_high(f)
                if f >= 6:
                    conv_out(f - 2)
            ahead(G["pw2"])
            conv_out(6)
            conv_out(7)
            for f in range(4):
                act.wait_ge(S("centred"), f // 2 + 1)
                act.activation(sq[:, 2 * f:2 * f + 2, :], y[:, 2 * f:2 * f + 2, :], ACT.Square).then_inc(S("y_sq"), 1)
            for a in range(2):
                for f in range(4 * a, 4 * a + 4):
                    act.wait_ge(S("scaled"), a + 1)
                    act.activation(v_f[:, f, :], y[:, f, :], ACT.Silu, scale=col("ln_g", f), bias=col("ln_b", f)) \
                       .then_inc(S("v_act"), 1)
            ahead(G["pw2"] + 2)
            h_split(0, 0)
            ahead(G["pw2"] + 3)
            h_split(0, 1)
            h_stats(0)
            ffn(0, 0)
            ple(0, 1)

            ahead(G["qkv"])
            act.wait_ge(S("lam_sum"), 1)
            act.activation(st[:, 90:92], st[:, 88:90], ACT.Exp).then_inc(S("lam_exp"), 1)
            p_split(1)
            act.wait_ge(S("r_done"), 3)
            act.wait_ge(S("attn_small"), 3)
            g = G["qkv"]

            def qk_evac(hg, i):
                for t in range(TT):
                    bank, free = take(act, (("qk"[i], hg), t))
                    if hg:
                        freed(act, ("tr", "qk", 0, i, t))
                    act.activation(qk_t[:, i, t, :], bank[:, :], ACT.Copy, scale=st2[:, 4 + t:5 + t]).then_inc(free, 1)
                for t in range(TT):
                    freed(act, (("qk"[i], hg), t))
                    if 2 * hg + i:
                        act.wait_ge(S("qk_ss"), 4 * hg + 2 * i + t - 1)
                    act.activation(sq_t[:, t, :], qk_t[:, i, t, :], ACT.Square).then_inc(S("qk_sq"), 1)

            def qk_features(hg, i):
                for t in range(TT):
                    bank, free = take(act, ("tr", "qk", hg, i, t))
                    if hg:
                        take(act, ("lg", 3, 1))
                    act.activation((q_f, k_f)[i][:, :, t * P:(t + 1) * P],
                                   bank[:, :].rearrange("p (j s) -> p j s", j=4), ACT.Copy,
                                   scale=st[:, 92 + i:93 + i]).then_inc(free, 1)

            def exps(hd):
                act.wait_ge(S("lg_read"), 2 * hd + 2)
                v, c0 = lg[hd % 2], 4 * (hd % 2)
                for lo, w, c in ((0, SEQ, 2), (SEQ, SEQ, 3), (2 * SEQ, P, 0), (2 * SEQ + P, P, 1)):
                    ins = act.activation(v[:, lo:lo + w], v[:, lo:lo + w], ACT.Exp, scale=-1.0,
                                         bias=st[:, 64 + c0 + c:65 + c0 + c], accum_out=st[:, 72 + c0 + c:73 + c0 + c])
                ins.then_inc(S("exps"), 1)

            def weights(hd):
                bank, free = take(act, ("tr", "w", hd))
                act.activation(w_f[hd], bank[:, 0:384], ACT.Copy).then_inc(S("w_copied"), 1)

            def v_evac(hg):
                for t in range(TT):
                    bank, free = take(act, (("v", hg), t))
                    act.activation(vv[:, t, hg * 512:(hg + 1) * 512], bank[:, :], ACT.Copy, scale=st2[:, 4 + t:5 + t]) \
                       .then_inc(S("v_copied"), 1)

            def o_squares(pair):
                freed(act, ("pv", pair))
                for j in range(4):
                    t, hd, n_ = j // 2, 2 * pair + j % 2, 4 * pair + j
                    if n_ >= 2:
                        act.wait_ge(S("o_ss"), n_ - 1)
                    act.activation(sq_o[:, j % 2, :], oo[:, t, hd * P:(hd + 1) * P], ACT.Square,
                                   accum_out=st[:, 48 + 8 * t + hd:49 + 8 * t + hd]).then_inc(S("o_ss"), 1)

            feed(g + 3)
            qk_evac(0, 0)
            feed(g + 5)
            qk_evac(0, 1)
            feed(g + 6)
            qk_features(0, 0)
            feed(g + 7)
            qk_features(0, 1)
            qk_evac(1, 0)
            feed(g + 8)
            exps(0)
            exps(1)
            weights(0)
            exps(2)
            feed(g + 9)
            qk_evac(1, 1)
            weights(1)
            feed(g + 10)
            exps(3)
            qk_features(1, 0)
            v_evac(0)
            weights(2)
            feed(g + 11)
            qk_features(1, 1)
            feed(g + 12)
            weights(3)
            exps(4)
            exps(5)
            weights(4)
            v_evac(1)
            exps(6)
            weights(5)
            exps(7)
            o_squares(0)
            weights(6)
            o_squares(1)
            weights(7)
            feed(g + 13)
            o_squares(2)
            o_squares(3)
            take(act, ("pv", 1))
            ahead(G["proj1"])
            proj_copy(1)
            for k in range(2):
                for t in range(TT):
                    split_hi(("o", k, t), z_hi, 4 * k, slice(t * P, (t + 1) * P))
            ahead(G["wo"] + 2)
            h_split(3, 0)
            ahead(G["wo"] + 3)
            h_split(3, 1)
            h_stats(3)
            ffn(1, 3)
            ple(1, 4)

            act.wait_ge(S("r_done"), 6)

            def evac(name, func, dst, extra=None, accum=None, sig=None):
                for n in range(2):
                    ahead(G[name] + 2 * n + 1)
                    for t in range(TT):
                        bank, free = take(act, ((name, n), t))
                        if extra:
                            extra(n, t)
                        act.activation(dst[:, t, n * 512:(n + 1) * 512], bank[:, :], func, scale=st2[:, 10 + t:11 + t],
                                       **({"accum_out": accum[:, 2 * t + n:2 * t + n + 1]} if accum is not None else {})) \
                           .then_inc(free, 1)

            evac("av", ACT.Gelu_apprx_tanh, av, accum=st[:, 16:20])
            act.wait_ge(S("v_mean"), 1)
            for t in range(TT):
                act.activation(junk_v[:, t, :], av[:, t, :], ACT.Square, bias=st[:, 20 + t:21 + t],
                               accum_out=st[:, 22 + t:23 + t]).then_inc(S("v_var"), 1)
            evac("au", ACT.Gelu_apprx_tanh, au)
            evac("az", ACT.Silu, az)
            for n in range(2):
                ahead(G["ga"] + 2 * n)
                if n:
                    for t in range(TT):
                        plain_hi(("ya", 0, t), z_hi, 0, slice(t * P, (t + 1) * P))
                ahead(G["ga"] + 2 * n + 1)
                for t in range(TT):
                    bank, free = take(act, (("ga", n), t))
                    act.activation(gate[:, t, n * 512:(n + 1) * 512], bank[:, :], ACT.Sigmoid,
                                   scale=st2[:, 10 + t:11 + t]).then_inc(free, 1)
            for t in range(TT):
                plain_hi(("ya", 1, t), z_hi, 4, slice(t * P, (t + 1) * P))
            ahead(G["wa"] + 3)
            evac("bp", ACT.Copy, av, extra=lambda n, t: freed(act, ("mixed", 1, 1)))
            for n in range(2):
                ahead(G["bz"] + 2 * n + 1)
                if n:
                    for w in range(4):
                        bank, _ = take(act, ("pool", w))
                        act.activation(z_hi[:, 2 * w:2 * w + 2, :], bank[:, :].rearrange("p (k s) -> p k s", k=2),
                                       ACT.Copy).then_inc(S("t_hi"), 1)
                for t in range(TT):
                    bank, free = take(act, (("bz", n), t))
                    if n == 0 and t == 0:
                        act.wait_ge(S("ya"), 4)
                    act.activation(az[:, t, n * 512:(n + 1) * 512], bank[:, :], ACT.Silu,
                                   scale=st2[:, 10 + t:11 + t]).then_inc(free, 1)
            ahead(G["poolw"])
            for n in range(2):
                ahead(G["gb"] + 2 * n)
                if n:
                    for t in range(TT):
                        plain_hi(("yb", 0, t), z_hi, 0, slice(t * P, (t + 1) * P))
                ahead(G["gb"] + 2 * n + 1)
                for t in range(TT):
                    bank, free = take(act, (("gb", n), t))
                    freed(act, (("wa", n), t))
                    act.activation(gate[:, t, n * 512:(n + 1) * 512], bank[:, :], ACT.Sigmoid,
                                   scale=st2[:, 10 + t:11 + t]).then_inc(free, 1)
            for t in range(TT):
                plain_hi(("yb", 1, t), z_hi, 4, slice(t * P, (t + 1) * P))
            ahead(G["wb"] + 3)
            act.wait_ge(S("c_zero"), 1)
            for j in range(KB):
                g = G["cc"] + 2 * j
                ahead(g)
                s = j % 2
                bank, free = take(act, ("cc", j, 0))
                if j >= 2:
                    act.wait_ge(S("yc_split"), j - 1)
                act.activation(c_h[:, s, :], bank[:, 0:SEQ], ACT.Copy).then_inc(S("c_hc"), 1)
                ahead(g + 1)
                act.wait_ge(S("c_zr"), j + 1)
                act.activation(c_s[:, s, :], c_z[:, s, :], ACT.Silu).then_inc(S("c_silu"), 1)
                act.wait_ge(S("yc"), j + 1)
                act.activation(z_hi[:, j, :], c_f[:, s, :], ACT.Copy).then_inc(S("yc_hi"), 1)
            for n in range(2):
                ahead(G["gc"] + 2 * n + 1)
                for t in range(TT):
                    bank, free = take(act, (("gc", n), t))
                    freed(act, (("wb", n), t))
                    act.activation(gate[:, t, n * 512:(n + 1) * 512], bank[:, :], ACT.Sigmoid,
                                   scale=st2[:, 10 + t:11 + t]).then_inc(free, 1)
            ahead(G["wc"] + 2)
            for t in range(TT):
                plain_hi(("merged", 0, t), x_hi, 0, slice(t * P, (t + 1) * P))
            ahead(G["wc"] + 3)
            for t in range(TT):
                plain_hi(("merged", 1, t), x_hi, 4, slice(t * P, (t + 1) * P))
            ahead(NPIECE)
            h_stats(6)

        @block.vector
        def _(dve):
            fed = [0]
            n = [0]

            def link(ins):
                n[0] += 1
                ins.then_inc(dve_step, 1)
                dve.wait_ge(dve_step, n[0])

            def feed(to):
                while fed[0] <= min(to, NPIECE - 1):
                    g = fed[0]
                    dve.wait_ge(hi_done, g + 1)
                    dve.tensor_tensor(w_lo[:, g % SPLIT, :], raw[:, g % RAW, :], w_hi[:, g % SPLIT, :].bitcast(F32),
                                      ALU.subtract).then_inc(lo_done, 1)
                    fed[0] += 1

            def ahead(g):
                feed(g + SPLIT - 1)

            def rsqrt(src, v, yy, tmp, scale, eps, done):
                link(dve.tensor_scalar(v, src, scale, eps, ALU.mult, ALU.add))
                link(dve.tensor_scalar(yy.bitcast(I32), v.bitcast(I32), 1, None, ALU.logical_shift_right))
                link(dve.tensor_scalar(yy.bitcast(I32), yy.bitcast(I32), -1.0, float(0x5F3759DF), ALU.mult, ALU.add))
                for it in range(3):
                    link(dve.tensor_tensor(tmp, yy, yy, ALU.mult))
                    link(dve.scalar_tensor_tensor(out=tmp, in0=v, scalar=-0.5, in1=tmp, op0=ALU.mult, op1=ALU.mult))
                    ins = dve.scalar_tensor_tensor(out=yy, in0=tmp, scalar=1.5, in1=yy, op0=ALU.add, op1=ALU.mult)
                    if it < 2:
                        link(ins)
                ins.then_inc(done, 1)

            hi_count = [0]
            stage_read = [0, 0]
            split_count = [0]

            def gain_block(key, gain, gcols):
                bank, free = take(dve, ("tr",) + key)
                s = job_no[key] % 2
                if stage_read[s]:
                    dve.wait_ge(S("x_split"), stage_read[s])
                dve.tensor_tensor(stage[:, s, :].rearrange("p (k c) -> p k c", k=4),
                                  bank[:, :].rearrange("p (k c) -> p k c", k=4),
                                  gain.unsqueeze(2).to_broadcast([P, 4, P]), ALU.mult).then_inc(free, 1)

            def split_lo(key, hi, lo, k0, w):
                s = job_no[key] % 2
                hi_count[0] += 1
                split_count[0] += 1
                stage_read[s] = split_count[0]
                dve.wait_ge(S("t_hi"), hi_count[0])
                dve.tensor_tensor(lo[:, k0:k0 + 4, w], stage[:, s, :].rearrange("p (k c) -> p k c", k=4),
                                  hi[:, k0:k0 + 4, w].bitcast(F32), ALU.subtract).then_inc(S("x_split"), 1)

            def h_split(m, n, gname):
                for t in range(TT):
                    gain_block((m, n, t), col(gname, 4 * n, 4), 4)
                for t in range(TT):
                    split_lo((m, n, t), x_hi, x_lo, 4 * n, slice(t * P, (t + 1) * P))

            def h_factor(m):
                dve.wait_ge(S("h_ss"), 2 * m + 2)
                c = slice(2 * m, 2 * m + 2)
                rsqrt(st[:, c], st2[:, 60:62], st2[:, c], st2[:, 62:64], 1.0 / D, EPS, S("r_done"))

            def plain_lo(key, hi, lo, k0, w):
                bank, free = take(dve, ("tr",) + key)
                hi_count[0] += 1
                dve.wait_ge(S("t_hi"), hi_count[0])
                dve.tensor_tensor(lo[:, k0:k0 + 4, w], bank[:, :].rearrange("p (k c) -> p k c", k=4),
                                  hi[:, k0:k0 + 4, w].bitcast(F32), ALU.subtract).then_inc(free, 1)

            def ffn(layer, m, gname):
                g0 = G[f"ffn{layer}"]

                def hidden_lo(i):
                    bank, free = take(dve, ("tr", "hid", layer, i))
                    k0 = (2 * i) % KB
                    hi_count[0] += 1
                    dve.wait_ge(S("t_hi"), hi_count[0])
                    dve.tensor_tensor(z_lo[:, k0:k0 + 2, :], bank[:, :].rearrange("p (k s) -> p k s", k=2),
                                      z_hi[:, k0:k0 + 2, :].bitcast(F32), ALU.subtract).then_inc(free, 1)

                dve.wait_ge(S("r_done"), m + 1)
                for i in range(GU):
                    g = g0 + gu_at(i)
                    ahead(g)
                    if i:
                        hidden_lo(i - 1)
                    ahead(g + 1)
                    for t in range(TT):
                        bank, free = take(dve, (("gu", layer, i), t))
                        dve.wait_ge(S("silu"), 2 * (GU * layer + i) + t + 1)
                        dve.scalar_tensor_tensor(out=hid[:, t, :], in0=bank[:, 256:512],
                                                 scalar=st2[:, 2 * m + t:2 * m + t + 1], in1=silu_t[:, t, :],
                                                 op0=ALU.mult, op1=ALU.mult).then_inc(S("hidden"), 1)
                    if i >= 2 and i % 2 == 0:
                        ahead(g0 + down_at(i // 2 - 1))
                        ahead(g0 + down_at(i // 2 - 1) + 1)
                hidden_lo(GU - 1)
                ahead(g0 + 32)
                for n in range(2):
                    for t in range(TT):
                        add_h(("ffn", layer, n, t), n, t)
                    h_split(m + 1, n, gname)
                h_factor(m + 1)

            def add_h(key, n, t):
                bank, free = take(dve, key)
                hs = h[:, t, n * 512:(n + 1) * 512]
                dve.tensor_tensor(hs, hs, bank[:, :], ALU.add).then_inc(S("h_done"), 1)

            def ple(layer, m, gname):
                g0 = G[f"ple{layer}"]
                for n in range(2):
                    ahead(g0 + 2 * n)
                    if n:
                        h_split(m + 1, 0, gname)
                    ahead(g0 + 2 * n + 1)
                    for t in range(TT):
                        freed(dve, (("ple", layer, n), t))
                        c = slice(n * 512, (n + 1) * 512)
                        dve.tensor_tensor(prod_t[:, t, :], gate_t[:, t, :], pp[:, t, c], ALU.mult).then_inc(S("gate_used"), 1)
                        dve.wait_ge(S("gate_used"), 4 * layer + 2 * n + t + 1)
                        dve.tensor_tensor(h[:, t, c], h[:, t, c], prod_t[:, t, :], ALU.add).then_inc(S("h_done"), 1)
                h_split(m + 1, 1, gname)
                h_factor(m + 1)

            def p_split(layer):
                dve.wait_ge(S("p_hi"), layer + 1)
                dve.tensor_tensor(z_lo[:, 0:2, :], p_t1 if layer else p_t0, z_hi[:, 0:2, :].bitcast(F32),
                                  ALU.subtract).then_inc(S("p_split"), 1)

            dve.wait_ge(S("ld_par"), 16)
            dve.wait_ge(S("taps_hi"), 1)
            taps = prm[:, PCOL["dw_w"] + CONV_PE * TAPS:PCOL["dw_w"] + KB * TAPS]
            dve.tensor_tensor(taps_lo.rearrange("p a b -> p (a b)").bitcast(F32R), taps,
                              taps_hi.rearrange("p a b -> p (a b)"), ALU.subtract).then_inc(S("taps_split"), 1)
            dve.wait_ge(S("x_ss"), 2)
            rsqrt(st[:, 80:82], st2[:, 60:62], st2[:, 48:50], st2[:, 62:64], 1.0 / D, EPS, S("x_r"))
            p_split(0)
            for t in range(TT):
                gain_block(("x", 0, t), col("conv_g", 0, 4), 4)
            feed(0)
            for n_ in range(2):
                for t in range(TT):
                    if n_:
                        gain_block(("x", 1, t), col("conv_g", 4, 4), 4)
                for t in range(TT):
                    split_lo(("x", n_, t), x_hi, x_lo, 4 * n_, slice(t * P, (t + 1) * P))
                feed(n_ + 1)
            dve.wait_ge(S("consts"), 4)

            def gated(f):
                ahead(G["pw1"] + f)
                bank, free = take(dve, ("pw1", f))
                dve.wait_ge(S("sig"), f + 1)
                dve.scalar_tensor_tensor(out=u_pad[:, f, TAPS - 1:], in0=bank[:, 0:SEQ], scalar=col("b_a", f),
                                         in1=sig[:, f % 2, :], op0=ALU.add, op1=ALU.mult).then_inc(S("u"), 1)
                if f >= CONV_PE:
                    dve.wait_ge(S("u_hi"), f - CONV_PE + 1)
                    w = slice((f - CONV_PE) * PADDED, (f - CONV_PE + 1) * PADDED)
                    dve.tensor_tensor(flat(z_lo)[:, w], u_pad[:, f, :], flat(z_hi)[:, w].bitcast(F32),
                                      ALU.subtract).then_inc(S("u_split"), 1)

            def taps_of_pair(f0, side):
                last = {}
                dve.wait_ge(S("u"), f0 + 2)
                for tap in range(TAPS):
                    for f in (f0, f0 + 1):
                        if tap == 0:
                            ins = dve.tensor_scalar(y[:, f, :], u_pad[:, f, 0:SEQ], col("dw_w", f * TAPS),
                                                    col("dw_b", f), ALU.mult, ALU.add)
                        else:
                            dve.wait_ge(dve_step, last[f])
                            ins = dve.scalar_tensor_tensor(out=y[:, f, :], in0=u_pad[:, f, tap:tap + SEQ],
                                                           scalar=col("dw_w", f * TAPS + tap), in1=y[:, f, :],
                                                           op0=ALU.mult, op1=ALU.add)
                        if tap < TAPS - 1:
                            n[0] += 1
                            ins.then_inc(dve_step, 1)
                            last[f] = n[0]
                        else:
                            ins.then_inc(S("conv"), 1)
                    if tap in side:
                        gated(side[tap])

            gated(0)
            gated(1)
            taps_of_pair(0, {4: 2, 8: 3, 12: 4, 18: 5})
            taps_of_pair(2, {0: 6, 14: 7})
            ahead(G["pw2"])
            bank, free = take(dve, "mean")
            dve.wait_ge(S("conv"), CONV_PE)
            dve.wait_ge(S("conv_pe"), KB - CONV_PE)
            for a in range(2):
                k = slice(4 * a, 4 * a + 4)
                dve.tensor_tensor(y[:, k, :], y[:, k, :], bank[:, 0:SEQ].unsqueeze(1).to_broadcast([P, 4, SEQ]),
                                  ALU.subtract).then_inc(S("centred"), 1)
            dve.wait_ge(S("centred"), 2)
            bank, free = take(dve, "var")
            rsqrt(bank[:, 0:SEQ], wide[:, 0, :], wide[:, 1, :], wide[:, 2, :], 1.0, EPS, S("y_r"))
            dve.wait_ge(S("y_r"), 1)
            for a in range(2):
                k = slice(4 * a, 4 * a + 4)
                dve.tensor_tensor(y[:, k, :], y[:, k, :], wide[:, 1:2, :].to_broadcast([P, 4, SEQ]), ALU.mult) \
                   .then_inc(S("scaled"), 1)
            for a in range(2):
                k = slice(4 * a, 4 * a + 4)
                dve.wait_ge(S("v_act"), 4 * a + 4)
                link(dve.tensor_copy(z_hi[:, k, :], v_f[:, k, :]))
                dve.tensor_tensor(z_lo[:, k, :], v_f[:, k, :], z_hi[:, k, :].bitcast(F32), ALU.subtract) \
                   .then_inc(S("v_split"), 1)
            dve.wait_ge(S("h_biased"), 2)
            ahead(G["pw2"] + 1)
            for t in range(TT):
                add_h((("pw2", 0), t), 0, t)
            ahead(G["pw2"] + 2)
            h_split(0, 0, "ffn_g0")
            ahead(G["pw2"] + 3)
            for t in range(TT):
                add_h((("pw2", 1), t), 1, t)
            h_split(0, 1, "ffn_g0")
            h_factor(0)
            ffn(0, 0, "ple_g0")
            bank, free = take(dve, "bias")
            dve.tensor_copy(bias_row[:, 0:SEQ], bank[0:HEADS, 0:SEQ]).then_inc(free, 1)
            freed(dve, "bias")
            dve.tensor_scalar(bias_row[:, 0:1], bias_row[:, 0:1], 1.0, None, ALU.mult).then_inc(S("bias_row"), 1)
            dve.memset(bias_row[:, SEQ:384], NEG).then_inc(S("bias_row"), 1)
            link(dve.tensor_tensor(lam_t[:, 0:4:2, :], lam_t[:, 0:4:2, :], lam_t[:, 1:4:2, :], ALU.mult))
            dve.tensor_reduce(st[:, 88:90], lam_t[:, 0:4:2, :], AX, ALU.add).then_inc(S("lam_sum"), 1)
            dve.tensor_scalar(st[:, 92:93], col("q_g"), HD ** -0.5, None, ALU.mult).then_inc(S("attn_small"), 1)
            dve.tensor_scalar(st[:, 93:94], col("k_g"), 1.0, None, ALU.mult).then_inc(S("attn_small"), 1)
            dve.tensor_scalar(st[:, 95:96], col("sub_g"), 1.0 - LAMBDA_INIT, None, ALU.mult).then_inc(S("attn_small"), 1)
            ple(0, 1, "attn_g")

            ahead(G["qkv"])
            dve.wait_ge(S("lam_exp"), 1)
            link(dve.tensor_tensor(st[:, 94:95], st[:, 91:92], st[:, 90:91], ALU.subtract))
            link(dve.tensor_scalar(st[:, 94:95], st[:, 94:95], -LAMBDA_INIT, None, ALU.add))
            p_split(1)
            g = G["qkv"]

            def qk_norm(hg, i):
                for t in range(TT):
                    dve.wait_ge(S("qk_sq"), 4 * hg + 2 * i + t + 1)
                    c = 16 + 16 * i + 8 * t
                    dve.tensor_reduce(st[:, c:c + 8], sq_t[:, t, :].rearrange("p (g d) -> p g d", d=HD), AX, ALU.add) \
                       .then_inc(S("qk_ss"), 1)
                dve.wait_ge(S("qk_ss"), 4 * hg + 2 * i + 2)
                c = 16 + 16 * i
                rsqrt(st[:, c:c + 16], qk_v, st2[:, c:c + 16], qk_tmp, 1.0 / HD, EPS, S("qk_r"))
                dve.wait_ge(S("qk_r"), 2 * hg + i + 1)
                for t in range(TT):
                    v = qk_t[:, i, t, :].rearrange("p (g d) -> p g d", d=HD)
                    c = 16 + 16 * i + 8 * t
                    dve.tensor_tensor(v, v, st2[:, c:c + 8].unsqueeze(2).to_broadcast([P, 8, HD]), ALU.mult) \
                       .then_inc(S("qk_normed"), 1)

            def masked(hd):
                v, c0 = lg[hd % 2], 64 + 4 * (hd % 2)
                if hd >= 2:
                    dve.wait_ge(S("w_mix"), hd - 1)
                for c in range(2):
                    bank, _ = take(dve, ("lg", hd, c))
                    for lo, w, k0, a in ((c * SEQ, SEQ, 0, 2 + c), (2 * SEQ + c * P, P, SEQ, c)):
                        ins = dve.tensor_tensor_reduce(v[:, lo:lo + w], bank[:, k0:k0 + w], toep_t[:, hd, k0:k0 + w],
                                                       -1.0, 3.0e38, ALU.add, ALU.min, st[:, c0 + a:c0 + a + 1])
                    ins.then_inc(S("lg_read"), 1)

            def mix(hd):
                dve.wait_ge(S("exps"), hd + 1)
                s, v, p = st[:, 72 + 4 * (hd % 2):76 + 4 * (hd % 2)], lg[hd % 2], hd % 2
                link(dve.reciprocal(rec[:, hd, :], s))
                link(dve.scalar_tensor_tensor(out=st2[:, 52 + 2 * p:54 + 2 * p], in0=rec[:, hd, 1:4:2], scalar=st[:, 94:95],
                                              in1=s[:, 0:4:2], op0=ALU.mult, op1=ALU.mult))
                if hd >= 2:
                    take(dve, ("tr", "w", hd - 2))
                dve.scalar_tensor_tensor(out=wt[:, p, 0:SEQ], in0=v[:, SEQ:2 * SEQ], scalar=st2[:, 53 + 2 * p:54 + 2 * p],
                                         in1=v[:, 0:SEQ], op0=ALU.mult, op1=ALU.add)
                dve.scalar_tensor_tensor(out=wt[:, p, SEQ:384], in0=v[:, 2 * SEQ + P:768],
                                         scalar=st2[:, 52 + 2 * p:53 + 2 * p], in1=v[:, 2 * SEQ:2 * SEQ + P],
                                         op0=ALU.mult, op1=ALU.add).then_inc(S("w_mix"), 1)

            def o_evac(pair):
                bank, free = take(dve, ("pv", pair))
                dve.tensor_tensor(oo[:, :, 2 * pair * P:(2 * pair + 2) * P].rearrange("p t (h d) -> p t h d", h=2),
                                  bank[:, :].rearrange("p (t h d) -> p t h d", t=TT, h=2),
                                  rec[:, 2 * pair:2 * pair + 2, 0:4:2].rearrange("p h t -> p t h").unsqueeze(3)
                                  .to_broadcast([P, TT, 2, P]), ALU.mult).then_inc(free, 1)

            feed(g + 4)
            qk_norm(0, 0)
            feed(g + 6)
            qk_norm(0, 1)
            feed(g + 7)
            dve.wait_ge(S("ld_toep"), 32)
            masked(0)
            masked(1)
            feed(g + 8)
            mix(0)
            masked(2)
            qk_norm(1, 0)
            mix(1)
            feed(g + 9)
            masked(3)
            mix(2)
            feed(g + 10)
            qk_norm(1, 1)
            feed(g + 11)
            mix(3)
            masked(4)
            masked(5)
            mix(4)
            masked(6)
            mix(5)
            masked(7)
            feed(g + 12)
            mix(6)
            o_evac(0)
            mix(7)
            o_evac(1)
            feed(g + 13)
            o_evac(2)
            o_evac(3)
            dve.wait_ge(S("o_ss"), 16)
            rsqrt(st[:, 48:64], qk_v, st2[:, 16:32], qk_tmp, 1.0 / P, EPS, S("o_r"))
            dve.wait_ge(S("o_r"), 1)
            for t in range(TT):
                v = oo[:, t, :].rearrange("p (g d) -> p g d", d=P)
                dve.tensor_tensor(v, v, st2[:, 16 + 8 * t:24 + 8 * t].unsqueeze(2).to_broadcast([P, 8, P]), ALU.mult) \
                   .then_inc(S("o_normed"), 1)
            ahead(G["proj1"])
            for n_ in range(2):
                for t in range(TT):
                    gain_block(("o", n_, t), st[:, 95:96], 1)
                for t in range(TT):
                    split_lo(("o", n_, t), z_hi, z_lo, 4 * n_, slice(t * P, (t + 1) * P))
            ahead(G["wo"] + 1)
            for t in range(TT):
                add_h((("wo", 0), t), 0, t)
            ahead(G["wo"] + 2)
            h_split(3, 0, "ffn_g1")
            ahead(G["wo"] + 3)
            for t in range(TT):
                add_h((("wo", 1), t), 1, t)
            h_split(3, 1, "ffn_g1")
            h_factor(3)
            ffn(1, 3, "ple_g1")
            ple(1, 4, "norm_g2")

            ahead(G["av"] + 3)
            for n_ in range(2):
                for t in range(TT):
                    freed(dve, (("av", n_), t))
            link(dve.tensor_tensor(st[:, 20:22], st[:, 16:20:2], st[:, 17:20:2], ALU.add))
            dve.tensor_scalar(st[:, 20:22], st[:, 20:22], -1.0 / D, None, ALU.mult).then_inc(S("v_mean"), 1)
            dve.wait_ge(S("v_mean"), 1)
            dve.wait_ge(S("v_var"), 2)
            rsqrt(st[:, 22:24], st2[:, 60:62], st2[:, 22:24], st2[:, 62:64], 1.0 / D, LN_EPS_2, S("v_r"))
            dve.wait_ge(S("v_r"), 1)
            dve.wait_ge(S("ld_sgu"), 32)
            for t in range(TT):
                link(dve.tensor_scalar(av[:, t, :], av[:, t, :], st[:, 20 + t:21 + t], st2[:, 22 + t:23 + t],
                                       ALU.add, ALU.mult))
                link(dve.tensor_tensor(av[:, t, :], av[:, t, :], ln_row[:, 0, :], ALU.mult))
                dve.tensor_tensor(av[:, t, :], av[:, t, :], ln_row[:, 1, :], ALU.add).then_inc(S("sgu_ready"), 1)
                ahead(G["au"] + t)
            for t in range(TT):
                dve.tensor_scalar(diag[:, t, :], ident[:, :], st2[:, 10 + t:11 + t], None, ALU.mult).then_inc(S("diag"), 1)
            ahead(G["au"] + 3)
            bank, free = take(dve, "r_row")
            dve.tensor_copy(rb, bank[:, 0:SEQ]).then_inc(free, 1)
            freed(dve, "r_row")
            link(dve.tensor_tensor(rb2, rb, rb, ALU.mult))
            ahead(G["az"] + 1)
            for n_ in range(2):
                for t in range(TT):
                    bank, free = take(dve, ("mixed", t, n_))
                    freed(dve, (("au", n_), t))
                    for j in range(4):
                        gi = 4 * n_ + j
                        c = slice(gi * P, (gi + 1) * P)
                        ins = dve.scalar_tensor_tensor(out=au[:, t, c], in0=bank[:, j * P:(j + 1) * P],
                                                       scalar=col("sgu_b", gi), in1=au[:, t, c], op0=ALU.add, op1=ALU.mult)
                    ins.then_inc(free, 1)
                if n_:
                    ahead(G["az"] + 3)
                for t in range(TT):
                    freed(dve, ("mixed", t, n_))
                    freed(dve, (("az", n_), t))
                    c = slice(n_ * 512, (n_ + 1) * 512)
                    dve.tensor_tensor(au[:, t, c], au[:, t, c], az[:, t, c], ALU.mult).then_inc(S("ya"), 1)
            for n_ in range(2):
                ahead(G["ga"] + 2 + n_)
                for t in range(TT):
                    plain_lo(("ya", n_, t), z_hi, z_lo, 4 * n_, slice(t * P, (t + 1) * P))
            for n_ in range(2):
                ahead(G["wa"] + 2 * n_ + 1)
                for t in range(TT):
                    c = slice(n_ * 512, (n_ + 1) * 512)
                    bank, free = take(dve, (("wa", n_), t))
                    freed(dve, (("ga", n_), t))
                    dve.tensor_tensor(merged[:, t, c], bank[:, :], gate[:, t, c], ALU.mult).then_inc(free, 1)

            ahead(G["bp"] + 3)
            ahead(G["bz"] + 1)
            for w in range(4):
                bank, free = take(dve, ("pool", w))
                hi_count[0] += 1
                dve.wait_ge(S("t_hi"), hi_count[0])
                dve.tensor_tensor(z_lo[:, 2 * w:2 * w + 2, :], bank[:, :].rearrange("p (k s) -> p k s", k=2),
                                  z_hi[:, 2 * w:2 * w + 2, :].bitcast(F32), ALU.subtract).then_inc(free, 1)
            ahead(G["bz"] + 3)
            ahead(G["poolw"])
            dve.wait_ge(S("ld_pool"), 16)
            for n_ in range(2):
                c = slice(n_ * 512, (n_ + 1) * 512)
                for t in range(TT):
                    bank, free = take(dve, ("pooled", n_, t))
                    dve.tensor_tensor(au[:, t, c], bank[:, :], pool_row[:, 0, c], ALU.add).then_inc(free, 1)
                    freed(dve, ("pooled", n_, t))
                    link(dve.tensor_tensor(au[:, t, c], au[:, t, c], pool_row[:, 1, c], ALU.mult))
                    freed(dve, (("bz", n_), t))
                    dve.tensor_tensor(au[:, t, c], au[:, t, c], az[:, t, c], ALU.mult).then_inc(S("yb"), 1)
            for n_ in range(2):
                ahead(G["gb"] + 2 + n_)
                for t in range(TT):
                    plain_lo(("yb", n_, t), z_hi, z_lo, 4 * n_, slice(t * P, (t + 1) * P))

            def merge(name, gate_name, done):
                for n_ in range(2):
                    ahead(G[name] + 2 * n_ + 1)
                    if name == "wc" and n_:
                        pass
                    c = slice(n_ * 512, (n_ + 1) * 512)
                    for t in range(TT):
                        bank, free = take(dve, ((name, n_), t))
                        freed(dve, ((gate_name, n_), t))
                        dve.tensor_tensor(tmp[:, t, :], bank[:, :], gate[:, t, c], ALU.mult).then_inc(free, 1)
                        freed(dve, ((name, n_), t))
                        dve.tensor_tensor(merged[:, t, c], merged[:, t, c], tmp[:, t, :], ALU.add).then_inc(S(done), 1)
                    if name == "wc":
                        if n_ == 0:
                            ahead(G[name] + 2)
                        for t in range(TT):
                            plain_lo(("merged", n_, t), x_hi, x_lo, 4 * n_, slice(t * P, (t + 1) * P))

            merge("wb", "gb", "merged_b")

            dve.wait_ge(S("merged_b"), 4)
            dve.memset(c_pad[:, :, 0:2], 0.0).then_inc(S("c_zero"), 1)
            for j in range(KB):
                g = G["cc"] + 2 * j
                s = j % 2
                ahead(g)
                bank, free = take(dve, ("cc", j, 0))
                dve.wait_ge(S("c_hc"), j + 1)
                dve.tensor_tensor(c_y[:, s, :], bank[:, SEQ:2 * SEQ], c_h[:, s, :], ALU.mult).then_inc(free, 1)
                freed(dve, ("cc", j, 0))
                link(dve.tensor_tensor(c_pad[:, s, 2:], c_y[:, s, :], rb2, ALU.mult))
                link(dve.tensor_scalar(c_y[:, s, :], c_pad[:, s, 0:SEQ], col("c3_w", 3 * j), col("c3_b", j),
                                       ALU.mult, ALU.add))
                for k in (1, 2):
                    link(dve.scalar_tensor_tensor(out=c_y[:, s, :], in0=c_pad[:, s, k:k + SEQ],
                                                  scalar=col("c3_w", 3 * j + k), in1=c_y[:, s, :],
                                                  op0=ALU.mult, op1=ALU.add))
                ahead(g + 1)
                bank, _ = take(dve, ("cc", j, 1))
                dve.tensor_tensor(c_b[:, s, :], bank[:, 0:SEQ], rb, ALU.mult)
                dve.tensor_tensor(c_z[:, s, :], bank[:, SEQ:2 * SEQ], rb, ALU.mult).then_inc(S("c_zr"), 1)
                dve.wait_ge(S("c_zr"), j + 1)
                link(dve.tensor_tensor(c_y[:, s, :], c_y[:, s, :], c_b[:, s, :], ALU.mult))
                dve.wait_ge(S("c_silu"), j + 1)
                dve.tensor_tensor(c_f[:, s, :], c_y[:, s, :], c_s[:, s, :], ALU.mult).then_inc(S("yc"), 1)
                dve.wait_ge(S("yc_hi"), j + 1)
                dve.tensor_tensor(z_lo[:, j, :], c_f[:, s, :], z_hi[:, j, :].bitcast(F32), ALU.subtract) \
                   .then_inc(S("yc_split"), 1)
            ahead(G["gc"] + 3)
            merge("wc", "gc", "merged")

            for n_ in range(2):
                ahead(G["wout"] + 2 * n_ + 1)
                for t in range(TT):
                    add_h((("wout", n_), t), n_, t)
            h_factor(6)
            dve.wait_ge(S("r_done"), 7)
            dve.wait_ge(S("ld_final"), 16)
            for t in range(TT):
                dve.scalar_tensor_tensor(out=av[:, t, :], in0=h[:, t, :], scalar=st2[:, 12 + t:13 + t], in1=final_row,
                                         op0=ALU.mult, op1=ALU.mult).then_inc(S("out_ready"), 1)


def bucket(dist):
    n = np.maximum(dist, 0)
    f = np.maximum(n, 1).astype(np.float32)
    large = 16 + (np.log(f / np.float32(16)) / np.float32(math.log(128 / 16)) * np.float32(16)).astype(np.int32)
    return np.where(n < 16, n, np.minimum(large, NBUCKET - 1))


def constants():
    onehot = np.zeros((NBUCKET, 384), np.float32)
    dist = np.arange(SEQ - 1, -1, -1)
    onehot[bucket(dist), np.arange(SEQ)] = 1.0
    pool = np.zeros((4, SEQ, SEQ), np.float32)
    for w, win in enumerate(WINDOWS):
        for s in range(SEQ):
            lo = max(0, s - win + 1)
            pool[w, lo:s + 1, s] = np.float32(1.0) / np.float32(s + 1 - lo)
            pool[w, s, s] -= 1.0
    pm = np.zeros((P, 4, 384), np.float32)
    for w in range(4):
        pm[:, w, 0:SEQ] = pool[w, 0:P, :]
        pm[:, w, SEQ:384] = pool[w, P:, P:]
    return onehot, pm


def kernel(**inputs):
    import concourse.bacc as bacc
    from concourse.bass_utils import run_bass_kernel_spmd

    a = {k: np.asarray(v) for k, v in inputs.items()}
    ws = np.empty((NPIECE, P, HALF), np.float32)

    def rows_cols(w, k0, nk, *cols):
        b = w[k0 * P:(k0 + nk) * P].reshape(nk, P, -1)
        parts = [b[:, :, c] for c in cols]
        return np.concatenate(parts, axis=2).transpose(1, 0, 2).reshape(P, -1)

    def chunks(name, w):
        for i in range(w.shape[1] // 512):
            for k in range(2):
                ws[G[name] + 2 * i + k] = rows_cols(w, 4 * k, 4, slice(i * 512, (i + 1) * 512))

    pw1 = a["conv_w_pw1"][0]
    for f in range(KB):
        ws[G["pw1"] + f] = rows_cols(pw1, 0, KB, slice(f * P, (f + 1) * P), slice(D + f * P, D + (f + 1) * P))
    chunks("pw2", a["conv_w_pw2"][0])
    for l in range(2):
        ws[G[f"proj{l}"]] = rows_cols(a["ple_w_proj"][l], 0, 2, slice(0, D))
        chunks(f"ple{l}", a["ple_w_gate"][l])
        g0 = G[f"ffn{l}"]
        both = np.stack([a["ffn_w_gate"][l].reshape(D, GU, 256), a["ffn_w_up"][l].reshape(D, GU, 256)], 2)             .reshape(D, GU * 512)
        for i in range(GU):
            for k in range(2):
                ws[g0 + gu_at(i) + k] = rows_cols(both, 4 * k, 4, slice(i * 512, (i + 1) * 512))
            at = down_at(i // 2) + i % 2 if i < 10 else 32
            ws[g0 + at] = rows_cols(a["ffn_w_down"][l], 2 * i, 2, slice(0, D))
    qkv = a["attn_w_qkv"][0]
    order = [m * D + hg * 512 for m, hg in ((0, 0), (1, 0), (0, 1), (1, 1), (2, 0), (2, 1))]
    for i, c in enumerate(order):
        for k in range(2):
            ws[G["qkv"] + 2 * i + k] = rows_cols(qkv, 4 * k, 4, slice(c, c + 512))
    chunks("wo", a["attn_w_o"][0])
    w_in = a["w_in_2"][0]
    for name, i in [("au", 0), ("av", 1), ("az", 2), ("bp", 3), ("bz", 4), ("ga", 9), ("gb", 10), ("gc", 11)]:
        chunks(name, w_in[:, i * D:(i + 1) * D])
    for j in range(KB):
        for k, (one, two) in enumerate([(5, 7), (6, 8)]):
            ws[G["cc"] + 2 * j + k] = rows_cols(w_in, 0, KB, slice(one * D + j * P, one * D + (j + 1) * P),
                                                slice(two * D + j * P, two * D + (j + 1) * P))
    ws[G["poolw"]] = a["pool_w_2"][0].reshape(4, 2, P, 256).transpose(2, 0, 1, 3).reshape(P, HALF)
    chunks("wa", a["w_branch_a_2"][0])
    chunks("wb", a["w_branch_b_2"][0])
    chunks("wc", a["w_branch_c_2"][0])
    chunks("wout", a["w_out_2"][0])

    par = np.zeros((P, PCOLS), np.float32)

    def features(name, v):
        v = v.reshape(-1, P).T
        par[:, PCOL[name]:PCOL[name] + v.shape[1]] = v

    features("conv_g", a["conv_norm_g"][0])
    features("b_a", a["conv_b_pw1"][0, :D])
    features("b_g", a["conv_b_pw1"][0, D:])
    features("dw_b", a["conv_dw_b"][0])
    features("ln_g", a["conv_ln_g"][0])
    features("ln_b", a["conv_ln_b"][0])
    for l in range(2):
        features(f"ffn_g{l}", a["ffn_norm_g"][l])
        features(f"ple_g{l}", a["ple_norm_g"][l])
    features("attn_g", a["attn_norm_g"][0])
    features("norm_g2", a["norm_g_2"][0])
    features("c3_b", a["conv_b_2"][0])
    features("q_g", np.tile(a["attn_q_norm_g"][0], 2))
    features("k_g", np.tile(a["attn_k_norm_g"][0], 2))
    features("sub_g", a["attn_sub_norm_g"][0])
    features("sgu_b", a["sgu_b_2"][0])
    par[:, PCOL["dw_w"]:PCOL["dw_w"] + KB * TAPS] =         a["conv_dw_w"][0].reshape(TAPS, KB, P).transpose(2, 1, 0).reshape(P, KB * TAPS)
    par[:, PCOL["c3_w"]:PCOL["c3_w"] + 24] = a["conv_w_2"][0].reshape(3, KB, P).transpose(2, 1, 0).reshape(P, 24)

    onehot, pool_m = constants()
    x = a["x"][0]
    arrays = {
        "ws": ws, "x_tok": x,
        "p_feat": a["p"][:, 0].transpose(0, 2, 1).reshape(2, 2, P, SEQ).transpose(0, 2, 1, 3),
        "par": par,
        "rows": np.concatenate([a["conv_b_pw2"], a["sgu_ln_g_2"], a["sgu_ln_b_2"], a["pool_b_2"], a["pool_scale_2"],
                                a["final_g_2"][None]]),
        "lam_rows": np.concatenate([a["attn_lambda_q1"], a["attn_lambda_k1"], a["attn_lambda_q2"],
                                    a["attn_lambda_k2"]]),
        "rel": a["rel_bias"], "onehot": onehot, "sgu_w": a["sgu_w_2"][0].transpose(2, 0, 1), "pool_m": pool_m,
    }
    arrays = {f"in_{k}": np.ascontiguousarray(v) for k, v in arrays.items()}
    nc = bacc.Bacc("TRN2", target_bir_lowering=False, num_devices=1)
    args = [nc.dram_tensor(k, v.shape, F32, kind="ExternalInput").ap() for k, v in arrays.items()]
    toep = nc.dram_tensor("toep", (HEADS, P, 384), F32).ap()
    out = nc.dram_tensor("out_0", (SEQ, D), F32, kind="ExternalOutput").ap()
    build(nc, *args, toep, out)
    r = run_bass_kernel_spmd(nc, [arrays], core_ids=[0])
    return r.results[0]["out_0"].reshape(1, SEQ, D)
```

```python
import math
from contextlib import ExitStack

import numpy as np

import concourse.bass as bass
from concourse import mybir

F32 = mybir.dt.float32
F32R = mybir.dt.float32r
I32 = mybir.dt.int32
ALU = mybir.AluOpType
ACT = mybir.ActivationFunctionType
AX = mybir.AxisListType.X

P = 128
SEQ, D = 256, 1024
TT = SEQ // P
KB = D // P
DFF = 2816
PLE = 256
TAPS = 31
HEADS = 8
HD = 64
NBUCKET = 32
EPS = 1e-6
LN_EPS_2 = 1e-5
LAMBDA_INIT = 0.8 - 0.6 * math.exp(-0.3)
NEG = -1e30
WINDOWS = (2, 4, 8, 16)
HALF = 2048
RAW, SPLIT = 4, 3
GU = DFF // 256

STREAM = [("pw1", 8), ("proj0", 1), ("pw2", 4), ("ffn0", 33), ("ple0", 4), ("qkv", 12), ("proj1", 1),
          ("wo", 4), ("ffn1", 33), ("ple1", 4), ("av", 4), ("au", 4), ("az", 4), ("ga", 4), ("wa", 4),
          ("bp", 4), ("bz", 4), ("poolw", 1), ("gb", 4), ("wb", 4), ("cc", 16), ("gc", 4), ("wc", 4),
          ("wout", 4)]
G, NPIECE = {}, 0
for _name, _n in STREAM:
    G[_name] = NPIECE
    NPIECE += _n


def gu_at(i):
    return 0 if i == 0 else 2 + 6 * ((i - 1) // 2) + 2 * ((i - 1) % 2)


def down_at(q):
    return 2 + 6 * q + 4


PCOL, PCOLS = {}, 0
for _name, _n in [("conv_g", 8), ("b_a", 8), ("b_g", 8), ("dw_b", 8), ("ln_g", 8), ("ln_b", 8), ("ffn_g0", 8),
                  ("ffn_g1", 8), ("ple_g0", 8), ("ple_g1", 8), ("attn_g", 8), ("norm_g2", 8), ("c3_w", 24),
                  ("c3_b", 8), ("q_g", 1), ("k_g", 1), ("sub_g", 1), ("sgu_b", 8), ("dw_w", 8 * TAPS)]:
    PCOL[_name] = PCOLS
    PCOLS += _n


CONV_PE = 4
PADDED = TAPS - 1 + SEQ
TAP_GROUPS = [(0, 7), (7, 6), (13, 6), (19, 6), (25, 6)]


def build(nc, ws, x_tok, p_feat, par, rows, lam_rows, rel, onehot, sgu_w, pool_m, toep, out):
    ctx = ExitStack()
    with ctx:
        def sb(name, shape, dt=F32):
            return ctx.enter_context(nc.sbuf_tensor(name, shape, dt))

        def sem(name):
            return ctx.enter_context(nc.semaphore(name))

        raw = sb("raw", [P, RAW, HALF])
        w_hi = sb("w_hi", [P, SPLIT, HALF], F32R)
        w_lo = sb("w_lo", [P, SPLIT, HALF], F32R)
        h = sb("h", [P, TT, D])
        x_hi = sb("x_hi", [P, KB, SEQ], F32R)
        x_lo = sb("x_lo", [P, KB, SEQ], F32R)
        z_hi = sb("z_hi", [P, KB, SEQ], F32R)
        z_lo = sb("z_lo", [P, KB, SEQ], F32R)
        prm = sb("prm", [P, PCOLS])
        ident = sb("ident", [P, P])
        ones = sb("ones", [P, P])
        st = sb("st", [P, 96])
        st2 = sb("st2", [P, 64])
        NA = 17664
        arena = sb("arena", [P, NA])
        arena_at = nc.sbuf_base - 4 * NA
        banks = [ctx.enter_context(nc.psum_tensor(f"bank{b}", [P, 512], F32)) for b in range(8)]

        def view(off, *dims):
            n = int(np.prod(dims))
            assert off + n <= NA
            v = arena[:, off:off + n]
            if len(dims) == 1:
                return v
            names = "abc"[:len(dims)]
            return v.rearrange(f"p ({' '.join(names)}) -> p {' '.join(names)}",
                               **{c: d for c, d in zip(names, dims)})

        v_f = view(0, KB, SEQ)
        x_s = view(4336, TT, D)
        inv_d = view(11760, P)
        diag_hi = nc.alloc_sbuf_tensor_at("diag_hi", [P, 2, 7, P], F32R, offset=arena_at + 4 * 12032)
        diag_lo = nc.alloc_sbuf_tensor_at("diag_lo", [P, 2, 7, P], F32R, offset=arena_at + 4 * (12032 + 1792))
        taps_hi = view(9968, KB - CONV_PE, TAPS)
        taps_lo = view(10104, KB - CONV_PE, TAPS)
        u_pad = view(2048, KB, PADDED)
        y = view(4336, KB, SEQ)
        sq = view(6384, KB, SEQ)
        sq_x = view(6384, TT, D)
        row_b2 = view(8432, D)
        p_t0 = view(9456, 2, SEQ)
        sig = view(10480, 2, SEQ)
        wide = view(10992, 3, SEQ)
        y_sum = wide[:, 0, :]
        pp = view(15616, TT, D)
        p_t1 = view(15616, 2, SEQ)
        stage = view(0, 2, 512)
        silu_t = view(1024, 2, 256)
        hid = view(1536, 2, 256)
        gate_t = view(2048, 2, 512)
        prod_t = view(3072, 2, 512)
        junk = view(4096, D)
        wt = view(1024, 2, 384)
        sq_o = view(1792, 2, P)
        oo = view(2048, TT, D)
        rec = view(4864, HEADS, 4)
        qk_t = arena[:, 5120:7168].rearrange("p (i t c) -> p i t c", i=2, t=TT)
        sq_t = view(0, TT, 512)
        qk_v, qk_tmp = view(7168, 16), view(7184, 16)
        vv = view(7680, TT, D)
        q_f = view(9728, 4, SEQ)
        k_f = view(10752, 4, SEQ)
        toep_t = view(11776, HEADS, 384)
        lg = [view(4096, 768), view(14848, 768)]
        w_f = [view(16128 + 384 * i, 384) for i in range(4)] + [view(5120 + 384 * i, 384) for i in range(4)]
        lam_t = view(14848, 4, HD)
        rel_t = arena[0:NBUCKET, 15104:15104 + HEADS]
        onehot_t = arena[0:NBUCKET, 15112:15112 + 384]
        bias_row = arena[0:HEADS, 9728:9728 + 384]
        av = view(2048, TT, D)
        au = view(4096, TT, D)
        az = view(6144, TT, D)
        gate = view(8192, TT, D)
        merged = view(10240, TT, D)
        ln_row = view(12288, 2, D)
        pool_row = view(12288, 2, D)
        sgu_t = view(14336, HEADS, P)
        final_row = view(14336, D)
        pm = view(15360, 4, 384)
        junk_v = view(10240, TT, D)
        junk_f = view(8192, D)
        tmp = view(2048, TT, 512)
        c_h = view(2048, 2, SEQ)
        c_pad = view(2560, 2, SEQ + 2)
        c_y = view(3076, 2, SEQ)
        c_b = view(3588, 2, SEQ)
        c_z = view(4100, 2, SEQ)
        c_s = view(4612, 2, SEQ)
        c_f = view(5124, 2, SEQ)
        rb = view(16896, SEQ)
        rb2 = view(17152, SEQ)
        diag = view(17408, TT, P)

        def flat(z):
            return z[:, :, :].rearrange("p k s -> p (k s)")

        raw_loaded = [sem(f"raw_loaded{s}") for s in range(RAW)]
        hi_done, lo_done, w_used = sem("hi_done"), sem("lo_done"), sem("w_used")
        pe_filled = sem("pe_filled")
        bank_free = [sem(f"bank_free{b}") for b in range(8)]
        dve_step, pool_step = sem("dve_step"), sem("pool_step")
        ev = {}

        def S(name):
            if name not in ev:
                ev[name] = sem(name)
            return ev[name]

        def col(name, i=0, n=1):
            return prm[:, PCOL[name] + i:PCOL[name] + i + n]

        filled = {}
        jobs = {}
        job_no = {}

        block = ctx.enter_context(nc.Block())

        @block.sync
        def _(sp):
            for t in range(TT):
                sp.dma_start(h[:, t, :], x_tok[t * P:(t + 1) * P, :]).then_inc(S(f"ld_h{t}"), 16)
            for g in range(NPIECE):
                if g >= RAW:
                    sp.wait_ge(lo_done, g - RAW + 1)
                sp.dma_start(raw[:, g % RAW, :], ws[g]).then_inc(raw_loaded[g % RAW], 16)
            for t in range(TT):
                sp.wait_ge(S(f"out_ready_{t}"), 1)
                sp.dma_start(out[t * P:(t + 1) * P, :], av[:, t, :]).then_inc(S("stored"), 16)
            sp.wait_ge(S("stored"), 16 * TT)

        def bcast(src, i, n=1):
            return bass.AP(src.tensor, i * D, [[0, P], [D, n], [1, D]]) if n > 1 else \
                bass.AP(src.tensor, i * D, [[0, P], [1, D]])

        @block.tensor
        def _(pe):
            released = [None] * 8
            frees = [0] * 8
            count = {"filled": 0, "gain": 0}

            def begin(b):
                if released[b]:
                    pe.wait_ge(*released[b])

            def end(key, b, ins, piece=None, release=None):
                if release is None:
                    frees[b] += 1
                    release = (bank_free[b], frees[b])
                if piece is None:
                    ins.then_inc(pe_filled, 1)
                    count["filled"] += 1
                    filled[key] = (pe_filled, count["filled"], b, release)
                else:
                    ins.then_inc(w_used, 1)
                    filled[key] = (w_used, piece + 1, b, release)
                released[b] = release

            def mm3(dst, s_hi, s_lo, m_hi, m_lo, first, last):
                pe.matmul(dst, s_hi, m_hi, start=first, stop=False)
                pe.matmul(dst, s_hi, m_lo, start=False, stop=False)
                return pe.matmul(dst, s_lo, m_hi, start=False, stop=last)

            def tok(ap, k, t):
                return ap[:, k, t * P:(t + 1) * P]

            def wait_job(*keys):
                for key in keys:
                    pe.wait_ge(*jobs[key])

            def token_chunk(key, g0, a_hi, a_lo, ready=None, between=None, release=None, hooks={}):
                for a in range(2):
                    if ready:
                        ready(a)
                    pe.wait_ge(lo_done, g0 + a + 1)
                    s = (g0 + a) % SPLIT
                    for t in range(TT):
                        b = t
                        if a == 0:
                            begin(b)
                        for k in range(4):
                            c = slice(k * 512, (k + 1) * 512)
                            ins = mm3(banks[b][:, :], tok(a_hi, 4 * a + k, t), tok(a_lo, 4 * a + k, t),
                                      w_hi[:, s, c], w_lo[:, s, c], a == 0 and k == 0, a == 1 and k == 3)
                        if a == 1:
                            end((key, t), b, ins, g0 + 1 if t == 1 else None, release(t) if release else None)
                        elif t == 1:
                            ins.then_inc(w_used, 1)
                        for step in hooks.get((a, t), ()):
                            step()
                    if a == 0 and between:
                        between()

            def transpose_job(key, src, wait, gain):
                pe.wait_ge(*wait)
                n = job_no[key] = len(job_no)
                b = 2 + n % 2
                begin(b)
                for k in range(4):
                    ins = pe.transpose(banks[b][:, k * P:(k + 1) * P], src[:, k * P:(k + 1) * P], ident[:, :])
                end(("tr",) + key, b, ins)
                if gain:
                    count["gain"] += 1
                    jobs[key] = (S("x_split"), count["gain"])
                else:
                    jobs[key] = released[b]

            def h_release(m, n):
                return lambda t: (S("h_done"), 4 * m + 2 * n + t + 1)

            def h_jobs(m, n):
                for t in range(TT):
                    transpose_job((m, n, t), h[:, t, n * 512:(n + 1) * 512], (S("h_done"), 4 * m + 2 * n + t + 1), True)

            def ready_from(m):
                def ready(a):
                    wait_job((m, a, 0), (m, a, 1))
                return ready

            def projection(layer, g, bank, between=None):
                pe.wait_ge(S("p_split"), layer + 1)
                pe.wait_ge(lo_done, g + 1)
                for t in range(TT):
                    for n in range(2):
                        b = bank[2 * t + n]
                        begin(b)
                        for k in range(2):
                            c = slice(k * D + n * 512, k * D + (n + 1) * 512)
                            ins = mm3(banks[b][:, :], tok(z_hi, KB - 2 + k, t), tok(z_lo, KB - 2 + k, t),
                                      w_hi[:, g % SPLIT, c], w_lo[:, g % SPLIT, c], k == 0, k == 1)
                        end(("proj", layer, t, n), b, ins, g if t == 1 and n == 1 else None)
                    if t == 0 and between:
                        between()

            def feature_piece(key, g, b, release=None, ready=None):
                pe.wait_ge(lo_done, g + 1)
                begin(b)
                for c in range(2):
                    for k in range(KB):
                        if ready and c == 0 and k % 4 == 0:
                            ready(k // 4)
                        w = slice(k * 256 + c * P, k * 256 + (c + 1) * P)
                        ins = mm3(banks[b][:, c * SEQ:(c + 1) * SEQ], w_hi[:, g % SPLIT, w], w_lo[:, g % SPLIT, w],
                                  x_hi[:, k, :], x_lo[:, k, :], k == 0, k == KB - 1)
                end(key, b, ins, g, release)

            def later(m, n):
                return {(0, 0): [lambda: h_jobs(m, n)]}

            def ffn(layer, m):
                g0 = G[f"ffn{layer}"]

                def hidden_job(i):
                    n = job_no[("hid", layer, i)] = len(job_no)
                    b = 2 + n % 2
                    begin(b)
                    for t in range(TT):
                        pe.wait_ge(S("hidden"), 2 * (GU * layer + i) + t + 1)
                        for k in range(2):
                            ins = pe.transpose(banks[b][:, k * SEQ + t * P:k * SEQ + (t + 1) * P],
                                               hid[:, t, k * P:(k + 1) * P], ident[:, :])
                    end(("tr", "hid", layer, i), b, ins)
                    jobs[("hid", layer, i)] = released[b]

                def down(q):
                    for a in range(2 if q < 5 else 1):
                        i = 2 * q + a
                        g = g0 + (down_at(q) + a if q < 5 else 32)
                        wait_job(("hid", layer, i))
                        pe.wait_ge(lo_done, g + 1)
                        for n in range(2):
                            for t in range(TT):
                                b = 4 + 2 * n + t
                                if i == 0:
                                    begin(b)
                                for k in range(2):
                                    c = slice(k * D + n * 512, k * D + (n + 1) * 512)
                                    zk = (2 * i + k) % KB
                                    ins = mm3(banks[b][:, :], tok(z_hi, zk, t), tok(z_lo, zk, t),
                                              w_hi[:, g % SPLIT, c], w_lo[:, g % SPLIT, c],
                                              i == 0 and k == 0, i == GU - 1 and k == 1)
                                if i == GU - 1:
                                    end(("ffn", layer, n, t), b, ins, g if n == 1 and t == 1 else None,
                                        (S("h_done"), 4 * (m + 1) + 2 * n + t + 1))
                                elif n == 1 and t == 1:
                                    ins.then_inc(w_used, 1)
                        if q == 4 and a == 0:
                            hidden_job(GU - 1)

                for i in range(GU):
                    token_chunk(("gu", layer, i), g0 + gu_at(i), x_hi, x_lo, ready=ready_from(m) if i == 0 else None,
                                release=lambda t: (S("hidden"), 2 * (GU * layer + i) + t + 1),
                                between=(lambda: hidden_job(i - 1)) if i else None,
                                hooks=later(m, 1) if i == 0 else {})
                    if i >= 2 and i % 2 == 0:
                        down(i // 2 - 1)
                down(5)
                h_jobs(m + 1, 0)

            def ple(layer, m):
                g0 = G[f"ple{layer}"]
                token_chunk(("ple", layer, 0), g0, x_hi, x_lo, ready=ready_from(m), hooks=later(m, 1))
                token_chunk(("ple", layer, 1), g0 + 2, x_hi, x_lo, between=lambda: h_jobs(m + 1, 0))

            def keep_warm(times, b):
                begin(b)
                for _ in range(times):
                    pe.transpose(banks[b][:, 0:P], ident[:, :], ident[:, :])

            pe.wait_ge(S("consts"), 4)
            for n in range(2):
                for t in range(TT):
                    transpose_job(("x", n, t), x_s[:, t, n * 512:(n + 1) * 512], (S(("x_scaled", "x_scaled_1")[t]), 1), True)

            def pw1(f):
                feature_piece(("pw1", f), G["pw1"] + f, (0, 1, 4, 7)[f % 4], (S("u"), f + 1),
                              ready=(lambda n: wait_job(("x", n, 0), ("x", n, 1))) if f == 0 else None)

            def conv_taps(f):
                i, b = f - CONV_PE, (2, 3, 5, 6)[f - CONV_PE]
                pe.wait_ge(S("u_split"), i + 1)
                begin(b)
                for q, (t0, nt) in enumerate(TAP_GROUPS):
                    gr = len(TAP_GROUPS) * i + q
                    pe.wait_ge(S("diag_built"), 2 * gr + 2)
                    for j in range(nt):
                        w = slice(i * PADDED + t0 + j, i * PADDED + t0 + j + SEQ)
                        ins = mm3(banks[b][:, 0:SEQ], diag_hi[:, gr % 2, j, :], diag_lo[:, gr % 2, j, :],
                                  flat(z_hi)[:, w], flat(z_lo)[:, w], q == 0 and j == 0, t0 + j == TAPS - 1)
                    if t0 + nt < TAPS:
                        ins.then_inc(S("diag_used"), 1)
                end(("conv", f), b, ins, release=(S("conv_pe"), i + 1))

            def mean_of(f, first=False, last=False):
                if first:
                    begin(0)
                pe.wait_ge(*((S("y_summed"), 1) if f is None else (S("conv_pe"), f - CONV_PE + 1)))
                ins = pe.matmul(banks[0][:, 0:SEQ], inv_d, y_sum if f is None else y[:, f, :], start=first, stop=last)
                if last:
                    end("mean", 0, ins, release=(S("centred"), 4))

            for f in range(6):
                pw1(f)
            conv_taps(4)
            pw1(6)
            conv_taps(5)
            pw1(7)
            conv_taps(6)
            mean_of(4, first=True)
            mean_of(5)
            conv_taps(7)
            mean_of(6)
            mean_of(None)
            mean_of(7, last=True)
            begin(7)
            for f in range(KB):
                pe.wait_ge(S("y_sq"), f // 2 + 1)
                ins = pe.matmul(banks[7][:, 0:SEQ], inv_d, sq[:, f, :], start=f == 0, stop=f == KB - 1)
            end("var", 7, ins, release=(S("y_r"), 1))
            projection(0, G["proj0"], (1, 4, 5, 6))
            keep_warm(32, 7)

            def z_ready(a):
                pe.wait_ge(S("v_split"), 2 * a + 2)
            token_chunk(("pw2", 0), G["pw2"], z_hi, z_lo, ready=z_ready, release=h_release(0, 0))
            token_chunk(("pw2", 1), G["pw2"] + 2, z_hi, z_lo, between=lambda: h_jobs(0, 0), release=h_release(0, 1))
            ffn(0, 0)
            pe.wait_ge(S("ld_attn"), 16 * 3)
            begin(4)
            end("bias", 4, pe.matmul(banks[4][0:HEADS, 0:384], rel_t, onehot_t, start=True, stop=True))
            ple(0, 1)

            def logits(hd):
                def go():
                    j, b0 = hd % 4, 4 + 2 * (hd % 2)
                    for c in range(2):
                        begin(b0 + c)
                        r = slice(c * HD, (c + 1) * HD)
                        pe.matmul(banks[b0 + c][:, 0:SEQ], q_f[r, j, P:SEQ], k_f[r, j, :], start=True, stop=True)
                        ins = pe.matmul(banks[b0 + c][:, SEQ:384], q_f[r, j, 0:P], k_f[r, j, 0:P], start=True, stop=True)
                        end(("lg", hd, c), b0 + c, ins, release=(S("lg_read"), 2 * hd + c + 1))
                return go

            def group_logits(hd):
                def go():
                    hg = hd // 4
                    wait_job(("qk", hg, 0, 0), ("qk", hg, 0, 1), ("qk", hg, 1, 0), ("qk", hg, 1, 1))
                    logits(hd)()
                return go

            def weights(hd):
                def go():
                    pe.wait_ge(S("w_mix"), hd + 1)
                    n = job_no[("w", hd)] = len(job_no)
                    b = 2 + n % 2
                    begin(b)
                    for k in range(3):
                        ins = pe.transpose(banks[b][:, k * P:(k + 1) * P], wt[:, hd % 2, k * P:(k + 1) * P], ident[:, :])
                    end(("tr", "w", hd), b, ins, release=(S("w_copied"), hd + 1))
                return go

            def values(pair):
                def go():
                    b = pair % 2
                    begin(b)
                    pe.wait_ge(S("v_copied"), 2 * (pair // 2) + 2)
                    pe.wait_ge(S("w_copied"), 2 * pair + 2)
                    for i in range(2):
                        hd = 2 * pair + i
                        w, d = w_f[hd], slice(hd * P, (hd + 1) * P)
                        t0, t1 = banks[b][:, i * P:(i + 1) * P], banks[b][:, (2 + i) * P:(3 + i) * P]
                        pe.matmul(t1, w[:, 0:P], vv[:, 0, d], start=True, stop=False)
                        pe.matmul(t1, w[:, P:2 * P], vv[:, 1, d], start=False, stop=True)
                        ins = pe.matmul(t0, w[:, 2 * P:3 * P], vv[:, 0, d], start=True, stop=True)
                    end(("pv", pair), b, ins)
                return go

            def qk_jobs(hg, i):
                def go():
                    for t in range(TT):
                        transpose_job(("qk", hg, i, t), qk_t[:, i, t, :], (S("qk_normed"), 4 * hg + 2 * i + t + 1), False)
                return go

            g = G["qkv"]
            token_chunk(("q", 0), g, x_hi, x_lo, ready=ready_from(2), hooks=later(2, 1))
            token_chunk(("k", 0), g + 2, x_hi, x_lo)
            token_chunk(("q", 1), g + 4, x_hi, x_lo,
                        hooks={(0, 1): [qk_jobs(0, 0)], (1, 0): [qk_jobs(0, 1)], (1, 1): [group_logits(0), logits(1)]})
            token_chunk(("k", 1), g + 6, x_hi, x_lo,
                        hooks={(0, 0): [logits(2)], (0, 1): [weights(0)], (1, 0): [logits(3)]})
            token_chunk(("v", 0), g + 8, x_hi, x_lo, release=lambda t: (S("v_copied"), t + 1),
                        hooks={(0, 0): [weights(1)], (0, 1): [qk_jobs(1, 0)], (1, 0): [weights(2)]})
            token_chunk(("v", 1), g + 10, x_hi, x_lo, release=lambda t: (S("v_copied"), t + 3),
                        hooks={(0, 0): [qk_jobs(1, 1)], (0, 1): [group_logits(4), logits(5)],
                               (1, 0): [weights(3), logits(6)], (1, 1): [weights(4), logits(7)]})
            for step in (values(0), weights(5), values(1), weights(6), values(2), weights(7), values(3)):
                step()

            def o_jobs(n):
                for t in range(TT):
                    transpose_job(("o", n, t), oo[:, t, n * 512:(n + 1) * 512], (S("o_normed"), 2 * n + t + 1), False)

            projection(1, G["proj1"], (4, 5, 6, 7), between=lambda: o_jobs(0))
            def o_ready(a):
                wait_job(("o", a, 0), ("o", a, 1))
            token_chunk(("wo", 0), G["wo"], z_hi, z_lo, ready=o_ready, hooks={(0, 0): [lambda: o_jobs(1)]}, release=h_release(3, 0))
            token_chunk(("wo", 1), G["wo"] + 2, z_hi, z_lo, between=lambda: h_jobs(3, 0), release=h_release(3, 1))
            ffn(1, 3)
            ple(1, 4)

            for name in ("av", "au"):
                for n in range(2):
                    token_chunk((name, n), G[name] + 2 * n, x_hi, x_lo,
                                ready=ready_from(5) if name == "av" and n == 0 else None,
                                hooks=later(5, 1) if name == "av" and n == 0 else {})
            begin(4)
            pe.wait_ge(S("diag"), 2)
            for t in range(TT):
                ins = pe.matmul(banks[4][:, t * P:(t + 1) * P], ones[:, :], diag[:, t, :], start=True, stop=True)
            end("r_row", 4, ins)
            token_chunk(("az", 0), G["az"], x_hi, x_lo)
            pe.wait_ge(S("sgu_masked"), 1)
            pe.wait_ge(S("sgu_ready"), 2)
            for t in range(TT):
                for q in range(2):
                    b = 4 + 2 * t + q
                    begin(b)
                    for j in range(4):
                        gi = 4 * q + j
                        ins = pe.matmul(banks[b][:, j * P:(j + 1) * P], sgu_t[:, gi, :],
                                        av[:, t, gi * P:(gi + 1) * P], start=True, stop=True)
                    end(("mixed", t, q), b, ins)
            token_chunk(("az", 1), G["az"] + 2, x_hi, x_lo)

            def y_jobs(name, src, n):
                def go():
                    for t in range(TT):
                        transpose_job((name, n, t), src[:, t, n * 512:(n + 1) * 512], (S(name), 2 * n + t + 1), False)
                return go

            def job_ready(name):
                def ready(a):
                    wait_job((name, a, 0), (name, a, 1))
                return ready

            token_chunk(("ga", 0), G["ga"], x_hi, x_lo)
            token_chunk(("ga", 1), G["ga"] + 2, x_hi, x_lo, between=y_jobs("ya", au, 0))
            for n in range(2):
                token_chunk(("wa", n), G["wa"] + 2 * n, z_hi, z_lo, ready=job_ready("ya") if n == 0 else None,
                            hooks={(0, 0): [y_jobs("ya", au, 1)]} if n == 0 else {})

            for n in range(2):
                token_chunk(("bp", n), G["bp"] + 2 * n, x_hi, x_lo)
            token_chunk(("bz", 0), G["bz"], x_hi, x_lo)
            for n in range(2):
                for t in range(TT):
                    pe.wait_ge(*filled[(("bp", n), t)][3])
            pe.wait_ge(S("ld_pm"), 16)
            for f in range(KB):
                b = 4 + f // 2
                if f % 2 == 0:
                    begin(b)
                w = f // 2
                dst = banks[b][:, (f % 2) * SEQ:(f % 2 + 1) * SEQ]
                fs = slice(f * P, (f + 1) * P)
                pe.matmul(dst, av[:, 0, fs], pm[:, w, 0:SEQ], start=True, stop=False)
                ins = pe.matmul(dst[:, P:SEQ], av[:, 1, fs], pm[:, w, SEQ:384], start=False, stop=True)
                if f % 2:
                    end(("pool", w), b, ins)
            token_chunk(("bz", 1), G["bz"] + 2, x_hi, x_lo)
            g = G["poolw"]
            pe.wait_ge(lo_done, g + 1)
            for w in range(4):
                pe.wait_ge(*filled[("pool", w)][3])
            for n in range(2):
                for t in range(TT):
                    b = 4 * n + t
                    begin(b)
                    for w in (2 * n, 2 * n + 1):
                        for k in range(2):
                            c = slice((2 * w + k) * 256, (2 * w + k + 1) * 256)
                            ins = mm3(banks[b][:, (w % 2) * 256:(w % 2 + 1) * 256], tok(z_hi, 2 * w + k, t),
                                      tok(z_lo, 2 * w + k, t), w_hi[:, g % SPLIT, c], w_lo[:, g % SPLIT, c],
                                      k == 0, k == 1)
                    end(("pooled", n, t), b, ins, g if n == 1 and t == 1 else None)
            token_chunk(("gb", 0), G["gb"], x_hi, x_lo)
            token_chunk(("gb", 1), G["gb"] + 2, x_hi, x_lo, between=y_jobs("yb", au, 0))
            for n in range(2):
                token_chunk(("wb", n), G["wb"] + 2 * n, z_hi, z_lo, ready=job_ready("yb") if n == 0 else None,
                            hooks={(0, 0): [y_jobs("yb", au, 1)]} if n == 0 else {})

            for j in range(KB):
                for a in range(2):
                    feature_piece(("cc", j, a), G["cc"] + 2 * j + a, 4 + (2 * j + a) % 4,
                                  (S("c_zr"), j + 1) if a else None)
            for n in range(2):
                token_chunk(("gc", n), G["gc"] + 2 * n, x_hi, x_lo)

            def c_ready(a):
                pe.wait_ge(S("yc_split"), 4 * a + 4)
            token_chunk(("wc", 0), G["wc"], z_hi, z_lo, ready=c_ready)
            token_chunk(("wc", 1), G["wc"] + 2, z_hi, z_lo, between=y_jobs("merged", merged, 0))
            for n in range(2):
                token_chunk(("wout", n), G["wout"] + 2 * n, x_hi, x_lo, ready=job_ready("merged") if n == 0 else None,
                            hooks={(0, 0): [y_jobs("merged", merged, 1)]} if n == 0 else {},
                            release=h_release(6, n))

        def take(eng, key):
            s, v, b, _ = filled[key]
            eng.wait_ge(s, v)
            return banks[b], bank_free[b]

        def freed(eng, key):
            eng.wait_ge(*filled[key][3])

        @block.gpsimd
        def _(pool):
            n = [0]

            def link(ins):
                n[0] += 1
                ins.then_inc(pool_step, 1)
                pool.wait_ge(pool_step, n[0])

            link(pool.memset(ident[:, :], 0.0))
            pool.affine_select(out=ident[:, :], in_=ident[:, :], compare_op=ALU.not_equal, fill=1.0, base=0,
                               pattern=[[-1, P]], channel_multiplier=1).then_inc(S("consts"), 1)
            pool.memset(ones[:, :], 1.0).then_inc(S("consts"), 1)
            pool.memset(inv_d, 1.0 / D).then_inc(S("consts"), 1)
            pool.memset(u_pad[:, :, 0:TAPS - 1], 0.0).then_inc(S("consts"), 1)
            pool.wait_ge(S("taps_split"), 1)
            for gr in range((KB - CONV_PE) * len(TAP_GROUPS)):
                i, (t0, nt) = gr // len(TAP_GROUPS), TAP_GROUPS[gr % len(TAP_GROUPS)]
                if gr >= 2:
                    f, q = divmod(gr - 2, len(TAP_GROUPS))
                    if q < len(TAP_GROUPS) - 1:
                        pool.wait_ge(S("diag_used"), (len(TAP_GROUPS) - 1) * f + q + 1)
                    else:
                        take(pool, ("conv", CONV_PE + f))
                for taps, dst in ((taps_hi, diag_hi), (taps_lo, diag_lo)):
                    pool.affine_select(out=dst[:, gr % 2, 0:nt, :],
                                       in_=taps[:, i, t0:t0 + nt].unsqueeze(2).to_broadcast([P, nt, P]),
                                       compare_op=ALU.is_equal, fill=0.0, base=0, pattern=[[0, nt], [1, P]],
                                       channel_multiplier=-1).then_inc(S("diag_built"), 1)
            pool.wait_ge(S("x_scaled"), 1)
            pool.wait_ge(S("x_scaled_1"), 1)
            pool.dma_start(row_b2, bcast(rows, 0)).then_inc(S("ld_b2"), 16)
            pool.wait_ge(S("ld_b2"), 16)
            for t in range(TT):
                pool.tensor_tensor(h[:, t, :], h[:, t, :], row_b2, ALU.add).then_inc(S("h_biased"), 1)

            pool.wait_ge(S("h_done"), 4)
            pool.dma_start(rel_t, rel).then_inc(S("ld_attn"), 16)
            pool.dma_start(onehot_t, onehot).then_inc(S("ld_attn"), 16)
            pool.dma_start(lam_t, bass.AP(lam_rows.tensor, 0, [[0, P], [HD, 4], [1, HD]])).then_inc(S("ld_attn"), 16)
            pool.wait_ge(S("bias_row"), 2)
            pool.dma_start(toep, bias_row.unsqueeze(1).to_broadcast([HEADS, P, 384])).then_inc(S("toep_out"), 16)
            pool.wait_ge(S("toep_out"), 16)
            pool.dma_start(toep_t[:, :, 0:SEQ], bass.AP(toep.tensor, P - 1, [[383, P], [P * 384, HEADS], [1, SEQ]])) \
                .then_inc(S("ld_toep"), 16)
            pool.dma_start(toep_t[:, :, SEQ:384], bass.AP(toep.tensor, 2 * P - 1, [[383, P], [P * 384, HEADS], [1, P]])) \
                .then_inc(S("ld_toep"), 16)
            pool.wait_ge(S("h_done"), 12)
            pool.dma_start(p_t1, p_feat[1]).then_inc(S("ld_p1"), 16)
            pool.wait_ge(S("h_done"), 16)
            pool.dma_start(ln_row, bcast(rows, 1, 2)).then_inc(S("ld_sgu"), 16)
            pool.dma_start(sgu_t, sgu_w).then_inc(S("ld_sgu"), 16)
            pool.wait_ge(S("ld_sgu"), 32)
            pool.memset(sgu_t[HD:P, :, 0:HD], 0.0).then_inc(S("sgu_masked"), 1)
            pool.wait_ge(S("h_done"), 24)
            pool.dma_start(pm, pool_m).then_inc(S("ld_pm"), 16)
            pool.wait_ge(S("sgu_ready"), 2)
            pool.dma_start(pool_row, bcast(rows, 3, 2)).then_inc(S("ld_pool"), 16)
            for t in range(TT):
                for q in range(2):
                    freed(pool, ("mixed", t, q))
            pool.dma_start(final_row, bcast(rows, 5)).then_inc(S("ld_final"), 16)

        @block.scalar
        def _(act):
            fed = [0]

            def feed(to):
                while fed[0] <= min(to, NPIECE - 1):
                    g = fed[0]
                    act.wait_ge(raw_loaded[g % RAW], 16 * (g // RAW + 1))
                    if g >= SPLIT:
                        act.wait_ge(w_used, g - SPLIT + 1)
                    act.activation(w_hi[:, g % SPLIT, :], raw[:, g % RAW, :], ACT.Copy).then_inc(hi_done, 1)
                    fed[0] += 1

            def ahead(g):
                feed(g + SPLIT - 1)

            tables = [0]

            def table(func):
                c = 10 + tables[0]
                tables[0] += 1
                act.activation(st[:, c:c + 1], ident[:, 0:1], func)

            def split_hi(key, dst, k0, w):
                freed(act, ("tr",) + key)
                src = stage[:, job_no[key] % 2, :].rearrange("p (k c) -> p k c", k=4)
                act.activation(dst[:, k0:k0 + 4, w], src, ACT.Copy).then_inc(S("t_hi"), 1)

            def h_split(m, n):
                for t in range(TT):
                    split_hi((m, n, t), x_hi, 4 * n, slice(t * P, (t + 1) * P))

            def h_stats(m, n):
                for t in range(TT):
                    act.wait_ge(S("h_done"), 4 * m + 2 * n + t + 1)
                    if 4 * m + 2 * n >= 2:
                        act.wait_ge(S("h_ss"), 4 * m + 2 * n + t - 1)
                    act.activation((junk if m < 6 else junk_f)[:, t * 512:(t + 1) * 512], h[:, t, n * 512:(n + 1) * 512],
                                   ACT.Square, accum_out=st[:, 4 * (m % 2) + 2 * n + t:4 * (m % 2) + 2 * n + t + 1]) \
                       .then_inc(S("h_ss"), 1)

            def plain_hi(key, dst, k0, w):
                bank, _ = take(act, ("tr",) + key)
                src = bank[:, :].rearrange("p (k c) -> p k c", k=4)
                act.activation(dst[:, k0:k0 + 4, w], src, ACT.Copy).then_inc(S("t_hi"), 1)

            def ffn(layer, m):
                g0 = G[f"ffn{layer}"]

                def hidden_hi(i):
                    bank, _ = take(act, ("tr", "hid", layer, i))
                    k0 = (2 * i) % KB
                    act.activation(z_hi[:, k0:k0 + 2, :], bank[:, :].rearrange("p (k s) -> p k s", k=2),
                                   ACT.Copy).then_inc(S("t_hi"), 1)

                for i in range(GU):
                    g = g0 + gu_at(i)
                    ahead(g)
                    if i:
                        hidden_hi(i - 1)
                        ahead(g + 1)
                    else:
                        act.wait_ge(S("r_done"), m + 1)
                    for t in range(TT):
                        bank, _ = take(act, (("gu", layer, i), t))
                        if i:
                            act.wait_ge(S("hidden"), 2 * (GU * layer + i - 1) + t + 1)
                        act.activation(silu_t[:, t, :], bank[:, 0:256], ACT.Silu,
                                       scale=st2[:, 2 * m + t:2 * m + t + 1]).then_inc(S("silu"), 1)
                        if i == 0 and t == 0:
                            ahead(g + 1)
                    if i >= 2 and i % 2 == 0:
                        ahead(g0 + down_at(i // 2 - 1))
                        ahead(g0 + down_at(i // 2 - 1) + 1)
                hidden_hi(GU - 1)
                ahead(g0 + 32)
                h_split(m + 1, 0)
                h_stats(m + 1, 0)
                h_stats(m + 1, 1)
                table(ACT.Sigmoid)
                h_split(m + 1, 1)

            gates = [0]

            def ple(layer, m):
                g0 = G[f"ple{layer}"]
                for n in range(2):
                    ahead(g0 + 2 * n)
                    if n:
                        h_split(m + 1, 0)
                        h_stats(m + 1, 0)
                    ahead(g0 + 2 * n + 1)
                    for t in range(TT):
                        bank, free = take(act, (("ple", layer, n), t))
                        if n == 0 and t == 0:
                            act.wait_ge(S("r_done"), m + 1)
                        if n:
                            act.wait_ge(S("gate_used"), 4 * layer + t + 1)
                        act.activation(gate_t[:, t, :], bank[:, :], ACT.Sigmoid,
                                       scale=st2[:, 2 * m + t:2 * m + t + 1]).then_inc(free, 1)
                h_stats(m + 1, 1)
                h_split(m + 1, 1)

            def p_split(layer):
                act.wait_ge(S(f"ld_p{layer}"), 16)
                act.activation(z_hi[:, KB - 2:KB, :], p_t1 if layer else p_t0, ACT.Copy).then_inc(S("p_hi"), 1)

            def proj_copy(layer):
                for t in range(TT):
                    for n in range(2):
                        bank, free = take(act, ("proj", layer, t, n))
                        act.activation(pp[:, t, n * 512:(n + 1) * 512], bank[:, :], ACT.Copy).then_inc(free, 1)

            act.dma_start(prm[:, :], par).then_inc(S("ld_par"), 16)
            for t in range(TT):
                act.wait_ge(S(f"ld_h{t}"), 16)
                act.activation(sq_x[:, t, :], h[:, t, :], ACT.Square, accum_out=st[:, 80 + t:81 + t]) \
                   .then_inc(S("x_ss"), 1)
            act.wait_ge(S("ld_par"), 16)
            taps = prm[:, PCOL["dw_w"] + CONV_PE * TAPS:PCOL["dw_w"] + KB * TAPS]
            act.activation(taps_hi.rearrange("p a b -> p (a b)").bitcast(F32R), taps, ACT.Copy).then_inc(S("taps_hi"), 1)
            act.wait_ge(S("x_r"), 1)
            act.activation(x_s[:, 0, :], h[:, 0, :], ACT.Copy, scale=st2[:, 48:49]).then_inc(S("x_scaled"), 1)
            act.dma_start(p_t0, p_feat[0]).then_inc(S("ld_p0"), 16)
            feed(0)
            h_split("x", 0)
            h_split("x", 1)
            feed(2)

            def u_high(f):
                act.wait_ge(S("u"), f + 1)
                w = slice((f - CONV_PE) * PADDED, (f - CONV_PE + 1) * PADDED)
                act.activation(flat(z_hi)[:, w], u_pad[:, f, :], ACT.Copy).then_inc(S("u_hi"), 1)

            def conv_out(f):
                bank, _ = take(act, ("conv", f))
                act.activation(y[:, f, :], bank[:, 0:SEQ], ACT.Identity, bias=col("dw_b", f)).then_inc(S("conv_pe"), 1)

            for f in range(KB):
                ahead(G["pw1"] + f)
                bank, _ = take(act, ("pw1", f))
                if f >= 2:
                    act.wait_ge(S("u"), f - 1)
                act.activation(sig[:, f % 2, :], bank[:, SEQ:2 * SEQ], ACT.Sigmoid, bias=col("b_g", f)).then_inc(S("sig"), 1)
                if f >= CONV_PE:
                    u_high(f)
                if f == 0:
                    p_split(0)
                if f >= 6:
                    conv_out(f - 2)
            ahead(G["proj0"])
            conv_out(6)
            conv_out(7)
            for f in range(4):
                act.wait_ge(S("centred"), f + 1)
                act.activation(sq[:, 2 * f:2 * f + 2, :], y[:, 2 * f:2 * f + 2, :], ACT.Square).then_inc(S("y_sq"), 1)
            for t, n_ in ((0, 0), (0, 1)):
                bank, free = take(act, ("proj", 0, t, n_))
                act.activation(pp[:, t, n_ * 512:(n_ + 1) * 512], bank[:, :], ACT.Copy).then_inc(free, 1)
            for f in range(KB):
                act.wait_ge(S("scaled"), f // 2 + 1)
                act.activation(v_f[:, f, :], y[:, f, :], ACT.Silu, scale=col("ln_g", f), bias=col("ln_b", f)) \
                   .then_inc(S("v_act"), 1)
                if f % 2:
                    if f == KB - 1:
                        take(act, ("proj", 0, 1, 1))
                    act.wait_ge(S("v_act"), f + 1)
                    act.activation(z_hi[:, f - 1:f + 1, :], v_f[:, f - 1:f + 1, :], ACT.Copy).then_inc(S("v_hi"), 1)
            for t, n_ in ((1, 0), (1, 1)):
                bank, free = take(act, ("proj", 0, t, n_))
                act.activation(pp[:, t, n_ * 512:(n_ + 1) * 512], bank[:, :], ACT.Copy).then_inc(free, 1)
            ahead(G["pw2"] + 2)
            ahead(G["pw2"] + 3)
            h_split(0, 0)
            h_stats(0, 0)
            h_stats(0, 1)
            h_split(0, 1)
            ffn(0, 0)
            ple(0, 1)

            ahead(G["qkv"])
            act.wait_ge(S("lam_sum"), 1)
            act.activation(st[:, 90:92], st[:, 88:90], ACT.Exp).then_inc(S("lam_exp"), 1)
            p_split(1)
            feed(G["qkv"] + 3)
            act.wait_ge(S("r_done"), 3)
            act.wait_ge(S("attn_small"), 3)
            g = G["qkv"]

            def qk_evac(hg, i):
                for t in range(TT):
                    bank, free = take(act, (("qk"[i], hg), t))
                    if hg:
                        freed(act, ("tr", "qk", 0, i, t))
                    act.activation(qk_t[:, i, t, :], bank[:, :], ACT.Copy, scale=st2[:, 4 + t:5 + t]).then_inc(free, 1)
                for t in range(TT):
                    freed(act, (("qk"[i], hg), t))
                    if 2 * hg + i:
                        act.wait_ge(S("qk_ss"), 4 * hg + 2 * i + t - 1)
                    act.activation(sq_t[:, t, :], qk_t[:, i, t, :], ACT.Square).then_inc(S("qk_sq"), 1)

            def qk_features(hg, i):
                for t in range(TT):
                    bank, free = take(act, ("tr", "qk", hg, i, t))
                    if hg:
                        take(act, ("lg", 3, 1))
                    act.activation((q_f, k_f)[i][:, :, t * P:(t + 1) * P],
                                   bank[:, :].rearrange("p (j s) -> p j s", j=4), ACT.Copy,
                                   scale=st[:, 92 + i:93 + i]).then_inc(free, 1)

            def exps(hd):
                act.wait_ge(S("lg_read"), 2 * hd + 2)
                v, c0 = lg[hd % 2], 4 * (hd % 2)
                for lo, w, c in ((0, SEQ, 2), (SEQ, SEQ, 3), (2 * SEQ, P, 0), (2 * SEQ + P, P, 1)):
                    ins = act.activation(v[:, lo:lo + w], v[:, lo:lo + w], ACT.Exp, scale=-1.0,
                                         bias=st[:, 64 + c0 + c:65 + c0 + c], accum_out=st[:, 72 + c0 + c:73 + c0 + c])
                ins.then_inc(S("exps"), 1)

            def weights(hd):
                bank, free = take(act, ("tr", "w", hd))
                act.activation(w_f[hd], bank[:, 0:384], ACT.Copy).then_inc(S("w_copied"), 1)

            def v_evac(hg):
                for t in range(TT):
                    bank, free = take(act, (("v", hg), t))
                    act.activation(vv[:, t, hg * 512:(hg + 1) * 512], bank[:, :], ACT.Copy, scale=st2[:, 4 + t:5 + t]) \
                       .then_inc(S("v_copied"), 1)

            def o_squares(pair):
                freed(act, ("pv", pair))
                for j in range(4):
                    t, hd, n_ = j // 2, 2 * pair + j % 2, 4 * pair + j
                    if n_ >= 2:
                        act.wait_ge(S("o_ss"), n_ - 1)
                    act.activation(sq_o[:, j % 2, :], oo[:, t, hd * P:(hd + 1) * P], ACT.Square,
                                   accum_out=st[:, 48 + 8 * (hd // 4) + 4 * t + hd % 4:
                                                49 + 8 * (hd // 4) + 4 * t + hd % 4]).then_inc(S("o_ss"), 1)

            def o_hi(n):
                for t in range(TT):
                    bank, _ = take(act, ("tr", "o", n, t))
                    act.activation(z_hi[:, 4 * n:4 * n + 4, t * P:(t + 1) * P], bank[:, :].rearrange("p (k c) -> p k c", k=4),
                                   ACT.Copy, scale=st[:, 95:96]).then_inc(S("t_hi"), 1)

            feed(g + 3)
            qk_evac(0, 0)
            feed(g + 5)
            qk_evac(0, 1)
            feed(g + 6)
            qk_features(0, 0)
            feed(g + 7)
            qk_features(0, 1)
            qk_evac(1, 0)
            feed(g + 8)
            exps(0)
            exps(1)
            weights(0)
            exps(2)
            feed(g + 9)
            qk_evac(1, 1)
            weights(1)
            feed(g + 10)
            exps(3)
            qk_features(1, 0)
            v_evac(0)
            weights(2)
            feed(g + 11)
            qk_features(1, 1)
            feed(g + 12)
            weights(3)
            exps(4)
            exps(5)
            weights(4)
            v_evac(1)
            exps(6)
            weights(5)
            exps(7)
            weights(6)
            o_squares(0)
            weights(7)
            o_squares(1)
            feed(g + 13)
            o_squares(2)
            o_squares(3)
            o_hi(0)
            ahead(G["proj1"])
            proj_copy(1)
            o_hi(1)
            ahead(G["wo"] + 2)
            ahead(G["wo"] + 3)
            h_split(3, 0)
            h_stats(3, 0)
            h_stats(3, 1)
            table(ACT.Silu)
            h_split(3, 1)
            ffn(1, 3)
            ple(1, 4)

            ahead(G["av"] + 1)
            table(ACT.Gelu_apprx_tanh)
            act.wait_ge(S("r_done"), 6)

            def evac(name, func, dst, extra=None, accum=None, sig=None):
                for n in range(2):
                    ahead(G[name] + 2 * n + 1)
                    for t in range(TT):
                        bank, free = take(act, ((name, n), t))
                        if extra:
                            extra(n, t)
                        act.activation(dst[:, t, n * 512:(n + 1) * 512], bank[:, :], func, scale=st2[:, 10 + t:11 + t],
                                       **({"accum_out": accum[:, 2 * t + n:2 * t + n + 1]} if accum is not None else {})) \
                           .then_inc(free, 1)

            evac("av", ACT.Gelu_apprx_tanh, av, accum=st[:, 16:20])
            ahead(G["au"])
            act.wait_ge(S("v_mean"), 1)
            for t in range(TT):
                act.activation(junk_v[:, t, :], av[:, t, :], ACT.Square, bias=st[:, 20 + t:21 + t],
                               accum_out=st[:, 22 + t:23 + t]).then_inc(S("v_var"), 1)
            evac("au", ACT.Gelu_apprx_tanh, au)
            evac("az", ACT.Silu, az)
            for n in range(2):
                ahead(G["ga"] + 2 * n)
                if n:
                    for t in range(TT):
                        plain_hi(("ya", 0, t), z_hi, 0, slice(t * P, (t + 1) * P))
                ahead(G["ga"] + 2 * n + 1)
                for t in range(TT):
                    bank, free = take(act, (("ga", n), t))
                    act.activation(gate[:, t, n * 512:(n + 1) * 512], bank[:, :], ACT.Sigmoid,
                                   scale=st2[:, 10 + t:11 + t]).then_inc(free, 1)
            for t in range(TT):
                plain_hi(("ya", 1, t), z_hi, 4, slice(t * P, (t + 1) * P))
            ahead(G["wa"] + 3)
            evac("bp", ACT.Copy, av, extra=lambda n, t: freed(act, ("mixed", 1, 1)))
            for n in range(2):
                if n:
                    for w in range(4):
                        bank, _ = take(act, ("pool", w))
                        act.activation(z_hi[:, 2 * w:2 * w + 2, :], bank[:, :].rearrange("p (k s) -> p k s", k=2),
                                       ACT.Copy).then_inc(S("t_hi"), 1)
                ahead(G["bz"] + 2 * n + 1)
                for t in range(TT):
                    bank, free = take(act, (("bz", n), t))
                    if n == 0 and t == 0:
                        act.wait_ge(S("ya"), 4)
                    act.activation(az[:, t, n * 512:(n + 1) * 512], bank[:, :], ACT.Silu,
                                   scale=st2[:, 10 + t:11 + t]).then_inc(free, 1)
            ahead(G["poolw"])
            for n in range(2):
                ahead(G["gb"] + 2 * n)
                if n:
                    for t in range(TT):
                        plain_hi(("yb", 0, t), z_hi, 0, slice(t * P, (t + 1) * P))
                ahead(G["gb"] + 2 * n + 1)
                for t in range(TT):
                    bank, free = take(act, (("gb", n), t))
                    freed(act, (("wa", n), t))
                    act.activation(gate[:, t, n * 512:(n + 1) * 512], bank[:, :], ACT.Sigmoid,
                                   scale=st2[:, 10 + t:11 + t]).then_inc(free, 1)
            for t in range(TT):
                plain_hi(("yb", 1, t), z_hi, 4, slice(t * P, (t + 1) * P))
            ahead(G["wb"] + 3)
            act.wait_ge(S("c_zero"), 1)
            for j in range(KB):
                g = G["cc"] + 2 * j
                ahead(g)
                s = j % 2
                bank, free = take(act, ("cc", j, 0))
                if j >= 2:
                    act.wait_ge(S("yc_split"), j - 1)
                act.activation(c_h[:, s, :], bank[:, 0:SEQ], ACT.Copy).then_inc(S("c_hc"), 1)
                ahead(g + 1)
                act.wait_ge(S("c_zr"), j + 1)
                act.activation(c_s[:, s, :], c_z[:, s, :], ACT.Silu).then_inc(S("c_silu"), 1)
                act.wait_ge(S("yc"), j + 1)
                act.activation(z_hi[:, j, :], c_f[:, s, :], ACT.Copy).then_inc(S("yc_hi"), 1)
            for n in range(2):
                ahead(G["gc"] + 2 * n + 1)
                for t in range(TT):
                    bank, free = take(act, (("gc", n), t))
                    freed(act, (("wb", n), t))
                    act.activation(gate[:, t, n * 512:(n + 1) * 512], bank[:, :], ACT.Sigmoid,
                                   scale=st2[:, 10 + t:11 + t]).then_inc(free, 1)
            ahead(G["wc"] + 2)
            for t in range(TT):
                plain_hi(("merged", 0, t), x_hi, 0, slice(t * P, (t + 1) * P))
            ahead(G["wc"] + 3)
            for t in range(TT):
                plain_hi(("merged", 1, t), x_hi, 4, slice(t * P, (t + 1) * P))
            ahead(NPIECE)
            h_stats(6, 0)
            h_stats(6, 1)
            act.wait_ge(S("out_gain"), 3)
            act.wait_ge(S("out_r"), 1)
            act.activation(av[:, 0, :], av[:, 0, :], ACT.Copy, scale=st2[:, 12:13]).then_inc(S("out_ready_0"), 1)

        @block.vector
        def _(dve):
            fed = [0]
            n = [0]

            def link(ins):
                n[0] += 1
                ins.then_inc(dve_step, 1)
                dve.wait_ge(dve_step, n[0])

            def feed(to):
                while fed[0] <= min(to, NPIECE - 1):
                    g = fed[0]
                    dve.wait_ge(hi_done, g + 1)
                    dve.tensor_tensor(w_lo[:, g % SPLIT, :], raw[:, g % RAW, :], w_hi[:, g % SPLIT, :].bitcast(F32),
                                      ALU.subtract).then_inc(lo_done, 1)
                    fed[0] += 1

            def ahead(g):
                feed(g + SPLIT - 1)

            def rsqrt(src, v, yy, tmp, scale, eps, done, fill={}):
                if not isinstance(src, list):
                    src, v, yy, tmp = [src], [v], [yy], [tmp]
                ts, tt, stt = dve.tensor_scalar, dve.tensor_tensor, dve.scalar_tensor_tensor
                steps = [lambda i: ts(v[i], src[i], scale, eps, ALU.mult, ALU.add),
                         lambda i: ts(yy[i].bitcast(I32), v[i].bitcast(I32), 1, None, ALU.logical_shift_right),
                         lambda i: ts(yy[i].bitcast(I32), yy[i].bitcast(I32), -1.0, float(0x5F3759DF), ALU.mult, ALU.add)]
                steps += [lambda i: tt(tmp[i], yy[i], yy[i], ALU.mult),
                          lambda i: stt(out=tmp[i], in0=v[i], scalar=-0.5, in1=tmp[i], op0=ALU.mult, op1=ALU.mult),
                          lambda i: stt(out=yy[i], in0=tmp[i], scalar=1.5, in1=yy[i], op0=ALU.add, op1=ALU.mult)] * 3
                at = [0] * len(src)
                for j, step in enumerate(steps):
                    for i in range(len(src)):
                        if j:
                            dve.wait_ge(dve_step, at[i])
                        ins = step(i)
                        if j == len(steps) - 1 and i == len(src) - 1:
                            ins.then_inc(done, 1)
                        else:
                            n[0] += 1
                            at[i] = n[0]
                            ins.then_inc(dve_step, 1)
                    if j in fill:
                        fill[j]()
                if len(src) > 1:
                    dve.wait_ge(dve_step, n[0])

            hi_count = [0]
            stage_read = [0, 0]
            split_count = [0]

            def gain_block(key, gain):
                bank, free = take(dve, ("tr",) + key)
                s = job_no[key] % 2
                if stage_read[s]:
                    dve.wait_ge(S("x_split"), stage_read[s])
                dve.tensor_tensor(stage[:, s, :].rearrange("p (k c) -> p k c", k=4),
                                  bank[:, :].rearrange("p (k c) -> p k c", k=4),
                                  gain.unsqueeze(2).to_broadcast([P, 4, P]), ALU.mult).then_inc(free, 1)

            def split_lo(key, hi, lo, k0, w):
                s = job_no[key] % 2
                hi_count[0] += 1
                split_count[0] += 1
                stage_read[s] = split_count[0]
                dve.wait_ge(S("t_hi"), hi_count[0])
                dve.tensor_tensor(lo[:, k0:k0 + 4, w], stage[:, s, :].rearrange("p (k c) -> p k c", k=4),
                                  hi[:, k0:k0 + 4, w].bitcast(F32), ALU.subtract).then_inc(S("x_split"), 1)

            def h_split(m, n, gname):
                for t in range(TT):
                    gain_block((m, n, t), col(gname, 4 * n, 4))
                for t in range(TT):
                    split_lo((m, n, t), x_hi, x_lo, 4 * n, slice(t * P, (t + 1) * P))

            def h_factor(m, fill={}):
                dve.wait_ge(S("h_ss"), 4 * m + 4)
                c = 4 * (m % 2)
                link(dve.tensor_tensor(st[:, 8:10], st[:, c:c + 2], st[:, c + 2:c + 4], ALU.add))
                c = slice(2 * m, 2 * m + 2)
                rsqrt(st[:, 8:10], st2[:, 60:62], st2[:, c], st2[:, 62:64], 1.0 / D, EPS, S("r_done"),
                      fill)

            def h_split_factor(m, gname):
                h_factor(m, {9: lambda: h_split(m, 1, gname)})

            def plain_lo(key, hi, lo, k0, w):
                bank, free = take(dve, ("tr",) + key)
                hi_count[0] += 1
                dve.wait_ge(S("t_hi"), hi_count[0])
                dve.tensor_tensor(lo[:, k0:k0 + 4, w], bank[:, :].rearrange("p (k c) -> p k c", k=4),
                                  hi[:, k0:k0 + 4, w].bitcast(F32), ALU.subtract).then_inc(free, 1)

            def ffn(layer, m, gname):
                g0 = G[f"ffn{layer}"]

                def hidden_lo(i):
                    bank, free = take(dve, ("tr", "hid", layer, i))
                    k0 = (2 * i) % KB
                    hi_count[0] += 1
                    dve.wait_ge(S("t_hi"), hi_count[0])
                    dve.tensor_tensor(z_lo[:, k0:k0 + 2, :], bank[:, :].rearrange("p (k s) -> p k s", k=2),
                                      z_hi[:, k0:k0 + 2, :].bitcast(F32), ALU.subtract).then_inc(free, 1)

                dve.wait_ge(S("r_done"), m + 1)
                for i in range(GU):
                    g = g0 + gu_at(i)
                    ahead(g)
                    if i:
                        hidden_lo(i - 1)
                        ahead(g + 1)
                    for t in range(TT):
                        bank, free = take(dve, (("gu", layer, i), t))
                        dve.wait_ge(S("silu"), 2 * (GU * layer + i) + t + 1)
                        dve.scalar_tensor_tensor(out=hid[:, t, :], in0=bank[:, 256:512],
                                                 scalar=st2[:, 2 * m + t:2 * m + t + 1], in1=silu_t[:, t, :],
                                                 op0=ALU.mult, op1=ALU.mult).then_inc(S("hidden"), 1)
                        if i == 0 and t == 0:
                            ahead(g + 1)
                    if i >= 2 and i % 2 == 0:
                        ahead(g0 + down_at(i // 2 - 1))
                        ahead(g0 + down_at(i // 2 - 1) + 1)
                hidden_lo(GU - 1)
                ahead(g0 + 32)
                for n in range(2):
                    for t in range(TT):
                        add_h(("ffn", layer, n, t), n, t)
                    if n == 0:
                        h_split(m + 1, 0, gname)
                h_split_factor(m + 1, gname)

            def add_h(key, n, t):
                bank, free = take(dve, key)
                hs = h[:, t, n * 512:(n + 1) * 512]
                dve.tensor_tensor(hs, hs, bank[:, :], ALU.add).then_inc(S("h_done"), 1)

            def ple(layer, m, gname):
                g0 = G[f"ple{layer}"]
                for n in range(2):
                    ahead(g0 + 2 * n)
                    if n:
                        h_split(m + 1, 0, gname)
                    ahead(g0 + 2 * n + 1)
                    for t in range(TT):
                        freed(dve, (("ple", layer, n), t))
                        c = slice(n * 512, (n + 1) * 512)
                        dve.tensor_tensor(prod_t[:, t, :], gate_t[:, t, :], pp[:, t, c], ALU.mult).then_inc(S("gate_used"), 1)
                        dve.wait_ge(S("gate_used"), 4 * layer + 2 * n + t + 1)
                        dve.tensor_tensor(h[:, t, c], h[:, t, c], prod_t[:, t, :], ALU.add).then_inc(S("h_done"), 1)
                h_split(m + 1, 1, gname)
                feed(g0 + 6)
                h_factor(m + 1)

            def p_split(layer):
                dve.wait_ge(S("p_hi"), layer + 1)
                dve.tensor_tensor(z_lo[:, KB - 2:KB, :], p_t1 if layer else p_t0, z_hi[:, KB - 2:KB, :].bitcast(F32),
                                  ALU.subtract).then_inc(S("p_split"), 1)

            dve.wait_ge(S("ld_par"), 16)
            dve.wait_ge(S("taps_hi"), 1)
            taps = prm[:, PCOL["dw_w"] + CONV_PE * TAPS:PCOL["dw_w"] + KB * TAPS]
            dve.tensor_tensor(taps_lo.rearrange("p a b -> p (a b)").bitcast(F32R), taps,
                              taps_hi.rearrange("p a b -> p (a b)"), ALU.subtract).then_inc(S("taps_split"), 1)
            dve.wait_ge(S("x_ss"), 2)
            rsqrt(st[:, 80:82], st2[:, 60:62], st2[:, 48:50], st2[:, 62:64], 1.0 / D, EPS, S("x_r"))
            dve.wait_ge(S("x_r"), 1)
            dve.tensor_scalar(x_s[:, 1, :], h[:, 1, :], st2[:, 49:50], None, ALU.mult).then_inc(S("x_scaled_1"), 1)
            for t in range(TT):
                gain_block(("x", 0, t), col("conv_g", 0, 4))
            feed(0)
            for n_ in range(2):
                for t in range(TT):
                    if n_:
                        gain_block(("x", 1, t), col("conv_g", 4, 4))
                for t in range(TT):
                    split_lo(("x", n_, t), x_hi, x_lo, 4 * n_, slice(t * P, (t + 1) * P))
            feed(2)
            dve.wait_ge(S("consts"), 4)

            def gated(f):
                ahead(G["pw1"] + f)
                bank, free = take(dve, ("pw1", f))
                dve.wait_ge(S("sig"), f + 1)
                dve.scalar_tensor_tensor(out=u_pad[:, f, TAPS - 1:], in0=bank[:, 0:SEQ], scalar=col("b_a", f),
                                         in1=sig[:, f % 2, :], op0=ALU.add, op1=ALU.mult).then_inc(S("u"), 1)
                if f >= CONV_PE:
                    dve.wait_ge(S("u_hi"), f - CONV_PE + 1)
                    w = slice((f - CONV_PE) * PADDED, (f - CONV_PE + 1) * PADDED)
                    dve.tensor_tensor(flat(z_lo)[:, w], u_pad[:, f, :], flat(z_hi)[:, w].bitcast(F32),
                                      ALU.subtract).then_inc(S("u_split"), 1)

            def taps_of_pair(f0, side):
                last = {}
                dve.wait_ge(S("u"), f0 + 2)
                for tap in range(TAPS):
                    for f in (f0, f0 + 1):
                        if tap == 0:
                            ins = dve.tensor_scalar(y[:, f, :], u_pad[:, f, 0:SEQ], col("dw_w", f * TAPS),
                                                    col("dw_b", f), ALU.mult, ALU.add)
                        else:
                            dve.wait_ge(dve_step, last[f])
                            ins = dve.scalar_tensor_tensor(out=y[:, f, :], in0=u_pad[:, f, tap:tap + SEQ],
                                                           scalar=col("dw_w", f * TAPS + tap), in1=y[:, f, :],
                                                           op0=ALU.mult, op1=ALU.add)
                        if tap < TAPS - 1:
                            n[0] += 1
                            ins.then_inc(dve_step, 1)
                            last[f] = n[0]
                        else:
                            ins.then_inc(S("conv"), 1)
                    if tap in side:
                        gated(side[tap])

            gated(0)
            p_split(0)
            gated(1)
            taps_of_pair(0, {4: 2, 8: 3, 12: 4, 18: 5})
            taps_of_pair(2, {0: 6, 14: 7})
            dve.wait_ge(S("conv"), CONV_PE)
            link(dve.tensor_tensor(y_sum, y[:, 0, :], y[:, 1, :], ALU.add))
            for f in range(2, CONV_PE):
                ins = dve.tensor_tensor(y_sum, y_sum, y[:, f, :], ALU.add)
                if f < CONV_PE - 1:
                    link(ins)
            ins.then_inc(S("y_summed"), 1)
            ahead(G["proj0"])
            bank, free = take(dve, "mean")
            dve.wait_ge(S("conv_pe"), KB - CONV_PE)
            for i in range(4):
                k = slice(2 * i, 2 * i + 2)
                dve.tensor_tensor(y[:, k, :], y[:, k, :], bank[:, 0:SEQ].unsqueeze(1).to_broadcast([P, 2, SEQ]),
                                  ALU.subtract).then_inc(S("centred"), 1)
            dve.wait_ge(S("centred"), 4)
            bank, free = take(dve, "var")
            rsqrt([bank[:, t * P:(t + 1) * P] for t in range(TT)], *[[wide[:, i, t * P:(t + 1) * P] for t in range(TT)]
                                                                     for i in range(3)], 1.0, EPS, S("y_r"))
            dve.wait_ge(S("y_r"), 1)
            def scaled(i):
                k = slice(2 * i, 2 * i + 2)
                dve.tensor_tensor(y[:, k, :], y[:, k, :], wide[:, 1:2, :].to_broadcast([P, 2, SEQ]), ALU.mult) \
                   .then_inc(S("scaled"), 1)

            def v_split(i):
                k = slice(2 * i, 2 * i + 2)
                dve.wait_ge(S("v_act"), 2 * i + 2)
                dve.wait_ge(S("v_hi"), i + 1)
                dve.tensor_tensor(z_lo[:, k, :], v_f[:, k, :], z_hi[:, k, :].bitcast(F32), ALU.subtract) \
                   .then_inc(S("v_split"), 1)

            scaled(0)
            scaled(1)
            scaled(2)
            v_split(0)
            scaled(3)
            v_split(1)
            v_split(2)
            v_split(3)
            dve.wait_ge(S("h_biased"), 2)
            ahead(G["pw2"] + 1)
            for t in range(TT):
                add_h((("pw2", 0), t), 0, t)
            ahead(G["pw2"] + 2)
            h_split(0, 0, "ffn_g0")
            ahead(G["pw2"] + 3)
            for t in range(TT):
                add_h((("pw2", 1), t), 1, t)
            h_split_factor(0, "ffn_g0")
            ffn(0, 0, "ple_g0")
            bank, free = take(dve, "bias")
            dve.tensor_copy(bias_row[:, 0:SEQ], bank[0:HEADS, 0:SEQ]).then_inc(free, 1)
            freed(dve, "bias")
            dve.tensor_scalar(bias_row[:, 0:1], bias_row[:, 0:1], 1.0, None, ALU.mult).then_inc(S("bias_row"), 1)
            dve.memset(bias_row[:, SEQ:384], NEG).then_inc(S("bias_row"), 1)
            link(dve.tensor_tensor(lam_t[:, 0:4:2, :], lam_t[:, 0:4:2, :], lam_t[:, 1:4:2, :], ALU.mult))
            dve.tensor_reduce(st[:, 88:90], lam_t[:, 0:4:2, :], AX, ALU.add).then_inc(S("lam_sum"), 1)
            dve.tensor_scalar(st[:, 92:93], col("q_g"), HD ** -0.5, None, ALU.mult).then_inc(S("attn_small"), 1)
            dve.tensor_scalar(st[:, 93:94], col("k_g"), 1.0, None, ALU.mult).then_inc(S("attn_small"), 1)
            dve.tensor_scalar(st[:, 95:96], col("sub_g"), 1.0 - LAMBDA_INIT, None, ALU.mult).then_inc(S("attn_small"), 1)
            ple(0, 1, "attn_g")

            ahead(G["qkv"])
            dve.wait_ge(S("lam_exp"), 1)
            link(dve.tensor_tensor(st[:, 94:95], st[:, 91:92], st[:, 90:91], ALU.subtract))
            link(dve.tensor_scalar(st[:, 94:95], st[:, 94:95], -LAMBDA_INIT, None, ALU.add))
            p_split(1)
            g = G["qkv"]

            def qk_norm(hg, i):
                for t in range(TT):
                    dve.wait_ge(S("qk_sq"), 4 * hg + 2 * i + t + 1)
                    c = 16 + 16 * i + 8 * t
                    dve.tensor_reduce(st[:, c:c + 8], sq_t[:, t, :].rearrange("p (g d) -> p g d", d=HD), AX, ALU.add) \
                       .then_inc(S("qk_ss"), 1)
                dve.wait_ge(S("qk_ss"), 4 * hg + 2 * i + 2)
                c = 16 + 16 * i
                rsqrt(st[:, c:c + 16], qk_v, st2[:, c:c + 16], qk_tmp, 1.0 / HD, EPS, S("qk_r"))
                dve.wait_ge(S("qk_r"), 2 * hg + i + 1)
                for t in range(TT):
                    v = qk_t[:, i, t, :].rearrange("p (g d) -> p g d", d=HD)
                    c = 16 + 16 * i + 8 * t
                    dve.tensor_tensor(v, v, st2[:, c:c + 8].unsqueeze(2).to_broadcast([P, 8, HD]), ALU.mult) \
                       .then_inc(S("qk_normed"), 1)

            def masked(hd):
                v, c0 = lg[hd % 2], 64 + 4 * (hd % 2)
                if hd >= 2:
                    dve.wait_ge(S("w_mix"), hd - 1)
                for c in range(2):
                    bank, _ = take(dve, ("lg", hd, c))
                    for lo, w, k0, a in ((c * SEQ, SEQ, 0, 2 + c), (2 * SEQ + c * P, P, SEQ, c)):
                        ins = dve.tensor_tensor_reduce(v[:, lo:lo + w], bank[:, k0:k0 + w], toep_t[:, hd, k0:k0 + w],
                                                       -1.0, 3.0e38, ALU.add, ALU.min, st[:, c0 + a:c0 + a + 1])
                    ins.then_inc(S("lg_read"), 1)

            def mix(hd):
                dve.wait_ge(S("exps"), hd + 1)
                s, v, p = st[:, 72 + 4 * (hd % 2):76 + 4 * (hd % 2)], lg[hd % 2], hd % 2
                link(dve.reciprocal(rec[:, hd, :], s))
                link(dve.scalar_tensor_tensor(out=st2[:, 52 + 2 * p:54 + 2 * p], in0=rec[:, hd, 1:4:2], scalar=st[:, 94:95],
                                              in1=s[:, 0:4:2], op0=ALU.mult, op1=ALU.mult))
                if hd >= 2:
                    take(dve, ("tr", "w", hd - 2))
                dve.scalar_tensor_tensor(out=wt[:, p, 0:SEQ], in0=v[:, SEQ:2 * SEQ], scalar=st2[:, 53 + 2 * p:54 + 2 * p],
                                         in1=v[:, 0:SEQ], op0=ALU.mult, op1=ALU.add)
                dve.scalar_tensor_tensor(out=wt[:, p, SEQ:384], in0=v[:, 2 * SEQ + P:768],
                                         scalar=st2[:, 52 + 2 * p:53 + 2 * p], in1=v[:, 2 * SEQ:2 * SEQ + P],
                                         op0=ALU.mult, op1=ALU.add).then_inc(S("w_mix"), 1)

            def o_evac(pair):
                bank, free = take(dve, ("pv", pair))
                dve.tensor_tensor(oo[:, :, 2 * pair * P:(2 * pair + 2) * P].rearrange("p t (h d) -> p t h d", h=2),
                                  bank[:, :].rearrange("p (t h d) -> p t h d", t=TT, h=2),
                                  rec[:, 2 * pair:2 * pair + 2, 0:4:2].rearrange("p h t -> p t h").unsqueeze(3)
                                  .to_broadcast([P, TT, 2, P]), ALU.mult).then_inc(free, 1)

            def o_norm(n_):
                dve.wait_ge(S("o_ss"), 8 * n_ + 8)
                c = slice(48 + 8 * n_, 56 + 8 * n_)
                rsqrt(st[:, c], qk_v[:, 0:8], st2[:, 16 + 8 * n_:24 + 8 * n_], qk_tmp[:, 0:8], 1.0 / P, EPS, S("o_r"))
                dve.wait_ge(S("o_r"), n_ + 1)
                for t in range(TT):
                    v = oo[:, t, n_ * 512:(n_ + 1) * 512].rearrange("p (g d) -> p g d", d=P)
                    f = st2[:, 16 + 8 * n_ + 4 * t:20 + 8 * n_ + 4 * t]
                    dve.tensor_tensor(v, v, f.unsqueeze(2).to_broadcast([P, 4, P]), ALU.mult).then_inc(S("o_normed"), 1)

            def o_split(n_):
                for t in range(TT):
                    bank, free = take(dve, ("tr", "o", n_, t))
                    hi_count[0] += 1
                    dve.wait_ge(S("t_hi"), hi_count[0])
                    k, c = slice(4 * n_, 4 * n_ + 4), slice(t * P, (t + 1) * P)
                    dve.scalar_tensor_tensor(out=z_lo[:, k, c], in0=bank[:, :].rearrange("p (k c) -> p k c", k=4),
                                             scalar=st[:, 95:96], in1=z_hi[:, k, c].bitcast(F32), op0=ALU.mult,
                                             op1=ALU.subtract).then_inc(free, 1)

            feed(g + 4)
            qk_norm(0, 0)
            feed(g + 6)
            qk_norm(0, 1)
            feed(g + 7)
            dve.wait_ge(S("ld_toep"), 32)
            masked(0)
            masked(1)
            feed(g + 8)
            mix(0)
            masked(2)
            qk_norm(1, 0)
            mix(1)
            feed(g + 9)
            masked(3)
            mix(2)
            feed(g + 10)
            qk_norm(1, 1)
            feed(g + 11)
            mix(3)
            masked(4)
            masked(5)
            mix(4)
            masked(6)
            mix(5)
            masked(7)
            mix(6)
            o_evac(0)
            mix(7)
            o_evac(1)
            feed(g + 12)
            o_evac(2)
            o_norm(0)
            o_evac(3)
            feed(g + 13)
            o_split(0)
            o_norm(1)
            ahead(G["proj1"])
            o_split(1)
            ahead(G["wo"] + 1)
            for t in range(TT):
                add_h((("wo", 0), t), 0, t)
            ahead(G["wo"] + 2)
            h_split(3, 0, "ffn_g1")
            ahead(G["wo"] + 3)
            for t in range(TT):
                add_h((("wo", 1), t), 1, t)
            h_split_factor(3, "ffn_g1")
            ffn(1, 3, "ple_g1")
            ple(1, 4, "norm_g2")

            ahead(G["av"] + 3)
            for n_ in range(2):
                for t in range(TT):
                    freed(dve, (("av", n_), t))
            link(dve.tensor_tensor(st[:, 20:22], st[:, 16:20:2], st[:, 17:20:2], ALU.add))
            dve.tensor_scalar(st[:, 20:22], st[:, 20:22], -1.0 / D, None, ALU.mult).then_inc(S("v_mean"), 1)
            dve.wait_ge(S("v_mean"), 1)
            ahead(G["au"])
            dve.wait_ge(S("v_var"), 2)
            rsqrt(st[:, 22:24], st2[:, 60:62], st2[:, 22:24], st2[:, 62:64], 1.0 / D, LN_EPS_2, S("v_r"))
            dve.wait_ge(S("v_r"), 1)
            dve.wait_ge(S("ld_sgu"), 32)
            for t in range(TT):
                link(dve.tensor_scalar(av[:, t, :], av[:, t, :], st[:, 20 + t:21 + t], st2[:, 22 + t:23 + t],
                                       ALU.add, ALU.mult))
                link(dve.tensor_tensor(av[:, t, :], av[:, t, :], ln_row[:, 0, :], ALU.mult))
                dve.tensor_tensor(av[:, t, :], av[:, t, :], ln_row[:, 1, :], ALU.add).then_inc(S("sgu_ready"), 1)
                if t:
                    ahead(G["au"] + 1)
            for t in range(TT):
                dve.tensor_scalar(diag[:, t, :], ident[:, :], st2[:, 10 + t:11 + t], None, ALU.mult).then_inc(S("diag"), 1)
            ahead(G["au"] + 3)
            bank, free = take(dve, "r_row")
            dve.tensor_copy(rb, bank[:, 0:SEQ]).then_inc(free, 1)
            freed(dve, "r_row")
            link(dve.tensor_tensor(rb2, rb, rb, ALU.mult))
            ahead(G["az"] + 1)
            for n_ in range(2):
                for t in range(TT):
                    bank, free = take(dve, ("mixed", t, n_))
                    freed(dve, (("au", n_), t))
                    for j in range(4):
                        gi = 4 * n_ + j
                        c = slice(gi * P, (gi + 1) * P)
                        ins = dve.scalar_tensor_tensor(out=au[:, t, c], in0=bank[:, j * P:(j + 1) * P],
                                                       scalar=col("sgu_b", gi), in1=au[:, t, c], op0=ALU.add, op1=ALU.mult)
                    ins.then_inc(free, 1)
                if n_:
                    ahead(G["az"] + 3)
                for t in range(TT):
                    freed(dve, ("mixed", t, n_))
                    freed(dve, (("az", n_), t))
                    c = slice(n_ * 512, (n_ + 1) * 512)
                    dve.tensor_tensor(au[:, t, c], au[:, t, c], az[:, t, c], ALU.mult).then_inc(S("ya"), 1)
            for n_ in range(2):
                ahead(G["ga"] + 2 + n_)
                for t in range(TT):
                    plain_lo(("ya", n_, t), z_hi, z_lo, 4 * n_, slice(t * P, (t + 1) * P))
            for n_ in range(2):
                ahead(G["wa"] + 2 * n_ + 1)
                for t in range(TT):
                    c = slice(n_ * 512, (n_ + 1) * 512)
                    bank, free = take(dve, (("wa", n_), t))
                    freed(dve, (("ga", n_), t))
                    dve.tensor_tensor(merged[:, t, c], bank[:, :], gate[:, t, c], ALU.mult).then_inc(free, 1)

            ahead(G["bp"] + 3)
            ahead(G["bz"] + 1)
            for w in range(4):
                bank, free = take(dve, ("pool", w))
                hi_count[0] += 1
                dve.wait_ge(S("t_hi"), hi_count[0])
                dve.tensor_tensor(z_lo[:, 2 * w:2 * w + 2, :], bank[:, :].rearrange("p (k s) -> p k s", k=2),
                                  z_hi[:, 2 * w:2 * w + 2, :].bitcast(F32), ALU.subtract).then_inc(free, 1)
            ahead(G["bz"] + 3)
            ahead(G["poolw"])
            dve.wait_ge(S("ld_pool"), 16)
            for n_ in range(2):
                c = slice(n_ * 512, (n_ + 1) * 512)
                for t in range(TT):
                    bank, free = take(dve, ("pooled", n_, t))
                    dve.tensor_tensor(au[:, t, c], bank[:, :], pool_row[:, 0, c], ALU.add).then_inc(free, 1)
            for n_ in range(2):
                c = slice(n_ * 512, (n_ + 1) * 512)
                for t in range(TT):
                    freed(dve, ("pooled", n_, t))
                    dve.tensor_tensor(au[:, t, c], au[:, t, c], pool_row[:, 1, c], ALU.mult).then_inc(S("pool_scaled"), 1)
                for t in range(TT):
                    freed(dve, (("bz", n_), t))
                    dve.wait_ge(S("pool_scaled"), 2 * n_ + t + 1)
                    dve.tensor_tensor(au[:, t, c], au[:, t, c], az[:, t, c], ALU.mult).then_inc(S("yb"), 1)
            for n_ in range(2):
                ahead(G["gb"] + 2 + n_)
                for t in range(TT):
                    plain_lo(("yb", n_, t), z_hi, z_lo, 4 * n_, slice(t * P, (t + 1) * P))

            def merge(name, gate_name, done):
                for n_ in range(2):
                    ahead(G[name] + 2 * n_ + 1)
                    c = slice(n_ * 512, (n_ + 1) * 512)
                    for t in range(TT):
                        bank, free = take(dve, ((name, n_), t))
                        freed(dve, ((gate_name, n_), t))
                        dve.tensor_tensor(tmp[:, t, :], bank[:, :], gate[:, t, c], ALU.mult).then_inc(free, 1)
                        freed(dve, ((name, n_), t))
                        dve.tensor_tensor(merged[:, t, c], merged[:, t, c], tmp[:, t, :], ALU.add).then_inc(S(done), 1)
                    if name == "wc":
                        if n_ == 0:
                            ahead(G[name] + 2)
                        for t in range(TT):
                            plain_lo(("merged", n_, t), x_hi, x_lo, 4 * n_, slice(t * P, (t + 1) * P))

            merge("wb", "gb", "merged_b")

            dve.wait_ge(S("merged_b"), 4)
            dve.memset(c_pad[:, :, 0:2], 0.0).then_inc(S("c_zero"), 1)
            for j in range(KB):
                g = G["cc"] + 2 * j
                s = j % 2
                ahead(g)
                bank, free = take(dve, ("cc", j, 0))
                dve.wait_ge(S("c_hc"), j + 1)
                dve.tensor_tensor(c_y[:, s, :], bank[:, SEQ:2 * SEQ], c_h[:, s, :], ALU.mult).then_inc(free, 1)
                freed(dve, ("cc", j, 0))
                link(dve.tensor_tensor(c_pad[:, s, 2:], c_y[:, s, :], rb2, ALU.mult))
                link(dve.tensor_scalar(c_y[:, s, :], c_pad[:, s, 0:SEQ], col("c3_w", 3 * j), col("c3_b", j),
                                       ALU.mult, ALU.add))
                for k in (1, 2):
                    link(dve.scalar_tensor_tensor(out=c_y[:, s, :], in0=c_pad[:, s, k:k + SEQ],
                                                  scalar=col("c3_w", 3 * j + k), in1=c_y[:, s, :],
                                                  op0=ALU.mult, op1=ALU.add))
                ahead(g + 1)
                bank, _ = take(dve, ("cc", j, 1))
                dve.tensor_tensor(c_b[:, s, :], bank[:, 0:SEQ], rb, ALU.mult)
                dve.tensor_tensor(c_z[:, s, :], bank[:, SEQ:2 * SEQ], rb, ALU.mult).then_inc(S("c_zr"), 1)
                dve.wait_ge(S("c_zr"), j + 1)
                link(dve.tensor_tensor(c_y[:, s, :], c_y[:, s, :], c_b[:, s, :], ALU.mult))
                dve.wait_ge(S("c_silu"), j + 1)
                dve.tensor_tensor(c_f[:, s, :], c_y[:, s, :], c_s[:, s, :], ALU.mult).then_inc(S("yc"), 1)
                dve.wait_ge(S("yc_hi"), j + 1)
                dve.tensor_tensor(z_lo[:, j, :], c_f[:, s, :], z_hi[:, j, :].bitcast(F32), ALU.subtract) \
                   .then_inc(S("yc_split"), 1)
            ahead(G["gc"] + 3)
            merge("wc", "gc", "merged")

            dve.wait_ge(S("ld_final"), 16)

            def out_part(n_, t):
                add_h((("wout", n_), t), n_, t)
                c = slice(n_ * 512, (n_ + 1) * 512)
                dve.wait_ge(S("h_done"), 24 + 2 * n_ + t + 1)
                dve.tensor_tensor(av[:, t, c], h[:, t, c], final_row[:, c], ALU.mult).then_inc(S("out_gain"), 1)

            def out_factor(t, fill={}):
                dve.wait_ge(S("h_ss"), 27 + t)
                link(dve.tensor_tensor(st[:, 8 + t:9 + t], st[:, t:t + 1], st[:, 2 + t:3 + t], ALU.add))
                rsqrt(st[:, 8 + t:9 + t], st2[:, 58 + t:59 + t], st2[:, 12 + t:13 + t], st2[:, 62 + t:63 + t], 1.0 / D, EPS,
                      S("out_r"), fill)

            ahead(G["wout"] + 1)
            for t in range(TT):
                out_part(0, t)
            ahead(G["wout"] + 3)
            out_part(1, 0)
            out_factor(0, fill={6: lambda: out_part(1, 1)})
            out_factor(1)
            dve.wait_ge(S("out_r"), 2)
            dve.wait_ge(S("out_gain"), 4)
            dve.tensor_scalar(av[:, 1, :], av[:, 1, :], st2[:, 13:14], None, ALU.mult).then_inc(S("out_ready_1"), 1)


def bucket(dist):
    n = np.maximum(dist, 0)
    f = np.maximum(n, 1).astype(np.float32)
    large = 16 + (np.log(f / np.float32(16)) / np.float32(math.log(128 / 16)) * np.float32(16)).astype(np.int32)
    return np.where(n < 16, n, np.minimum(large, NBUCKET - 1))


def constants():
    onehot = np.zeros((NBUCKET, 384), np.float32)
    dist = np.arange(SEQ - 1, -1, -1)
    onehot[bucket(dist), np.arange(SEQ)] = 1.0
    pool = np.zeros((4, SEQ, SEQ), np.float32)
    for w, win in enumerate(WINDOWS):
        for s in range(SEQ):
            lo = max(0, s - win + 1)
            pool[w, lo:s + 1, s] = np.float32(1.0) / np.float32(s + 1 - lo)
            pool[w, s, s] -= 1.0
    pm = np.zeros((P, 4, 384), np.float32)
    for w in range(4):
        pm[:, w, 0:SEQ] = pool[w, 0:P, :]
        pm[:, w, SEQ:384] = pool[w, P:, P:]
    return onehot, pm


def kernel(**inputs):
    import concourse.bacc as bacc
    from concourse.bass_utils import run_bass_kernel_spmd

    a = {k: np.asarray(v) for k, v in inputs.items()}
    ws = np.empty((NPIECE, P, HALF), np.float32)

    def rows_cols(w, k0, nk, *cols):
        b = w[k0 * P:(k0 + nk) * P].reshape(nk, P, -1)
        parts = [b[:, :, c] for c in cols]
        return np.concatenate(parts, axis=2).transpose(1, 0, 2).reshape(P, -1)

    def chunks(name, w):
        for i in range(w.shape[1] // 512):
            for k in range(2):
                ws[G[name] + 2 * i + k] = rows_cols(w, 4 * k, 4, slice(i * 512, (i + 1) * 512))

    pw1 = a["conv_w_pw1"][0]
    for f in range(KB):
        ws[G["pw1"] + f] = rows_cols(pw1, 0, KB, slice(f * P, (f + 1) * P), slice(D + f * P, D + (f + 1) * P))
    chunks("pw2", a["conv_w_pw2"][0])
    for l in range(2):
        ws[G[f"proj{l}"]] = rows_cols(a["ple_w_proj"][l], 0, 2, slice(0, D))
        chunks(f"ple{l}", a["ple_w_gate"][l])
        g0 = G[f"ffn{l}"]
        both = np.stack([a["ffn_w_gate"][l].reshape(D, GU, 256), a["ffn_w_up"][l].reshape(D, GU, 256)], 2)             .reshape(D, GU * 512)
        for i in range(GU):
            for k in range(2):
                ws[g0 + gu_at(i) + k] = rows_cols(both, 4 * k, 4, slice(i * 512, (i + 1) * 512))
            at = down_at(i // 2) + i % 2 if i < 10 else 32
            ws[g0 + at] = rows_cols(a["ffn_w_down"][l], 2 * i, 2, slice(0, D))
    qkv = a["attn_w_qkv"][0]
    order = [m * D + hg * 512 for m, hg in ((0, 0), (1, 0), (0, 1), (1, 1), (2, 0), (2, 1))]
    for i, c in enumerate(order):
        for k in range(2):
            ws[G["qkv"] + 2 * i + k] = rows_cols(qkv, 4 * k, 4, slice(c, c + 512))
    chunks("wo", a["attn_w_o"][0])
    w_in = a["w_in_2"][0]
    for name, i in [("au", 0), ("av", 1), ("az", 2), ("bp", 3), ("bz", 4), ("ga", 9), ("gb", 10), ("gc", 11)]:
        chunks(name, w_in[:, i * D:(i + 1) * D])
    for j in range(KB):
        for k, (one, two) in enumerate([(5, 7), (6, 8)]):
            ws[G["cc"] + 2 * j + k] = rows_cols(w_in, 0, KB, slice(one * D + j * P, one * D + (j + 1) * P),
                                                slice(two * D + j * P, two * D + (j + 1) * P))
    ws[G["poolw"]] = a["pool_w_2"][0].reshape(4, 2, P, 256).transpose(2, 0, 1, 3).reshape(P, HALF)
    chunks("wa", a["w_branch_a_2"][0])
    chunks("wb", a["w_branch_b_2"][0])
    chunks("wc", a["w_branch_c_2"][0])
    chunks("wout", a["w_out_2"][0])

    par = np.zeros((P, PCOLS), np.float32)

    def features(name, v):
        v = v.reshape(-1, P).T
        par[:, PCOL[name]:PCOL[name] + v.shape[1]] = v

    features("conv_g", a["conv_norm_g"][0])
    features("b_a", a["conv_b_pw1"][0, :D])
    features("b_g", a["conv_b_pw1"][0, D:])
    features("dw_b", a["conv_dw_b"][0])
    features("ln_g", a["conv_ln_g"][0])
    features("ln_b", a["conv_ln_b"][0])
    for l in range(2):
        features(f"ffn_g{l}", a["ffn_norm_g"][l])
        features(f"ple_g{l}", a["ple_norm_g"][l])
    features("attn_g", a["attn_norm_g"][0])
    features("norm_g2", a["norm_g_2"][0])
    features("c3_b", a["conv_b_2"][0])
    features("q_g", np.tile(a["attn_q_norm_g"][0], 2))
    features("k_g", np.tile(a["attn_k_norm_g"][0], 2))
    features("sub_g", a["attn_sub_norm_g"][0])
    features("sgu_b", a["sgu_b_2"][0])
    par[:, PCOL["dw_w"]:PCOL["dw_w"] + KB * TAPS] =         a["conv_dw_w"][0].reshape(TAPS, KB, P).transpose(2, 1, 0).reshape(P, KB * TAPS)
    par[:, PCOL["c3_w"]:PCOL["c3_w"] + 24] = a["conv_w_2"][0].reshape(3, KB, P).transpose(2, 1, 0).reshape(P, 24)

    onehot, pool_m = constants()
    x = a["x"][0]
    arrays = {
        "ws": ws, "x_tok": x,
        "p_feat": a["p"][:, 0].transpose(0, 2, 1).reshape(2, 2, P, SEQ).transpose(0, 2, 1, 3),
        "par": par,
        "rows": np.concatenate([a["conv_b_pw2"], a["sgu_ln_g_2"], a["sgu_ln_b_2"], a["pool_b_2"], a["pool_scale_2"],
                                a["final_g_2"][None]]),
        "lam_rows": np.concatenate([a["attn_lambda_q1"], a["attn_lambda_k1"], a["attn_lambda_q2"],
                                    a["attn_lambda_k2"]]),
        "rel": a["rel_bias"], "onehot": onehot, "sgu_w": a["sgu_w_2"][0].transpose(2, 0, 1), "pool_m": pool_m,
    }
    arrays = {f"in_{k}": np.ascontiguousarray(v) for k, v in arrays.items()}
    nc = bacc.Bacc("TRN2", target_bir_lowering=False, num_devices=1)
    args = [nc.dram_tensor(k, v.shape, F32, kind="ExternalInput").ap() for k, v in arrays.items()]
    toep = nc.dram_tensor("toep", (HEADS, P, 384), F32).ap()
    out = nc.dram_tensor("out_0", (SEQ, D), F32, kind="ExternalOutput").ap()
    build(nc, *args, toep, out)
    r = run_bass_kernel_spmd(nc, [arrays], core_ids=[0])
    return r.results[0]["out_0"].reshape(1, SEQ, D)
```
